# Optimizing a Trainium2 kernel written in Bass

```python
import math
import jax
import jax.numpy as jnp
from jax import lax
import numpy as np

D_MODEL = 1024
BATCH = 1
SEQ = 2048
DEPTH = 1
DEC_BATCH = 8
DEC_SEQ = 8
PAST_LEN = 4096
PAGE_SIZE = 128

D_MIX = D_MODEL
HD_R = 64
C_R = D_MIX // 4
H_R = C_R // HD_R
R_DECAY = 32
R_AAA = 32
R_GATE = 64
RWKV_LN_EPS = 64e-5
C_CONV = D_MIX // 4
CONV_W = 31
CONV_LN_EPS = 1e-5
HD_A = 64
C_A = D_MIX - C_R - C_CONV
H_A = C_A // HD_A
N_KV = 2
G_A = H_A // N_KV
H_I = H_A // 2
D_IDX = 64
TOPK_MAX = 256
Q_BLOCK = 128
N_BUCKETS = 32
MAX_DISTANCE = 128
D_FF = 2816
FFN_CONV_W = 3
D_PLE = 256
NORM_EPS = 1e-6
RWKV_SPLITS = (C_R, C_R, C_R, R_DECAY, R_AAA, R_GATE)
ATT_SPLITS = (C_A, N_KV * HD_A, N_KV * HD_A, H_I * D_IDX, D_IDX, H_I)
N_RWKV_COLS = 3 * C_R + R_DECAY + R_AAA + R_GATE
N_CONV_COLS = 2 * C_CONV
N_ATT_COLS = C_A + 2 * N_KV * HD_A + H_I * D_IDX + D_IDX + H_I
N_IN = N_RWKV_COLS + N_CONV_COLS + N_ATT_COLS
N_KEYS = 48

kernel_name = 'hybrid_rwkv7_conformer_dsa_step'

def split_cols(x, sizes):
    parts, start = [], 0
    for s in sizes:
        parts.append(x[..., start:start + s])
        start += s
    return parts

def rmsnorm(x, g):
    xf = x.astype(jnp.float32)
    y = xf * lax.rsqrt(jnp.mean(xf * xf, axis=-1, keepdims=True) + NORM_EPS)
    return (y * g.astype(jnp.float32)).astype(x.dtype)

def layernorm(x, g, b, eps):
    xf = x.astype(jnp.float32)
    mu = jnp.mean(xf, axis=-1, keepdims=True)
    var = jnp.mean(jnp.square(xf - mu), axis=-1, keepdims=True)
    return ((xf - mu) * lax.rsqrt(var + eps) * g + b).astype(x.dtype)

def causal_dwconv(x_pad, w, b):
    y = lax.conv_general_dilated(x_pad, w[:, None, :].astype(x_pad.dtype), window_strides=(1,), padding='VALID',
                                 dimension_numbers=('NWC', 'WIO', 'NWC'), feature_group_count=x_pad.shape[-1])
    return y + b

def _wkv7_step(S, inp):
    rt, wt, kt, vt, at, bt = inp
    sa = jnp.einsum('bhvk,bhk->bhv', S, at)
    S = S * wt[:, :, None, :] + sa[..., None] * bt[:, :, None, :] + vt[..., None] * kt[:, :, None, :]
    return S, jnp.einsum('bhvk,bhk->bhv', S, rt)

def rwkv7_mix(z_rw, shift0, wkv0, W, i):
    B, T, _ = z_rw.shape
    dt = z_rw.dtype
    z_prev = jnp.concatenate([shift0.astype(dt)[:, None], z_rw[:, :-1]], axis=1)
    zs = z_rw + (z_prev - z_rw) * W['mu_shift'][i]
    r, k, v, xw, xa, xg = split_cols(zs, RWKV_SPLITS)
    w_log = -jax.nn.softplus(-(W['w0'][i] + jnp.tanh(xw) @ W['w_lora'][i]).astype(jnp.float32)) - 0.5
    decay = jnp.exp(-jnp.exp(w_log)).astype(dt)
    a = jax.nn.sigmoid(W['a0'][i] + xa @ W['a_lora'][i])
    g = jax.nn.sigmoid(xg) @ W['g_lora'][i]
    heads = lambda t: t.reshape(B, T, H_R, HD_R)
    kk = heads(k * W['k_k'][i]).astype(jnp.float32)
    kk = (kk / jnp.maximum(jnp.sqrt(jnp.sum(kk * kk, axis=-1, keepdims=True)), 1e-12)).astype(dt)
    k = k * (1.0 + (a - 1.0) * W['k_a'][i])
    r4, k4, v4, a4 = heads(r), heads(k), heads(v), heads(a)
    seq = tuple(jnp.swapaxes(t, 0, 1) for t in (r4, heads(decay), k4, v4, -kk, kk * a4))
    S_T, y = lax.scan(_wkv7_step, wkv0.astype(dt), seq)
    yf = jnp.swapaxes(y, 0, 1).astype(jnp.float32)
    mu = jnp.mean(yf, axis=-1, keepdims=True)
    var = jnp.mean(jnp.square(yf - mu), axis=-1, keepdims=True)
    yn = ((yf - mu) * lax.rsqrt(var + RWKV_LN_EPS)).reshape(B, T, C_R) * W['lnx_g'][i] + W['lnx_b'][i]
    bonus = (jnp.sum(r4 * k4 * W['r_k'][i], axis=-1, keepdims=True) * v4).reshape(B, T, C_R)
    out = ((yn + bonus) * g).astype(dt)
    return out, S_T, z_rw[:, -1]

def conformer_conv_mix(z_glu, conv0, W, i):
    dt = z_glu.dtype
    u = z_glu[..., :C_CONV] * jax.nn.sigmoid(z_glu[..., C_CONV:])
    u_pad = jnp.concatenate([conv0.astype(dt), u], axis=1)
    c = causal_dwconv(u_pad, W['conv_w'][i], W['conv_b'][i])
    c = layernorm(c, W['conv_ln_g'][i], W['conv_ln_b'][i], CONV_LN_EPS)
    return jax.nn.silu(c), u_pad[:, -(CONV_W - 1):]

def rel_bucket(dist):
    max_exact = N_BUCKETS // 2
    d_f = jnp.maximum(dist, max_exact).astype(jnp.float32)
    large = max_exact + (jnp.log(d_f / max_exact) / math.log(MAX_DISTANCE / max_exact)
                         * (N_BUCKETS - max_exact)).astype(jnp.int32)
    return jnp.where(dist < max_exact, dist, jnp.minimum(large, N_BUCKETS - 1))

def dsa_block(q, qi, wi, q_pos, k_all, v_all, ki_all, rel_bias, top_k):
    B, Tq = q.shape[:2]
    L = k_all.shape[1]
    dots = jnp.einsum('bthd,bsd->bths', qi, ki_all, preferred_element_type=jnp.float32) * (D_IDX ** -0.5)
    score = jnp.einsum('bths,bth->bts', jax.nn.relu(dots), wi.astype(jnp.float32) * (H_I ** -0.5))
    key_pos = jnp.arange(L, dtype=jnp.int32)
    score = jnp.where(key_pos[None, None, :] <= q_pos[None, :, None], score, -jnp.inf)
    _, sel = lax.top_k(score, top_k)
    valid = sel <= q_pos[None, :, None]
    k_sel = jax.vmap(lambda kb, ib: kb[ib])(k_all, sel)
    v_sel = jax.vmap(lambda vb, ib: vb[ib])(v_all, sel)
    dist = jnp.maximum(q_pos[None, :, None] - sel, 0)
    bias = rel_bias[rel_bucket(dist)].astype(jnp.float32)
    bias = bias.reshape(B, Tq, top_k, N_KV, G_A).transpose(0, 1, 3, 4, 2)
    qg = q.reshape(B, Tq, N_KV, G_A, HD_A)
    logits = jnp.einsum('btngd,btknd->btngk', qg, k_sel, preferred_element_type=jnp.float32) * (HD_A ** -0.5) + bias
    logits = jnp.where(valid[:, :, None, None, :], logits, -jnp.inf)
    p = jax.nn.softmax(logits, axis=-1).astype(v_sel.dtype)
    o = jnp.einsum('btngk,btknd->btngd', p, v_sel)
    return o.reshape(B, Tq, C_A)

def dsa_attend(q, qi, wi, q_pos, k_all, v_all, ki_all, rel_bias, top_k):
    B, T = q.shape[:2]
    if T > Q_BLOCK and T % Q_BLOCK == 0:
        nb = T // Q_BLOCK
        blk = lambda t: jnp.swapaxes(t.reshape((B, nb, Q_BLOCK) + t.shape[2:]), 0, 1)
        xs = (blk(q), blk(qi), blk(wi), q_pos.reshape(nb, Q_BLOCK))
        out = lax.map(lambda a: dsa_block(a[0], a[1], a[2], a[3], k_all, v_all, ki_all, rel_bias, top_k), xs)
        return jnp.swapaxes(out, 0, 1).reshape(B, T, C_A)
    return dsa_block(q, qi, wi, q_pos, k_all, v_all, ki_all, rel_bias, top_k)

def dsa_mix(z_att, q_pos, past, W, i, top_k):
    B, T, _ = z_att.shape
    q, k, v, qi, ki, wi = split_cols(z_att, ATT_SPLITS)
    q = rmsnorm(q.reshape(B, T, H_A, HD_A), W['q_norm'][i])
    k = rmsnorm(k.reshape(B, T, N_KV, HD_A), W['k_norm'][i])
    v = v.reshape(B, T, N_KV, HD_A)
    ki = rmsnorm(ki, W['kidx_norm'][i])
    qi = qi.reshape(B, T, H_I, D_IDX)
    k_past, v_past, ki_past = past
    k_all = jnp.concatenate([k_past.astype(k.dtype), k], axis=1)
    v_all = jnp.concatenate([v_past.astype(v.dtype), v], axis=1)
    ki_all = jnp.concatenate([ki_past.astype(ki.dtype), ki], axis=1)
    o = dsa_attend(q, qi, wi, q_pos, k_all, v_all, ki_all, W['rel_bias'], top_k)
    return o, k, v, ki

def conv_ffn(h, ffn0, W, i):
    u = h @ W['ffn_up'][i]
    gate_pre, val = u[..., :D_FF], u[..., D_FF:]
    pad = jnp.concatenate([ffn0.astype(u.dtype), gate_pre], axis=1)
    gate = causal_dwconv(pad, W['ffn_conv_w'][i], W['ffn_conv_b'][i])
    out = (jax.nn.gelu(gate, approximate=False) * val) @ W['ffn_down'][i]
    return out, pad[:, -(FFN_CONV_W - 1):]

def decoder_layer(i, x, p_i, q_pos, st, past, W, top_k):
    shift0, wkv0, conv0, ffn0 = st
    h = rmsnorm(x, W['norm_mix'][i])
    z = h @ W['w_in'][i]
    o_rw, wkv_T, shift_T = rwkv7_mix(z[..., :N_RWKV_COLS], shift0, wkv0, W, i)
    o_cv, conv_T = conformer_conv_mix(z[..., N_RWKV_COLS:N_RWKV_COLS + N_CONV_COLS], conv0, W, i)
    o_at, k, v, ki = dsa_mix(z[..., N_RWKV_COLS + N_CONV_COLS:], q_pos, past, W, i, top_k)
    x = x + jnp.concatenate([o_rw, o_cv.astype(o_rw.dtype), o_at.astype(o_rw.dtype)], axis=-1) @ W['w_out'][i]
    f, ffn_T = conv_ffn(rmsnorm(x, W['norm_ffn'][i]), ffn0, W, i)
    x = x + f
    gate = jax.nn.sigmoid(rmsnorm(x, W['ple_norm'][i]) @ W['ple_gate'][i])
    x = x + (p_i @ W['ple_proj'][i]) * gate
    return x, (k, v, ki, wkv_T, shift_T, conv_T, ffn_T)

def stack_layers(new_list):
    return tuple(jnp.stack(t) for t in zip(*new_list))

def setup_inputs(seed: int = 0) -> dict:
    key = jax.random.key(seed)
    ks = iter([jax.random.fold_in(key, j) for j in range(N_KEYS)])

    def nrm(shape, scale):
        return jax.random.normal(next(ks), shape, jnp.float32) * scale

    def unif(shape, lo, hi):
        return jax.random.uniform(next(ks), shape, jnp.float32, lo, hi)

    n_pages = PAST_LEN // PAGE_SIZE
    n_pool = (DEC_BATCH * n_pages * 5) // 4
    perm = jax.random.permutation(next(ks), n_pool)
    page_table = perm[:DEC_BATCH * n_pages].reshape(DEC_BATCH, n_pages).astype(jnp.int32)
    return dict(
        x_prompt=nrm((BATCH, SEQ, D_MODEL), 1.0),
        x_sample=nrm((DEC_BATCH, DEC_SEQ, D_MODEL), 1.0),
        cache_k=nrm((DEPTH, n_pool, PAGE_SIZE, N_KV, HD_A), 1.0),
        cache_v=nrm((DEPTH, n_pool, PAGE_SIZE, N_KV, HD_A), 1.0),
        cache_kidx=nrm((DEPTH, n_pool, PAGE_SIZE, D_IDX), 1.0),
        state_wkv=nrm((DEPTH, DEC_BATCH, H_R, HD_R, HD_R), 1.0),
        state_shift=nrm((DEPTH, DEC_BATCH, N_RWKV_COLS), 1.0),
        state_conv=nrm((DEPTH, DEC_BATCH, CONV_W - 1, C_CONV), 0.5),
        state_ffn=nrm((DEPTH, DEC_BATCH, FFN_CONV_W - 1, D_FF), 1.0),
        page_table=page_table,
        p_prompt=nrm((DEPTH, BATCH, SEQ, D_PLE), 1.0),
        p_sample=nrm((DEPTH, DEC_BATCH, DEC_SEQ, D_PLE), 1.0),
        norm_mix=1.0 + nrm((DEPTH, D_MODEL), 0.05),
        w_in=nrm((DEPTH, D_MODEL, N_IN), D_MODEL ** -0.5),
        w_out=nrm((DEPTH, D_MIX, D_MODEL), D_MIX ** -0.5),
        mu_shift=unif((DEPTH, N_RWKV_COLS), 0.0, 1.0),
        w0=unif((DEPTH, C_R), -6.0, 1.0),
        w_lora=nrm((DEPTH, R_DECAY, C_R), 0.1),
        a0=nrm((DEPTH, C_R), 0.5),
        a_lora=nrm((DEPTH, R_AAA, C_R), R_AAA ** -0.5),
        g_lora=nrm((DEPTH, R_GATE, C_R), R_GATE ** -0.5),
        k_k=0.85 + nrm((DEPTH, C_R), 0.05),
        k_a=1.0 + nrm((DEPTH, C_R), 0.05),
        r_k=nrm((DEPTH, H_R, HD_R), 0.1),
        lnx_g=1.0 + nrm((DEPTH, C_R), 0.05),
        lnx_b=nrm((DEPTH, C_R), 0.02),
        conv_w=nrm((DEPTH, CONV_W, C_CONV), CONV_W ** -0.5),
        conv_b=nrm((DEPTH, C_CONV), 0.02),
        conv_ln_g=1.0 + nrm((DEPTH, C_CONV), 0.05),
        conv_ln_b=nrm((DEPTH, C_CONV), 0.02),
        q_norm=1.0 + nrm((DEPTH, HD_A), 0.05),
        k_norm=1.0 + nrm((DEPTH, HD_A), 0.05),
        kidx_norm=1.0 + nrm((DEPTH, D_IDX), 0.05),
        rel_bias=nrm((N_BUCKETS, H_A), 0.5),
        norm_ffn=1.0 + nrm((DEPTH, D_MODEL), 0.05),
        ffn_up=nrm((DEPTH, D_MODEL, 2 * D_FF), D_MODEL ** -0.5),
        ffn_conv_w=nrm((DEPTH, FFN_CONV_W, D_FF), FFN_CONV_W ** -0.5),
        ffn_conv_b=nrm((DEPTH, D_FF), 0.02),
        ffn_down=nrm((DEPTH, D_FF, D_MODEL), D_FF ** -0.5),
        ple_norm=1.0 + nrm((DEPTH, D_MODEL), 0.05),
        ple_proj=nrm((DEPTH, D_PLE, D_MODEL), D_PLE ** -0.5),
        ple_gate=nrm((DEPTH, D_MODEL, D_MODEL), D_MODEL ** -0.5),
    )

def reference(x_prompt, x_sample, cache_k, cache_v, cache_kidx, state_wkv, state_shift, state_conv, state_ffn,
              page_table, p_prompt, p_sample, norm_mix, w_in, w_out, mu_shift, w0, w_lora, a0, a_lora, g_lora,
              k_k, k_a, r_k, lnx_g, lnx_b, conv_w, conv_b, conv_ln_g, conv_ln_b, q_norm, k_norm, kidx_norm,
              rel_bias, norm_ffn, ffn_up, ffn_conv_w, ffn_conv_b, ffn_down, ple_norm, ple_proj, ple_gate):
    W = dict(norm_mix=norm_mix, w_in=w_in, w_out=w_out, mu_shift=mu_shift, w0=w0, w_lora=w_lora, a0=a0,
             a_lora=a_lora, g_lora=g_lora, k_k=k_k, k_a=k_a, r_k=r_k, lnx_g=lnx_g, lnx_b=lnx_b,
             conv_w=conv_w, conv_b=conv_b, conv_ln_g=conv_ln_g, conv_ln_b=conv_ln_b, q_norm=q_norm,
             k_norm=k_norm, kidx_norm=kidx_norm, rel_bias=rel_bias, norm_ffn=norm_ffn, ffn_up=ffn_up,
             ffn_conv_w=ffn_conv_w, ffn_conv_b=ffn_conv_b, ffn_down=ffn_down, ple_norm=ple_norm,
             ple_proj=ple_proj, ple_gate=ple_gate)

    B, T, _ = x_prompt.shape
    dt = x_prompt.dtype
    pos_p = jnp.arange(T, dtype=jnp.int32)
    topk_p = min(TOPK_MAX, T // 4)
    st0 = (jnp.zeros((B, N_RWKV_COLS), dt), jnp.zeros((B, H_R, HD_R, HD_R), dt),
           jnp.zeros((B, CONV_W - 1, C_CONV), dt), jnp.zeros((B, FFN_CONV_W - 1, D_FF), dt))
    past0 = (jnp.zeros((B, 0, N_KV, HD_A), dt), jnp.zeros((B, 0, N_KV, HD_A), dt), jnp.zeros((B, 0, D_IDX), dt))
    x = x_prompt
    new_p = []
    for i in range(DEPTH):
        x, new = decoder_layer(i, x, p_prompt[i], pos_p, st0, past0, W, topk_p)
        new_p.append(new)
    y_prompt = x
    k_p, v_p, ki_p, wkv_p, shift_p, conv_p, ffn_p = stack_layers(new_p)

    Bs, Ts, _ = x_sample.shape
    past_len = page_table.shape[1] * cache_k.shape[2]
    pos_s = past_len + jnp.arange(Ts, dtype=jnp.int32)
    topk_s = min(TOPK_MAX, (past_len + Ts) // 4)
    x = x_sample
    new_s = []
    for i in range(DEPTH):
        past = tuple(c[i][page_table].reshape((Bs, past_len) + c.shape[3:]) for c in (cache_k, cache_v, cache_kidx))
        st = (state_shift[i], state_wkv[i], state_conv[i], state_ffn[i])
        x, new = decoder_layer(i, x, p_sample[i], pos_s, st, past, W, topk_s)
        new_s.append(new)
    y_sample = x
    k_s, v_s, ki_s, wkv_s, shift_s, conv_s, ffn_s = stack_layers(new_s)

    return (y_prompt, y_sample, k_p, v_p, ki_p, wkv_p, shift_p, conv_p, ffn_p,
            k_s, v_s, ki_s, wkv_s, shift_s, conv_s, ffn_s)


_drawn_inputs = setup_inputs


def setup_inputs(seed=0):
    import zlib

    import numpy as np

    out = dict(_drawn_inputs(seed))
    spreads = {}
    factors = {'lnx_g': 4.311,
     'lnx_b': 8.0,
     'conv_b': 4.798,
     'conv_ln_g': 3.199,
     'conv_ln_b': 8.0,
     'q_norm': 8.0,
     'ffn_conv_b': 5.951,
     'ple_norm': 24.994}
    for name, (base, spread) in spreads.items():
        noise = np.random.default_rng([zlib.crc32(name.encode()), seed]).standard_normal(out[name].shape)
        drawn = base * np.exp(spread * noise) if base else spread * noise
        out[name] = jnp.asarray(drawn.astype(out[name].dtype))
    for name, factor in factors.items():
        out[name] = (out[name] * factor).astype(out[name].dtype)
    return out
```

```python
from contextlib import ExitStack

import numpy as np

import concourse.bass as bass
from concourse import mybir

F32 = mybir.dt.float32
I32 = mybir.dt.int32
ALU = mybir.AluOpType
ACT = mybir.ActivationFunctionType
AX = mybir.AxisListType

P = 128
D_MODEL = 1024
KD = D_MODEL // P
SEQ = 2048
DEC_BATCH = 8
DEC_SEQ = 8
TS = DEC_BATCH * DEC_SEQ
NT = SEQ + TS
GROUP = 512
GROUPS = SEQ // GROUP
N_RWKV = 896
N_CONV = 512
N_CM = N_RWKV + N_CONV
CMB = N_CM // P
N_ATT = 1092
N_IN = N_CM + N_ATT
D_FF = 2816
FB = D_FF // P
D_PLE = 256
PAGE = 128
N_PAGES = 32
PAST = PAGE * N_PAGES
NORM_EPS = 1e-6
N_BUCKETS = 32
BIAS_W = 384


def wait_loop(engine, passed, sem, value):
    engine.wait_ge(sem, value)
    engine.sem_inc(passed, 1)


class Steps:

    def __init__(self, nc, ctx, name, names, unit=1, before=None):
        self.sem = ctx.enter_context(nc.semaphore(name))
        self.names, self.unit, self.before = list(names), unit, before
        self.ahead = 1 if unit == 1 and before is None else 0
        self.told = 0

    def open(self, engine):
        engine.sem_inc(self.sem, len(self.names))

    def step(self, name):
        want = self.names[self.told % len(self.names)]
        assert want == name, (name, want)
        self.told += 1
        return self.sem, self.unit

    def at(self, name, i):
        n = len(self.names) * self.unit
        return self.sem, i * n + (self.ahead * n + (self.names.index(name) + 1) * self.unit)

    def prev(self, name, i, iterations=0):
        if self.before is not None:
            return self.before.at(name, iterations - 1)
        n = len(self.names) * self.unit
        value = (self.ahead - 1) * n + (self.names.index(name) + 1) * self.unit
        assert value >= 0, name
        return self.sem, i * n + value


def make_identity(nc, ident, made):
    block = nc.Block()
    with block:
        @block.gpsimd
        def _(pool):
            pool.memset(ident, 0.0).then_inc(made, 1)
            pool.wait_ge(made, 1)
            pool.affine_select(out=ident, in_=ident, compare_op=ALU.not_equal, fill=1.0, base=0,
                               pattern=[[-1, P]], channel_multiplier=1).then_inc(made, 1)
            pool.wait_ge(made, 2)


def project_in(nc, ident, x_prompt, x_sample, norm_mix, w_in, zT, za):
    with ExitStack() as ctx:
        def sb(name, shape):
            return ctx.enter_context(nc.sbuf_tensor(name, shape, F32))

        w = sb("pi_w", [P, KD, N_IN])
        gain = sb("pi_gain", [P, D_MODEL])
        xt = sb("pi_x", [P, 4, D_MODEL])
        sq = sb("pi_sq", [P, D_MODEL])
        ss = sb("pi_ss", [P, 4])
        std = sb("pi_std", [P, 4])
        rstd = sb("pi_rstd", [P, 4])
        hn = sb("pi_hn", [P, 4, D_MODEL])
        hT = sb("pi_hT", [P, KD, GROUP])
        zc_sb = sb("pi_zc", [P, 2, GROUP])
        za_sb = sb("pi_za", [P, 2, N_ATT])
        eps = sb("pi_eps", [P, 1])
        zero = sb("pi_zero", [P, CMB])
        psT = ctx.enter_context(nc.psum_tensor("pi_psT", [P, 2, KD, P], F32))
        psz = ctx.enter_context(nc.psum_tensor("pi_psz", [P, 4, GROUP], F32))
        w_in_s = [ctx.enter_context(nc.semaphore(f"pi_w_loaded{k}")) for k in range(2)]
        g_in = ctx.enter_context(nc.semaphore("pi_gain_loaded"))
        const = ctx.enter_context(nc.semaphore("pi_constants"))
        zs = ctx.enter_context(nc.semaphore("pi_zero_stored"))

        att_cols = [(0, 512), (512, 512), (1024, N_ATT - 1024)]

        def plan(tag, tokens, before):
            subs = [(s, min(P, tokens - s * P)) for s in range(-(-tokens // P))]
            evac = [f"zc{c}" for c in range(CMB)] + [f"za{s}_{j}" for s, _ in subs for j in range(3)]
            b = before or {}
            return dict(
                tokens=tokens, subs=subs, evac=evac,
                x=[Steps(nc, ctx, f"pi_x_loaded{tag}{s}", ["x"], 16, b["x"][s] if b else None) for s, _ in subs],
                act=Steps(nc, ctx, f"pi_act{tag}", [f"{k}{s}" for s, _ in subs for k in ("sq", "std")] + [f"hT{s}" for s, _ in subs], 1, b.get("act")),
                vec=Steps(nc, ctx, f"pi_vec{tag}", [f"{k}{s}" for s, _ in subs for k in ("rstd", "hn")] + evac, 1, b.get("vec")),
                pe=Steps(nc, ctx, f"pi_pe{tag}", [f"T{s}" for s, _ in subs] + evac, 1, b.get("pe")),
                zc=[Steps(nc, ctx, f"pi_zc_stored{tag}{k}", ["s"], 16, None) for k in range(2)],
                za=[Steps(nc, ctx, f"pi_za_stored{tag}{k}", ["s"], 16, None) for k in range(2)],
            )

        main = plan("", GROUP, None)
        tail = plan("t", TS, main)
        nzc = [(CMB + 1) // 2, CMB // 2]

        block = ctx.enter_context(nc.Block())

        @block.sync
        def _(sp):
            sp.dma_start(gain[:, :], norm_mix.partition_broadcast(P)).then_inc(g_in, 16)
            for k in range(2):
                sp.dma_start(w[:, 4 * k:4 * k + 4, :], w_in.rearrange("(k p) n -> p k n", p=P)[:, 4 * k:4 * k + 4, :]).then_inc(w_in_s[k], 16)
            def loads(g, i, src):
                for s, n in g["subs"]:
                    sp.wait_ge(*g["vec"].prev(f"hn{s}", i, GROUPS))
                    sp.dma_start(xt[0:n, s, :], src(s, n)).then_inc(*g["x"][s].step("x"))

            with sp.Fori(0, GROUPS) as i:
                loads(main, i, lambda s, n: x_prompt[bass.ds(i * GROUP + s * P, n), :])
            loads(tail, 0, lambda s, n: x_sample[0:n, :])

        @block.gpsimd
        def _(pool):
            pool.memset(eps[:, :], NORM_EPS).then_inc(const, 1)
            pool.memset(zero[:, :], 0.0).then_inc(const, 1)
            pool.wait_ge(const, 2)
            with nc.allow_non_contiguous_dma(reason="one column"):
                pool.dma_start(zT[:, :, 0:1].rearrange("b p o -> p b o"), zero[:, :].unsqueeze(2)).then_inc(zs, 16)

            def stores(g, i, tok):
                n = g["tokens"]
                for c in range(CMB):
                    pool.wait_ge(*g["vec"].at(f"zc{c}", i))
                    pool.dma_start(zT[c, :, bass.ds(tok + 1, n)], zc_sb[:, c % 2, 0:n]).then_inc(g["zc"][c % 2].sem, 16)
                for s, m in g["subs"]:
                    pool.wait_ge(*g["vec"].at(f"za{s}_2", i))
                    pool.dma_start(za[bass.ds(tok + s * P, m), :], za_sb[0:m, s % 2, :]).then_inc(g["za"][s % 2].sem, 16)

            with pool.Fori(0, GROUPS) as i:
                stores(main, i, i * GROUP)
            stores(tail, 0, SEQ)
            pool.wait_ge(zs, 16)
            for k in range(2):
                pool.wait_ge(main["zc"][k].sem, 16 * GROUPS * nzc[k])
                pool.wait_ge(tail["zc"][k].sem, 16 * nzc[k])
                pool.wait_ge(main["za"][k].sem, 16 * GROUPS * 2)
            pool.wait_ge(tail["za"][0].sem, 16)

        @block.scalar
        def _(act):
            act.wait_ge(const, 2)
            main["act"].open(act)

            def body(g, i):
                a = g["act"]
                for s, n in g["subs"]:
                    act.wait_ge(*g["x"][s].at("x", i))
                    act.activation(sq[0:n, :], xt[0:n, s, :], ACT.Square, accum_out=ss[0:n, s:s + 1]).then_inc(*a.step(f"sq{s}"))
                    act.wait_ge(*a.at(f"sq{s}", i))
                    act.activation(std[0:n, s:s + 1], ss[0:n, s:s + 1], ACT.Sqrt, scale=1.0 / D_MODEL, bias=eps[0:n, :]).then_inc(*a.step(f"std{s}"))
                for s, n in g["subs"]:
                    act.wait_ge(*g["pe"].at(f"T{s}", i))
                    act.wait_ge(*g["pe"].prev(main["evac"][-1], i, GROUPS))
                    act.activation(hT[:, :, s * P:s * P + n], psT[:, s % 2, :, 0:n], ACT.Copy).then_inc(*a.step(f"hT{s}"))

            with act.Fori(0, GROUPS) as i:
                body(main, i)
            body(tail, 0)

        @block.tensor
        def _(pe):
            main["pe"].open(pe)
            for k in range(2):
                pe.wait_ge(w_in_s[k], 16)

            def body(g, i):
                n_tok, t, v, a = g["tokens"], g["pe"], g["vec"], g["act"]
                for s, n in g["subs"]:
                    pe.wait_ge(*v.at(f"hn{s}", i))
                    if s >= 2:
                        pe.wait_ge(*a.at(f"hT{s - 2}", i))
                    else:
                        pe.wait_ge(*a.prev(f"hT{s + 2}", i, GROUPS))
                    for k in range(KD):
                        mm = pe.transpose(psT[:, s % 2, k, 0:n], hn[0:n, s, k * P:(k + 1) * P], ident[0:n, 0:n])
                    mm.then_inc(*t.step(f"T{s}"))
                pe.wait_ge(*a.at(f"hT{g['subs'][-1][0]}", i))
                for u, name in enumerate(g["evac"]):
                    bank = u % 4
                    if u >= 4:
                        pe.wait_ge(*v.at(g["evac"][u - 4], i))
                    else:
                        last = max(x for x in range(len(main["evac"])) if x % 4 == bank)
                        pe.wait_ge(*v.prev(main["evac"][last], i, GROUPS))
                    if name.startswith("zc"):
                        c = int(name[2:])
                        for k in range(KD):
                            mm = pe.matmul(psz[:, bank, 0:n_tok], w[:, k, c * P:(c + 1) * P], hT[:, k, 0:n_tok], start=(k == 0), stop=(k == KD - 1))
                    else:
                        s, j = map(int, name[2:].split("_"))
                        at, m = att_cols[j]
                        n = g["subs"][s][1]
                        for k in range(KD):
                            mm = pe.matmul(psz[0:n, bank, 0:m], hT[:, k, s * P:s * P + n], w[:, k, N_CM + at:N_CM + at + m], start=(k == 0), stop=(k == KD - 1))
                    mm.then_inc(*t.step(name))

            with pe.Fori(0, GROUPS) as i:
                body(main, i)
            body(tail, 0)

        @block.vector
        def _(dve):
            dve.wait_ge(g_in, 16)
            main["vec"].open(dve)

            def body(g, i, stored):
                n_tok, v, a = g["tokens"], g["vec"], g["act"]
                for s, n in g["subs"]:
                    dve.wait_ge(*a.at(f"std{s}", i))
                    dve.reciprocal(rstd[0:n, s:s + 1], std[0:n, s:s + 1]).then_inc(*v.step(f"rstd{s}"))
                    dve.wait_ge(*v.at(f"rstd{s}", i))
                    dve.wait_ge(*g["pe"].prev(f"T{s}", i, GROUPS))
                    dve.scalar_tensor_tensor(out=hn[0:n, s, :], in0=xt[0:n, s, :], scalar=rstd[0:n, s:s + 1], in1=gain[0:n, :],
                                             op0=ALU.mult, op1=ALU.mult).then_inc(*v.step(f"hn{s}"))
                for u, name in enumerate(g["evac"]):
                    bank = u % 4
                    dve.wait_ge(*g["pe"].at(name, i))
                    if name.startswith("zc"):
                        c = int(name[2:])
                        dve.wait_ge(*stored("zc", c % 2, c // 2))
                        dve.tensor_copy(zc_sb[:, c % 2, 0:n_tok], psz[:, bank, 0:n_tok]).then_inc(*v.step(name))
                    else:
                        s, j = map(int, name[2:].split("_"))
                        at, m = att_cols[j]
                        n = g["subs"][s][1]
                        if j == 0:
                            dve.wait_ge(*stored("za", s % 2, s // 2))
                        dve.tensor_copy(za_sb[0:n, s % 2, at:at + m], psz[0:n, bank, 0:m]).then_inc(*v.step(name))

            with dve.Fori(0, GROUPS) as i:
                per = dict(zc=nzc, za=[2, 2])
                body(main, i, lambda kind, k, j: (main[kind][k].sem, i * (16 * per[kind][k]) + 16 * j))

            def tail_stored(kind, k, j):
                per = dict(zc=nzc, za=[2, 2])
                if j == 0:
                    return main[kind][k].sem, 16 * GROUPS * per[kind][k]
                return tail[kind][k].sem, 16 * j
            body(tail, 0, tail_stored)


def mix_out(nc, ident, oT, x_prompt, x_sample, w_out, norm_ffn, x1, h2T):
    with ExitStack() as ctx:
        def sb(name, shape):
            return ctx.enter_context(nc.sbuf_tensor(name, shape, F32))

        w = sb("mo_w", [P, KD, D_MODEL])
        gain = sb("mo_gain", [P, D_MODEL])
        o_sb = sb("mo_o", [P, 2, KD, P])
        xt = sb("mo_x", [P, 2, D_MODEL])
        x1_sb = sb("mo_x1", [P, 2, D_MODEL])
        sq = sb("mo_sq", [P, D_MODEL])
        ss = sb("mo_ss", [P, 2])
        std = sb("mo_std", [P, 2])
        rstd = sb("mo_rstd", [P, 2])
        hn = sb("mo_hn", [P, 2, D_MODEL])
        hT = sb("mo_hT", [P, 2, KD, P])
        eps = sb("mo_eps", [P, 1])
        psm = ctx.enter_context(nc.psum_tensor("mo_psm", [P, 2, 2, 512], F32))
        psT = ctx.enter_context(nc.psum_tensor("mo_psT", [P, 2, KD, P], F32))
        w_ld = ctx.enter_context(nc.semaphore("mo_w_loaded"))
        passed = ctx.enter_context(nc.semaphore("mo_waits_passed"))
        const = ctx.enter_context(nc.semaphore("mo_constants"))
        PAIRS = SEQ // P // 2

        def plan(tag, subs, before):
            b = before or {}
            st = lambda k, names, unit=1: Steps(nc, ctx, f"mo_{k}{tag}", names, unit, b.get(k))
            return dict(
                subs=subs,
                **{f"x{s}": st(f"x{s}", ["x", "o"], 16) for s, _ in subs},
                **{f"x1s{s}": st(f"x1s{s}", ["x1"], 16) for s, _ in subs},
                **{f"hs{s}": st(f"hs{s}", ["h"], 16) for s, _ in subs},
                pe=st("pe", [f"M{s}" for s, _ in subs] + [f"T{s}" for s, _ in subs]),
                act=st("act", [f"{k}{s}" for s, _ in subs for k in ("sq", "std")] + [f"hT{s}" for s, _ in subs]),
                vec=st("vec", [f"{k}{s}" for s, _ in subs for k in ("x1", "rstd", "hn")]),
            )

        main = plan("", [(0, P), (1, P)], None)
        tail = plan("t", [(0, TS)], main)
        block = ctx.enter_context(nc.Block())

        @block.sync
        def _(sp):
            sp.dma_start(gain[:, :], norm_ffn.partition_broadcast(P)).then_inc(w_ld, 16)
            sp.dma_start(w[:, :, :], w_out.rearrange("(k p) n -> p k n", p=P)).then_inc(w_ld, 16)

            def body(g, i, xsrc, tok):
                for s, n in g["subs"]:
                    src_o = oT[:, :, bass.ds(tok(s), n)].rearrange("k p t -> p k t")
                    src_x = xsrc(s, n)
                    wait_loop(sp, passed, *g["vec"].prev(f"x1{s}", i, PAIRS))
                    sp.dma_start(xt[0:n, s, :], src_x).then_inc(*g[f"x{s}"].step("x"))
                    wait_loop(sp, passed, *g["pe"].prev(f"M{s}", i, PAIRS))
                    sp.dma_start(o_sb[:, s, :, 0:n], src_o).then_inc(*g[f"x{s}"].step("o"))

            with sp.Fori(0, PAIRS) as i:
                at = [sp.snap(i * 256 + s * P) for s in range(2)]
                body(main, i, lambda s, n: x_prompt[bass.ds(at[s], n), :], lambda s: at[s])
            body(tail, 0, lambda s, n: x_sample[0:n, :], lambda s: SEQ)

        @block.gpsimd
        def _(pool):
            pool.memset(eps[:, :], NORM_EPS).then_inc(const, 1)

            def body(g, i, tok):
                for s, n in g["subs"]:
                    pool.wait_ge(*g["vec"].at(f"x1{s}", i))
                    pool.dma_start(x1[bass.ds(tok + s * P, n), :], x1_sb[0:n, s, :]).then_inc(*g[f"x1s{s}"].step("x1"))
                    pool.wait_ge(*g["act"].at(f"hT{s}", i))
                    pool.dma_start(h2T[:, :, bass.ds(tok + s * P, n)].rearrange("k p t -> p k t"), hT[:, s, :, 0:n]).then_inc(*g[f"hs{s}"].step("h"))

            with pool.Fori(0, PAIRS) as i:
                body(main, i, i * 256)
            body(tail, 0, SEQ)
            for g, n in ((main, PAIRS), (tail, 1)):
                for s, _ in g["subs"]:
                    pool.wait_ge(*g[f"x1s{s}"].at("x1", n - 1))
                    pool.wait_ge(*g[f"hs{s}"].at("h", n - 1))

        @block.tensor
        def _(pe):
            main["pe"].open(pe)
            pe.wait_ge(w_ld, 32)

            def body(g, i):
                for s, n in g["subs"]:
                    pe.wait_ge(*g[f"x{s}"].at("o", i))
                    pe.wait_ge(*g["vec"].prev(f"x1{s}", i, PAIRS))
                    for c in range(2):
                        for k in range(KD):
                            mm = pe.matmul(psm[0:n, s, c, :], o_sb[:, s, k, 0:n], w[:, k, c * 512:(c + 1) * 512], start=(k == 0), stop=(k == KD - 1))
                    mm.then_inc(*g["pe"].step(f"M{s}"))
                for s, n in g["subs"]:
                    pe.wait_ge(*g["vec"].at(f"hn{s}", i))
                    pe.wait_ge(*g["act"].prev(f"hT{s}", i, PAIRS))
                    for k in range(KD):
                        mm = pe.transpose(psT[:, s, k, 0:n], hn[0:n, s, k * P:(k + 1) * P], ident[0:n, 0:n])
                    mm.then_inc(*g["pe"].step(f"T{s}"))

            with pe.Fori(0, PAIRS) as i:
                body(main, i)
            body(tail, 0)

        @block.scalar
        def _(act):
            main["act"].open(act)
            act.wait_ge(const, 1)

            def body(g, i):
                a = g["act"]
                for s, n in g["subs"]:
                    act.wait_ge(*g["vec"].at(f"x1{s}", i))
                    act.activation(sq[0:n, :], x1_sb[0:n, s, :], ACT.Square, accum_out=ss[0:n, s:s + 1]).then_inc(*a.step(f"sq{s}"))
                    act.wait_ge(*a.at(f"sq{s}", i))
                    act.activation(std[0:n, s:s + 1], ss[0:n, s:s + 1], ACT.Sqrt, scale=1.0 / D_MODEL, bias=eps[0:n, :]).then_inc(*a.step(f"std{s}"))
                for s, n in g["subs"]:
                    act.wait_ge(*g["pe"].at(f"T{s}", i))
                    act.wait_ge(*g[f"hs{s}"].prev("h", i, PAIRS))
                    act.activation(hT[:, s, :, 0:n], psT[:, s, :, 0:n], ACT.Copy).then_inc(*a.step(f"hT{s}"))

            with act.Fori(0, PAIRS) as i:
                body(main, i)
            body(tail, 0)

        @block.vector
        def _(dve):
            main["vec"].open(dve)
            dve.wait_ge(w_ld, 32)

            def body(g, i):
                v = g["vec"]
                for s, n in g["subs"]:
                    dve.wait_ge(*g["pe"].at(f"M{s}", i))
                    dve.wait_ge(*g[f"x{s}"].at("o", i))
                    dve.wait_ge(*g[f"x1s{s}"].prev("x1", i, PAIRS))
                    dve.wait_ge(*g["act"].prev(f"sq{s}", i, PAIRS))
                    dve.tensor_tensor(x1_sb[0:n, s, :], psm[0:n, s, :, :].rearrange("p a b -> p (a b)"), xt[0:n, s, :], ALU.add).then_inc(*v.step(f"x1{s}"))
                    dve.wait_ge(*g["act"].at(f"std{s}", i))
                    dve.reciprocal(rstd[0:n, s:s + 1], std[0:n, s:s + 1]).then_inc(*v.step(f"rstd{s}"))
                    dve.wait_ge(*v.at(f"rstd{s}", i))
                    dve.wait_ge(*g["pe"].prev(f"T{s}", i, PAIRS))
                    dve.scalar_tensor_tensor(out=hn[0:n, s, :], in0=x1_sb[0:n, s, :], scalar=rstd[0:n, s:s + 1], in1=gain[0:n, :],
                                             op0=ALU.mult, op1=ALU.mult).then_inc(*v.step(f"hn{s}"))

            with dve.Fori(0, PAIRS) as i:
                body(main, i)
            body(tail, 0)


def ffn_up(nc, h2T, up, conv_w, conv_b, state_ffn, aT, ffn_p, ffn_s):
    with ExitStack() as ctx:
        def sb(name, shape):
            return ctx.enter_context(nc.sbuf_tensor(name, shape, F32))

        W1 = DEC_SEQ + 2
        hT = sb("fu_h", [P, KD, NT])
        wg = sb("fu_wg", [P, 2, KD, P])
        wv = sb("fu_wv", [P, 2, KD, P])
        cw = sb("fu_cw", [P, 2, 4])
        gpre = sb("fu_gpre", [P, 2, SEQ + 2])
        gprs = sb("fu_gprs", [P, 2, DEC_BATCH, W1])
        gate = sb("fu_gate", [P, 2, NT])
        a_sb = sb("fu_a", [P, 2, NT])
        ps = ctx.enter_context(nc.psum_tensor("fu_ps", [P, 8, 512], F32))
        h_ld = [ctx.enter_context(nc.semaphore(f"fu_h_loaded{k}")) for k in range(2)]
        const = ctx.enter_context(nc.semaphore("fu_constants"))
        passed = ctx.enter_context(nc.semaphore("fu_waits_passed"))
        groups = [(g * 512, 512) for g in range(4)] + [(SEQ, TS)]
        PAIRS = FB // 2
        uses = [(b, kind, g) for b in range(2) for kind in ("g", "v") for g in range(5)]
        bank_of = {u: n % 8 for n, u in enumerate(uses)}
        order = [f"{k}{b}{g}" for b, k, g in uses]

        def before_of(n):
            same = [m for m in range(len(uses)) if m % 8 == n % 8]
            at = same.index(n)
            return (order[same[at - 1]], at == 0)

        pe_s = Steps(nc, ctx, "fu_pe", order)
        act_s = Steps(nc, ctx, "fu_act", [x for b in range(2) for x in [f"g{b}{g}" for g in range(5)] + [f"gelu{b}"]])
        vec_s = Steps(nc, ctx, "fu_vec", [x for b in range(2) for x in [f"c{b}{j}" for j in range(6)] + [f"v{b}{g}" for g in range(5)]])
        w_s = [Steps(nc, ctx, f"fu_w_loaded{b}", ["w"], 16 * 6) for b in range(2)]
        for s in w_s:
            s.ahead = 0
        a_s = [Steps(nc, ctx, f"fu_a_stored{b}", ["a"], 16) for b in range(2)]
        f_s = [Steps(nc, ctx, f"fu_state_stored{b}", ["f"], 48) for b in range(2)]
        for s in f_s:
            s.ahead = 0
        block = ctx.enter_context(nc.Block())

        @block.sync
        def _(sp):
            for k in range(2):
                sp.dma_start(hT[:, 4 * k:4 * k + 4, :], h2T[4 * k:4 * k + 4, :, :].rearrange("k p t -> p k t")).then_inc(h_ld[k], 16)
            up_k = up.rearrange("(k p) n -> p k n", p=P)
            with nc.allow_non_contiguous_dma(reason="channel-major taps and states"), sp.Fori(0, PAIRS) as i:
                at_b = [sp.snap(i * 256 + b * P) for b in range(2)]
                at_v = [sp.snap(i * 256 + (b * P + D_FF)) for b in range(2)]
                for b in range(2):
                    at = at_b[b]
                    wait_loop(sp, passed, *pe_s.prev(f"v{b}4", i))
                    wait_loop(sp, passed, *vec_s.prev(f"c{b}5", i))
                    sp.dma_start(wg[:, b, :, :], up_k[:, :, bass.ds(at, P)]).then_inc(w_s[b].sem, 16)
                    sp.dma_start(wv[:, b, :, :], up_k[:, :, bass.ds(at_v[b], P)]).then_inc(w_s[b].sem, 16)
                    sp.dma_start(cw[:, b, 0:3], conv_w[:, bass.ds(at, P)].rearrange("w c -> c w")).then_inc(w_s[b].sem, 16)
                    sp.dma_start(cw[:, b, 3:4], conv_b[bass.ds(at, P)].unsqueeze(1)).then_inc(w_s[b].sem, 16)
                    sp.wait_ge(*f_s[b].prev("f", i))
                    for j in range(2):
                        sp.dma_start(gprs[:, b, :, j], state_ffn[:, j, bass.ds(at, P)].rearrange("b c -> c b")).then_inc(w_s[b].sem, 16)

        @block.gpsimd
        def _(pool):
            pool.memset(gpre[:, :, 0:2], 0.0).then_inc(const, 1)
            with nc.allow_non_contiguous_dma(reason="channel-major states"), pool.Fori(0, PAIRS) as i:
                for b in range(2):
                    at = i * 256 + b * P
                    pool.wait_ge(*act_s.at(f"g{b}4", i))
                    pool.dma_start(ffn_p[:, bass.ds(at, P)].rearrange("w c -> c w"), gpre[:, b, SEQ:SEQ + 2]).then_inc(f_s[b].sem, 16)
                    for j in range(2):
                        pool.dma_start(ffn_s[:, j, bass.ds(at, P)].rearrange("b c -> c b"), gprs[:, b, :, DEC_SEQ + j]).then_inc(f_s[b].sem, 16)
                    pool.wait_ge(*vec_s.at(f"v{b}4", i))
                    pool.dma_start(aT[bass.ds(i * 2 + b, 1), :, :].rearrange("o p t -> (o p) t"), a_sb[:, b, :]).then_inc(*a_s[b].step("a"))
            for b in range(2):
                pool.wait_ge(*a_s[b].at("a", PAIRS - 1))
                pool.wait_ge(*f_s[b].at("f", PAIRS - 1))

        @block.tensor
        def _(pe):
            pe_s.open(pe)
            for k in range(2):
                pe.wait_ge(h_ld[k], 16)
            with pe.Fori(0, PAIRS) as i:
                for n, (b, kind, g) in enumerate(uses):
                    if kind == "g" and g == 0:
                        pe.wait_ge(*w_s[b].at("w", i))
                    last, earlier = before_of(n)
                    reader = act_s if last[0] == "g" else vec_s
                    pe.wait_ge(*(reader.prev(last, i) if earlier else reader.at(last, i)))
                    at, m = groups[g]
                    w = wg if kind == "g" else wv
                    for k in range(KD):
                        mm = pe.matmul(ps[:, bank_of[b, kind, g], 0:m], w[:, b, k, :], hT[:, k, at:at + m], start=(k == 0), stop=(k == KD - 1))
                    mm.then_inc(*pe_s.step(order[n]))

        @block.scalar
        def _(act):
            act_s.open(act)
            act.wait_ge(const, 1)
            with act.Fori(0, PAIRS) as i:
                for b in range(2):
                    act.wait_ge(*vec_s.prev(f"c{b}5", i))
                    act.wait_ge(*f_s[b].prev("f", i))
                    for g in range(5):
                        act.wait_ge(*pe_s.at(f"g{b}{g}", i))
                        src = ps[:, bank_of[b, "g", g], 0:groups[g][1]]
                        if g < 4:
                            dst = gpre[:, b, 2 + g * 512:2 + (g + 1) * 512]
                        else:
                            dst, src = gprs[:, b, :, 2:W1], src.rearrange("p (b t) -> p b t", t=DEC_SEQ)
                        act.activation(dst, src, ACT.Copy).then_inc(*act_s.step(f"g{b}{g}"))
                    act.wait_ge(*vec_s.at(f"c{b}5", i))
                    act.activation(gate[:, b, :], gate[:, b, :], ACT.Gelu).then_inc(*act_s.step(f"gelu{b}"))

        @block.vector
        def _(dve):
            vec_s.open(dve)
            with dve.Fori(0, PAIRS) as i:
                for b in range(2):
                    dve.wait_ge(*w_s[b].at("w", i))
                    dve.wait_ge(*act_s.at(f"g{b}4", i))
                    dve.wait_ge(*vec_s.prev(f"v{b}4", i))
                    tap = lambda j: cw[:, b, j:j + 1]
                    parts = [(gate[:, b, 0:SEQ], lambda j: gpre[:, b, j:j + SEQ]),
                             (gate[:, b, SEQ:NT].rearrange("p (b t) -> p b t", t=DEC_SEQ), lambda j: gprs[:, b, :, j:j + DEC_SEQ])]
                    for j in range(3):
                        for q, (out, src) in enumerate(parts):
                            if j == 0:
                                op = dve.tensor_scalar(out, src(0), tap(0), tap(3), ALU.mult, ALU.add)
                            else:
                                dve.wait_ge(*vec_s.at(f"c{b}{2 * j + q - 2}", i))
                                op = dve.scalar_tensor_tensor(out=out, in0=src(j), scalar=tap(j), in1=out, op0=ALU.mult, op1=ALU.add)
                            op.then_inc(*vec_s.step(f"c{b}{2 * j + q}"))
                    dve.wait_ge(*act_s.at(f"gelu{b}", i))
                    dve.wait_ge(*a_s[b].prev("a", i))
                    for g, (at, m) in enumerate(groups):
                        dve.wait_ge(*pe_s.at(f"v{b}{g}", i))
                        dve.tensor_tensor(a_sb[:, b, at:at + m], ps[:, bank_of[b, "v", g], 0:m], gate[:, b, at:at + m], ALU.mult).then_inc(*vec_s.step(f"v{b}{g}"))


def ffn_down(nc, ident, aT, x1, down, ple_norm, ple_gate, ple_proj, p_prompt, p_sample, y_p, y_s):
    with ExitStack() as ctx:
        def sb(name, shape):
            return ctx.enter_context(nc.sbuf_tensor(name, shape, F32))

        KP = D_PLE // P
        w = sb("fd_w", [P, FB, D_MODEL])
        wg = sb("fd_wg", [P, KD, D_MODEL])
        wp = sb("fd_wp", [P, KP, D_MODEL])
        gain = sb("fd_gain", [P, D_MODEL])
        a_sb = sb("fd_a", [P, 2, FB, P])
        pt = sb("fd_p", [P, 2, D_PLE])
        pT = sb("fd_pT", [P, KP, P])
        x2 = sb("fd_x2", [P, 2, D_MODEL])
        sg = sb("fd_sg", [P, D_MODEL])
        ss = sb("fd_ss", [P, 2])
        std = sb("fd_std", [P, 2])
        rstd = sb("fd_rstd", [P, 2])
        hn = sb("fd_hn", [P, 2, D_MODEL])
        hT = sb("fd_hT", [P, KD, P])
        eps = sb("fd_eps", [P, 1])
        psf = ctx.enter_context(nc.psum_tensor("fd_psf", [P, 2, 2, 512], F32))
        psT = ctx.enter_context(nc.psum_tensor("fd_psT", [P, KD, P], F32))
        psg = ctx.enter_context(nc.psum_tensor("fd_psg", [P, 2, 512], F32))
        psl = psT[:, :, :].rearrange("p (c k) t -> p c (k t)", c=2)
        w_ld = ctx.enter_context(nc.semaphore("fd_w_loaded"))
        passed = ctx.enter_context(nc.semaphore("fd_waits_passed"))
        const = ctx.enter_context(nc.semaphore("fd_constants"))
        PAIRS = SEQ // P // 2

        def plan(tag, subs, before):
            b = before or {}
            st = lambda k, names, unit=1: Steps(nc, ctx, f"fd_{k}{tag}", names, unit, b.get(k))
            return dict(
                subs=subs,
                **{f"a{s}": st(f"a{s}", ["a"], 16) for s, _ in subs},
                **{f"x{s}": st(f"x{s}", ["x"], 16) for s, _ in subs},
                **{f"p{s}": st(f"p{s}", ["p"], 16) for s, _ in subs},
                **{f"y{s}": st(f"y{s}", ["y"], 16) for s, _ in subs},
                pe=st("pe", [f"F{s}" for s, _ in subs] + [f"{k}{s}" for s, _ in subs for k in ("P", "T", "G", "L")]),
                act=st("act", [f"{k}{s}" for s, _ in subs for k in ("sq", "std")] + [f"{k}{s}" for s, _ in subs for k in ("pT", "hT", "sg")]),
                vec=st("vec", [f"{k}{s}" for s, _ in subs for k in ("x2", "rstd", "hn")] + [f"{k}{s}" for s, _ in subs for k in ("m", "y")]),
            )

        main = plan("", [(0, P), (1, P)], None)
        tail = plan("t", [(0, TS)], main)
        block = ctx.enter_context(nc.Block())

        @block.sync
        def _(sp):
            sp.dma_start(gain[:, :], ple_norm.partition_broadcast(P)).then_inc(w_ld, 16)
            sp.dma_start(w[:, :, :], down.rearrange("(k p) n -> p k n", p=P)).then_inc(w_ld, 16)
            sp.dma_start(wg[:, :, :], ple_gate.rearrange("(k p) n -> p k n", p=P)).then_inc(w_ld, 16)
            sp.dma_start(wp[:, :, :], ple_proj.rearrange("(k p) n -> p k n", p=P)).then_inc(w_ld, 16)

            def body(g, i, tok, psrc):
                for s, n in g["subs"]:
                    src_a = aT[:, :, bass.ds(tok(s), n)].rearrange("k p t -> p k t")
                    src_p, src_x = psrc(s, n), x1[bass.ds(tok(s), n), :]
                    wait_loop(sp, passed, *g["pe"].prev(f"F{s}", i, PAIRS))
                    sp.dma_start(a_sb[:, s, :, 0:n], src_a).then_inc(*g[f"a{s}"].step("a"))
                    wait_loop(sp, passed, *g["pe"].prev(f"P{s}", i, PAIRS))
                    sp.dma_start(pt[0:n, s, :], src_p).then_inc(*g[f"p{s}"].step("p"))
                    sp.wait_ge(*g[f"y{s}"].prev("y", i, PAIRS))
                    sp.dma_start(x2[0:n, s, :], src_x).then_inc(*g[f"x{s}"].step("x"))

            with sp.Fori(0, PAIRS) as i:
                at = [sp.snap(i * 256 + s * P) for s in range(2)]
                body(main, i, lambda s: at[s], lambda s, n: p_prompt[bass.ds(at[s], n), :])
            body(tail, 0, lambda s: SEQ, lambda s, n: p_sample[0:n, :])

        @block.gpsimd
        def _(pool):
            pool.memset(eps[:, :], NORM_EPS).then_inc(const, 1)

            def body(g, i, dst):
                for s, n in g["subs"]:
                    pool.wait_ge(*g["vec"].at(f"y{s}", i))
                    pool.dma_start(dst(s, n), x2[0:n, s, :]).then_inc(*g[f"y{s}"].step("y"))

            with pool.Fori(0, PAIRS) as i:
                body(main, i, lambda s, n: y_p[bass.ds(i * 256 + s * P, n), :])
            body(tail, 0, lambda s, n: y_s[0:n, :])
            for g, n in ((main, PAIRS), (tail, 1)):
                for s, _ in g["subs"]:
                    pool.wait_ge(*g[f"y{s}"].at("y", n - 1))

        @block.tensor
        def _(pe):
            main["pe"].open(pe)
            pe.wait_ge(w_ld, 64)

            def body(g, i):
                t, v, a = g["pe"], g["vec"], g["act"]
                for s, n in g["subs"]:
                    pe.wait_ge(*g[f"a{s}"].at("a", i))
                    pe.wait_ge(*v.prev(f"x2{s}", i, PAIRS))
                    for c in range(2):
                        for k in range(FB):
                            mm = pe.matmul(psf[0:n, s, c, :], a_sb[:, s, k, 0:n], w[:, k, c * 512:(c + 1) * 512], start=(k == 0), stop=(k == FB - 1))
                    mm.then_inc(*t.step(f"F{s}"))
                for s, n in g["subs"]:
                    last = g["subs"][-1][0] if s else None
                    pe.wait_ge(*g[f"p{s}"].at("p", i))
                    pe.wait_ge(*(v.at("m0", i) if s else v.prev("m1", i, PAIRS)))
                    for k in range(KP):
                        mm = pe.transpose(psT[:, k, 0:n], pt[0:n, s, k * P:(k + 1) * P], ident[0:n, 0:n])
                    mm.then_inc(*t.step(f"P{s}"))
                    pe.wait_ge(*v.at(f"hn{s}", i))
                    pe.wait_ge(*a.at(f"pT{s}", i))
                    for k in range(KD):
                        mm = pe.transpose(psT[:, k, 0:n], hn[0:n, s, k * P:(k + 1) * P], ident[0:n, 0:n])
                    mm.then_inc(*t.step(f"T{s}"))
                    pe.wait_ge(*a.at(f"hT{s}", i))
                    pe.wait_ge(*(a.at("sg0", i) if s else a.prev("sg1", i, PAIRS)))
                    for c in range(2):
                        for k in range(KD):
                            mm = pe.matmul(psg[0:n, c, :], hT[:, k, 0:n], wg[:, k, c * 512:(c + 1) * 512], start=(k == 0), stop=(k == KD - 1))
                    mm.then_inc(*t.step(f"G{s}"))
                    for c in range(2):
                        for k in range(KP):
                            mm = pe.matmul(psl[0:n, c, :], pT[:, k, 0:n], wp[:, k, c * 512:(c + 1) * 512], start=(k == 0), stop=(k == KP - 1))
                    mm.then_inc(*t.step(f"L{s}"))

            with pe.Fori(0, PAIRS) as i:
                body(main, i)
            body(tail, 0)

        @block.scalar
        def _(act):
            main["act"].open(act)
            act.wait_ge(const, 1)

            def body(g, i):
                a = g["act"]
                for s, n in g["subs"]:
                    act.wait_ge(*g["vec"].at(f"x2{s}", i))
                    if s == 0:
                        act.wait_ge(*g["vec"].prev("y1", i, PAIRS))
                    else:
                        act.wait_ge(*a.at("std0", i))
                    act.activation(sg[0:n, :], x2[0:n, s, :], ACT.Square, accum_out=ss[0:n, s:s + 1]).then_inc(*a.step(f"sq{s}"))
                    act.wait_ge(*a.at(f"sq{s}", i))
                    act.activation(std[0:n, s:s + 1], ss[0:n, s:s + 1], ACT.Sqrt, scale=1.0 / D_MODEL, bias=eps[0:n, :]).then_inc(*a.step(f"std{s}"))
                for s, n in g["subs"]:
                    act.wait_ge(*g["pe"].at(f"P{s}", i))
                    act.wait_ge(*(g["pe"].at("L0", i) if s else g["pe"].prev("L1", i, PAIRS)))
                    act.activation(pT[:, :, 0:n], psT[:, 0:KP, 0:n], ACT.Copy).then_inc(*a.step(f"pT{s}"))
                    act.wait_ge(*g["pe"].at(f"T{s}", i))
                    act.activation(hT[:, :, 0:n], psT[:, :, 0:n], ACT.Copy).then_inc(*a.step(f"hT{s}"))
                    act.wait_ge(*g["pe"].at(f"G{s}", i))
                    if s:
                        act.wait_ge(*g["vec"].at("y0", i))
                    act.activation(sg[0:n, :], psg[0:n, :, :].rearrange("p a b -> p (a b)"), ACT.Sigmoid).then_inc(*a.step(f"sg{s}"))

            with act.Fori(0, PAIRS) as i:
                body(main, i)
            body(tail, 0)

        @block.vector
        def _(dve):
            main["vec"].open(dve)
            dve.wait_ge(w_ld, 64)

            def body(g, i):
                v = g["vec"]
                for s, n in g["subs"]:
                    dve.wait_ge(*g["pe"].at(f"F{s}", i))
                    dve.wait_ge(*g[f"x{s}"].at("x", i))
                    dve.tensor_tensor(x2[0:n, s, :], psf[0:n, s, :, :].rearrange("p a b -> p (a b)"), x2[0:n, s, :], ALU.add).then_inc(*v.step(f"x2{s}"))
                    dve.wait_ge(*g["act"].at(f"std{s}", i))
                    dve.reciprocal(rstd[0:n, s:s + 1], std[0:n, s:s + 1]).then_inc(*v.step(f"rstd{s}"))
                    dve.wait_ge(*v.at(f"rstd{s}", i))
                    dve.wait_ge(*g["pe"].prev(f"T{s}", i, PAIRS))
                    dve.scalar_tensor_tensor(out=hn[0:n, s, :], in0=x2[0:n, s, :], scalar=rstd[0:n, s:s + 1], in1=gain[0:n, :],
                                             op0=ALU.mult, op1=ALU.mult).then_inc(*v.step(f"hn{s}"))
                for s, n in g["subs"]:
                    dve.wait_ge(*g["pe"].at(f"L{s}", i))
                    dve.wait_ge(*g["act"].at(f"sg{s}", i))
                    dve.tensor_tensor(sg[0:n, :], psl[0:n, :, :].rearrange("p a b -> p (a b)"), sg[0:n, :], ALU.mult).then_inc(*v.step(f"m{s}"))
                    dve.wait_ge(*v.at(f"m{s}", i))
                    dve.tensor_tensor(x2[0:n, s, :], x2[0:n, s, :], sg[0:n, :], ALU.add).then_inc(*v.step(f"y{s}"))

            with dve.Fori(0, PAIRS) as i:
                body(main, i)
            body(tail, 0)


def rwkv(nc, ident, t):
    with ExitStack() as ctx:
        def sb(name, shape):
            return ctx.enter_context(nc.sbuf_tensor("rw_" + name, shape, F32))

        C, H = 64, 4
        EPS = 64e-5
        tri = sb("tri", [P, 2, P])
        x16 = sb("x16", [P, P])
        x32 = sb("x32", [P, P])
        x64 = sb("x64", [P, P])
        o32 = sb("o32", [P, P])
        o64 = sb("o64", [P, P])
        x16T = sb("x16T", [P, P])
        headones = sb("headones", [P, P])
        cmask = sb("cmask", [P, 2])
        mu = sb("mu", [P, 7])
        w0 = sb("w0", [P, 256])
        chp = sb("chp", [P, 3, 2])
        rk_w = sb("rk_w", [P, 2, H])
        ln_g = sb("ln_g", [P, 256])
        ln_b = sb("ln_b", [P, 256])
        lora = sb("lora", [P, 256])
        eps = sb("eps", [P, 1])
        zin = sb("zin", [P, 2, 7, C + 1])
        zd = sb("zd", [P, 7, 2, C])
        zs = sb("zs", [P, 7, 2, C])
        low = sb("low", [P, P])
        u = sb("u", [P, 256])
        lw = sb("lw", [P, 256])
        g_sb = sb("g", [P, 256])
        a_sb = sb("a", [P, 2, P])
        kraw = sb("kraw", [P, 2, P])
        sqk = sb("sqk", [P, 2, P])
        rn = sb("rn", [P, 2, P])
        kk = sb("kk", [P, 2, P])
        kt = sb("kt", [P, 2, P])
        pall = sb("pall", [P, 2, 2, P])
        pinv = sb("pinv", [P, 2, P])
        RA = sb("RA", [P, 2, 2, P])
        Bc = sb("Bc", [P, 2, P])
        Kc = sb("Kc", [P, 2, P])
        rk = sb("rk", [P, 2, P])
        tok = sb("tok", [P, 4, 256])
        bonus = sb("bonus", [P, H])
        X = sb("X", [P, H, P])
        XT = sb("XT", [P, H, P])
        O32 = sb("O32", [P, H, P])
        O64 = sb("O64", [P, H, P])
        QB = sb("QB", [P, H, P])
        KM = sb("KM", [P, H, 2, P])
        X2 = sb("X2", [P, H, P])
        X2T = sb("X2T", [P, H, P])
        T = [sb(f"T{j}", [P, H, P]) for j in range(2)]
        AM = sb("AM", [P, H, P])
        WU = sb("WU", [P, H, P])
        R2 = sb("R2", [P, 2, P])
        y0 = sb("y0", [P, H, C])
        GT = sb("GT", [P, 2, 2, C])
        Hs = sb("Hs", [P, 2, 2, C])
        ST = sb("ST", [P, 2, C])
        St = sb("St", [P, 2, C])
        S_in = sb("S_in", [P, 2, 2, C])
        S_out = sb("S_out", [P, 2, 2, C])
        sel8 = sb("sel8", [P, 2])
        y = sb("y", [P, H, C])
        yq = sb("yq", [P, H, C])
        mean = sb("mean", [P, H])
        var = sb("var", [P, H])
        oT_sb = sb("oT", [P, 2, P])
        pb = [ctx.enter_context(nc.psum_tensor(f"rw_ps{k}", [P, 512], F32)) for k in range(8)]
        bank = lambda k: pb[k][:, :]
        heads = lambda k: pb[k][:, :].rearrange("p (h t) -> p h t", h=H)
        par = ctx.enter_context(nc.semaphore("rw_parameters_loaded"))
        const = ctx.enter_context(nc.semaphore("rw_constants"))
        shift_st = ctx.enter_context(nc.semaphore("rw_shift_stored"))
        passed, pe_passed, wkv_turned, wkv_made, zcl = [ctx.enter_context(nc.semaphore("rw_" + x)) for x in ("waits_passed", "pe_waits_passed", "state_turned", "state_out_made", "zs_cleared")]
        wkv_st = ctx.enter_context(nc.semaphore("rw_wkv_stored"))
        NPAR = 17
        TILES = SEQ // P
        S_TILES = DEC_BATCH // 2

        ACT_STEPS = ["tanh", "xa", "sig", "a0", "a1", "g", "sg", "skk", "pall", "pinv", "tok", "X2", "X4", "T16", "T32",
                     "WU", "y0", "H", "std", "oT"]
        VEC_STEPS = ["zd", "zm", "zs", "kr0", "kr1", "sqk", "u", "lw", "mx", "rn", "kk", "t0", "t1", "kt", "bb", "R", "rk", "A", "B", "K",
                     "bonus", "X", "XT", "T1", "O32", "O64", "QB", "KM", "AM0", "MV", "X2T", "X4T", "T2", "X8", "T3", "T4", "P1", "T5", "P2", "T6", "R2", "G",
                     "St0", "Sa0", "S0", "St1", "Sa1", "S1",
                     "y", "mean", "yc", "yq", "var", "rstd", "yn", "yg", "yb", "bv", "yv", "out"]
        PE_STEPS = ["lora", "kn", "lp", "tok", "bonus", "L", "BT", "KT", "MV", "X2", "X2T", "X4", "X4T", "D1", "X8", "D2", "D3", "T16", "P1", "D4",
                    "T32", "P2", "D5", "WU", "R2", "Y0", "G", "H", "S0", "Y0s", "S1", "Y1s", "oT"]

        def plan(tag, sample):
            act_steps, pe_steps, vec_steps = list(ACT_STEPS), list(PE_STEPS), list(VEC_STEPS)
            if sample:
                for c in range(2):
                    pe_steps.insert(pe_steps.index(f"S{c}"), f"in{c}")
                    act_steps.insert(act_steps.index("std"), f"in{c}")
                    pe_steps.insert(pe_steps.index(f"Y{c}s") + 1, f"out{c}")
                    act_steps.insert(act_steps.index("std"), f"out{c}")
            return dict(
                sample=sample, valid=DEC_SEQ if sample else C,
                z=Steps(nc, ctx, f"rw_z_loaded{tag}", ["z"], 64 if sample else 32),
                o=Steps(nc, ctx, f"rw_o_stored{tag}", ["o"], 32 if sample else 16),
                s=Steps(nc, ctx, f"rw_state_loaded{tag}", ["s"], 64),
                so=[Steps(nc, ctx, f"rw_state_stored{tag}{c}", ["s"], 16) for c in range(2)],
                act=Steps(nc, ctx, f"rw_act{tag}", act_steps), pe=Steps(nc, ctx, f"rw_pe{tag}", pe_steps),
                vec=Steps(nc, ctx, f"rw_vec{tag}", vec_steps))

        main, samp = plan("", False), plan("s", True)
        for g in (main, samp):
            for k in ("z", "o", "s"):
                g[k].ahead = 0
        samp["so"] = [Steps(nc, ctx, f"rw_state_out{c}", ["s"], 32) for c in range(2)]
        for s in samp["so"]:
            s.ahead = 0

        setup = nc.Block()
        with setup:
            @setup.sync
            def _(sp):
                with nc.allow_non_contiguous_dma(reason="parameters by channel"):
                    loads = ((mu[:, :], t["mu_shift"].rearrange("(b p) -> p b", p=P)), (w0[:, :], t["w0"].partition_broadcast(P)),
                             (chp[:, 0, :], t["a0"].rearrange("(b p) -> p b", p=P)), (chp[:, 1, :], t["k_k"].rearrange("(b p) -> p b", p=P)),
                             (chp[:, 2, :], t["k_a"].rearrange("(b p) -> p b", p=P)), (ln_g[:, :], t["lnx_g"].partition_broadcast(P)),
                             (ln_b[:, :], t["lnx_b"].partition_broadcast(P)), (lora[0:32, :], t["w_lora"]), (lora[32:64, :], t["a_lora"]),
                             (lora[64:128, :], t["g_lora"]))
                    for dst, src in loads:
                        sp.dma_start(dst, src).then_inc(par, 16)
                    sp.wait_ge(const, 1)
                    for h in range(H):
                        sp.dma_start(rk_w[64 * (h % 2):64 * (h % 2) + 64, h // 2, h:h + 1], t["r_k"][h, :].unsqueeze(1)).then_inc(par, 16)
                    sp.dma_start(t["shift_p"].rearrange("o (b p) -> b p o", p=P), t["zT"][0:7, :, SEQ:SEQ + 1]).then_inc(shift_st, 16)
                    for b in range(7):
                        sp.dma_start(t["shift_s"][:, b * P:(b + 1) * P].rearrange("j p -> p j"),
                                     t["zT"][b, :, SEQ + 1:NT + 1].rearrange("p (j s) -> p j s", s=DEC_SEQ)[:, :, DEC_SEQ - 1]).then_inc(shift_st, 16)
                sp.wait_ge(par, 16 * (len(loads) + H))
                sp.wait_ge(shift_st, 16 * 8)

            @setup.gpsimd
            def _(pool):
                n = 0

                def own(op):
                    nonlocal n
                    n += 1
                    op.then_inc(const, 1)
                    pool.wait_ge(const, n)

                def select(m, pattern, base, mult, op=ALU.is_ge):
                    own(pool.affine_select(out=m, in_=m, compare_op=op, fill=0.0, base=base, pattern=pattern, channel_multiplier=mult))

                def same_block(m, size):
                    select(m, [[-size, P // size], [0, size]], 0, 1)
                    select(m, [[size, P // size], [0, size]], size - 1, -1)

                own(pool.memset(rk_w[:, :, :], 0.0))
                for m in (x16, x32, x64, x16T, headones):
                    own(pool.memset(m[:, :], 1.0))
                own(pool.memset(tri[:, :, :], 1.0))
                own(pool.memset(cmask[:, :], -float(np.exp(-0.5))))
                own(pool.memset(eps[:, :], EPS))
                own(pool.memset(zs[:, :, :, :], 0.0))
                own(pool.memset(ST[:, :, :], 0.0))
                for m, size in ((x16, 16), (x32, 32), (x64, 64)):
                    same_block(m[:, :], size)
                    select(m[:, :], [[-1, P]], 0, 1, ALU.is_gt)
                same_block(x16T[:, :], 16)
                select(x16T[:, :], [[1, P]], 0, -1, ALU.is_gt)
                same_block(headones[:, :], 64)
                for j in range(2):
                    same_block(tri[:, j, :], C)
                    select(tri[:, j, :], [[1, P]], 0, -1, ALU.is_gt if j else ALU.is_ge)
                own(pool.tensor_tensor(o32[:, :], x32[:, :], x16[:, :], ALU.subtract))
                own(pool.tensor_tensor(o64[:, :], x64[:, :], x32[:, :], ALU.subtract))
                own(pool.memset(cmask[:, 1:2], 0.0))
                for c in range(2):
                    own(pool.affine_select(out=sel8[:, c:c + 1], in_=cmask[:, 0:1], compare_op=ALU.is_ge, fill=0.0, base=-64 * c, pattern=[[0, 1]], channel_multiplier=1))
                    own(pool.affine_select(out=sel8[:, c:c + 1], in_=sel8[:, c:c + 1], compare_op=ALU.is_ge, fill=0.0, base=64 * c + DEC_SEQ - 1, pattern=[[0, 1]], channel_multiplier=-1))
                own(pool.tensor_tensor(cmask[:, 1:2], sel8[:, 0:1], sel8[:, 1:2], ALU.add))

        block = ctx.enter_context(nc.Block())

        @block.sync
        def _(sp):
            with sp.Fori(0, TILES) as i:
                at = sp.snap(i * P)
                wait_loop(sp, passed, *main["vec"].prev("zs", i))
                for c in range(2):
                    sp.dma_start(zin[:, c, :, :], t["zT"][0:7, :, bass.ds(at + c * C, C + 1)].rearrange("b p t -> p b t")).then_inc(main["z"].sem, 16)
            sp.wait_ge(*main["vec"].at("zs", TILES - 1))
            with nc.allow_non_contiguous_dma(reason="states by channel"), sp.Fori(0, S_TILES) as i:
                wait_loop(sp, passed, *samp["vec"].prev("zs", i))
                for c in range(2):
                    sp.dma_start(zin[:, c, :, 0], t["state_shift"][bass.ds(i * 2 + c, 1), :].rearrange("o (b p) -> p (o b)", p=P)).then_inc(samp["z"].sem, 16)
                    sp.dma_start(zin[:, c, :, 1:1 + DEC_SEQ], t["zT"][0:7, :, bass.ds(i * 16 + (1 + SEQ + c * DEC_SEQ), DEC_SEQ)].rearrange("b p t -> p b t")).then_inc(samp["z"].sem, 16)
                wait_loop(sp, passed, *samp["pe"].prev("in1", i))
                for c in range(2):
                    for hp in range(2):
                        sp.dma_start(S_in[64 * hp:64 * hp + 64, c, :, :],
                                     t["state_wkv"][bass.ds(i * 2 + c, 1), :, :, :].rearrange("o (b two) v k -> two v (o b) k", two=2)[hp]).then_inc(samp["s"].sem, 16)

        @block.gpsimd
        def _(pool):
            with pool.Fori(0, TILES) as i:
                pool.wait_ge(*main["act"].at("oT", i))
                pool.dma_start(t["oT"][0:2, :, bass.ds(i * P, P)].rearrange("b p t -> p b t"), oT_sb[:, :, :]).then_inc(main["o"].sem, 16)
            pool.wait_ge(wkv_made, 1)
            for hp in range(2):
                pool.dma_start(t["wkv_p"].rearrange("(b two) v k -> two v b k", two=2)[hp], S_out[64 * hp:64 * hp + 64, 0, :, :]).then_inc(wkv_st, 16)
            with pool.Fori(0, S_TILES) as i:
                for c in range(2):
                    pool.wait_ge(*samp["act"].at(f"out{c}", i))
                    for hp in range(2):
                        pool.dma_start(t["wkv_s"][bass.ds(i * 2 + c, 1), :, :, :].rearrange("o (b two) v k -> two v (o b) k", two=2)[hp],
                                       S_out[64 * hp:64 * hp + 64, c, :, :]).then_inc(samp["so"][c].sem, 16)
                pool.wait_ge(*samp["act"].at("oT", i))
                for c in range(2):
                    pool.dma_start(t["oT"][0:2, :, bass.ds(i * 16 + (SEQ + c * DEC_SEQ), DEC_SEQ)].rearrange("b p t -> p b t"),
                                   oT_sb[:, :, c * C:c * C + DEC_SEQ]).then_inc(samp["o"].sem, 16)
            pool.wait_ge(wkv_st, 32)
            pool.wait_ge(*main["o"].at("o", TILES - 1))
            pool.wait_ge(*samp["o"].at("o", S_TILES - 1))
            for c in range(2):
                pool.wait_ge(*samp["so"][c].at("s", S_TILES - 1))

        hb = lambda h: (64 * (h % 2), h // 2)

        def per_head(x, h):
            p0, b = hb(h)
            return x[p0:p0 + 64, b]

        @block.tensor
        def _(pe):
            for g in (main, samp):
                g["pe"].open(pe)

            def body(g, i):
                s = g["pe"]
                act = lambda name: pe.wait_ge(*g["act"].at(name, i))
                vec = lambda name: pe.wait_ge(*g["vec"].at(name, i))

                def each(name, k, make):
                    for h in range(H):
                        mm = make(heads(k)[:, h, :], h)
                    mm.then_inc(*s.step(name))

                def mul(out, lhsT, rhs, start=True, stop=True):
                    return pe.matmul(out, lhsT, rhs, start=start, stop=stop, skip_group_check=True)

                pe.wait_ge(*g["vec"].prev("out", i))
                pe.wait_ge(*g["act"].prev("oT", i))
                for name in ("tanh", "xa", "sig"):
                    act(name)
                mul(bank(0)[:, 0:256], low[0:32, :], lora[0:32, :])
                mul(bank(3)[:, 0:256], low[64:128, :], lora[64:128, :])
                for b in range(2):
                    mm = mul(bank(1)[:, b * P:(b + 1) * P], lora[32:64, b * P:(b + 1) * P], low[32:64, :])
                mm.then_inc(*s.step("lora"))
                vec("sqk")
                act("a1")
                mul(bank(1)[:, 256:512], headones[:, :], sqk[:, :, :].rearrange("p b t -> p (b t)")).then_inc(*s.step("kn"))
                vec("lw")
                for b in range(2):
                    mm = mul(bank(2)[:, b * 256:(b + 1) * 256], lw[:, b * P:(b + 1) * P], tri[:, :, :].rearrange("p j t -> p (j t)"))
                mm.then_inc(*s.step("lp"))
                for name in ("A", "B", "K"):
                    vec(name)
                for j, src in enumerate((lambda b: RA[:, b, 1, :], lambda b: Bc[:, b, :], lambda b: Kc[:, b, :],
                                         lambda b: zs[:, 4 + b, :, :].rearrange("p c t -> p (c t)"))):
                    for b in range(2):
                        mm = pe.transpose(bank(3 + j // 2)[:, (j % 2) * 256 + b * P:(j % 2) * 256 + (b + 1) * P], src(b), ident)
                mm.then_inc(*s.step("tok"))
                vec("rk")
                act("g")
                for b in range(2):
                    mm = mul(bank(0)[:, 0:H], rk[:, b, :], rk_w[:, b, :], b == 0, b == 1)
                mm.then_inc(*s.step("bonus"))
                for h in range(H):
                    mm = mul(bank(2 if h % 2 else 5)[:, (h // 2) * P:(h // 2 + 1) * P], RA[hb(h)[0]:hb(h)[0] + 64, hb(h)[1], 1, :], per_head(Bc, h))
                mm.then_inc(*s.step("L"))
                two = lambda k, h: bank(k + h % 2)[:, (h // 2) * 256:(h // 2) * 256 + 256]
                ra = lambda h: RA[hb(h)[0]:hb(h)[0] + 64, hb(h)[1], :, :].rearrange("p j t -> p (j t)")
                for h in range(H):
                    mm = mul(two(6, h), per_head(Bc, h), ra(h))
                mm.then_inc(*s.step("BT"))
                vec("bonus")
                vec("rn")
                for h in range(H):
                    mm = mul(two(0, h), per_head(Kc, h), ra(h))
                mm.then_inc(*s.step("KT"))
                vec("KM")
                act("tok")
                for h in range(H):
                    mm = mul(bank(3)[:, h * 64:h * 64 + 64], KM[:, h, 1, :], tok[:, 3, h * 64:(h + 1) * 64])
                mm.then_inc(*s.step("MV"))
                vec("O64")
                each("X2", 2, lambda out, h: mul(out, XT[:, h, :], X[:, h, :]))
                each("X2T", 5, lambda out, h: mul(out, X[:, h, :], XT[:, h, :]))
                act("X2")
                vec("X2T")
                each("X4", 6, lambda out, h: mul(out, X2T[:, h, :], X2[:, h, :]))
                each("X4T", 7, lambda out, h: mul(out, X2[:, h, :], X2T[:, h, :]))
                each("D1", 0, lambda out, h: mul(out, X2[:, h, :], T[0][:, h, :]))
                act("X4")
                vec("X4T")
                each("X8", 1, lambda out, h: mul(out, XT[:, h, :], X[:, h, :]))
                vec("T2")
                each("D2", 2, lambda out, h: mul(out, X[:, h, :], T[1][:, h, :]))
                vec("X8")
                vec("T3")
                each("D3", 5, lambda out, h: mul(out, X2[:, h, :], T[0][:, h, :]))
                vec("T4")
                each("T16", 6, lambda out, h: pe.transpose(out, T[1][:, h, :], ident))
                each("P1", 7, lambda out, h: mul(out, O32[:, h, :], T[1][:, h, :]))
                act("T16")
                vec("P1")
                each("D4", 0, lambda out, h: mul(out, X[:, h, :], XT[:, h, :]))
                vec("T5")
                each("T32", 1, lambda out, h: pe.transpose(out, T[0][:, h, :], ident))
                each("P2", 2, lambda out, h: mul(out, O64[:, h, :], T[0][:, h, :]))
                act("T32")
                vec("P2")
                each("D5", 5, lambda out, h: mul(out, X2[:, h, :], X2T[:, h, :]))
                vec("T6")
                vec("MV")
                each("WU", 6, lambda out, h: mul(out, T[1][:, h, :], AM[:, h, :]))
                act("WU")
                for h in range(H):
                    p0, b = hb(h)
                    mm = mul(bank(7)[p0:p0 + 64, b * P:(b + 1) * P], WU[:, h, 0:64], QB[:, h, :])
                mm.then_inc(*s.step("R2"))
                for h in range(H):
                    out = bank(0)[:, h * 64:(h + 1) * 64]
                    mul(out, QB[:, h, :], WU[:, h, 64:128], True, False)
                    mm = mul(out, KM[:, h, 0, :], tok[:, 3, h * 64:(h + 1) * 64], False, True)
                mm.then_inc(*s.step("Y0"))
                for h in range(H):
                    p0, b = hb(h)
                    for c in range(2):
                        r = slice(64 * c, 64 * c + 64)
                        mm = mul(bank(1 + c)[p0:p0 + 64, b * 64:b * 64 + 64], WU[r, h, 0:64], tok[r, 1, h * 64:(h + 1) * 64])
                mm.then_inc(*s.step("G"))
                for h in range(H):
                    p0, b = hb(h)
                    for c in range(2):
                        r = slice(64 * c, 64 * c + 64)
                        out = bank(3 + c)[p0:p0 + 64, b * 64:b * 64 + 64]
                        mul(out, tok[r, 1, h * 64:(h + 1) * 64], WU[r, h, 64:128], True, False)
                        mm = mul(out, tok[r, 2, h * 64:(h + 1) * 64], tok[r, 3, h * 64:(h + 1) * 64], False, True)
                mm.then_inc(*s.step("H"))
                vec("G")
                vec("R2")
                act("H")
                if not g["sample"]:
                    pe.wait_ge(*g["vec"].prev("S1", i))
                for c in range(2):
                    if g["sample"]:
                        pe.wait_ge(*g["s"].at("s", i))
                        if c == 1:
                            act("in0")
                        pe.sem_inc(pe_passed, 1)
                        for h in range(H):
                            p0, b = hb(h)
                            mm = mul(bank(4)[p0:p0 + 64, b * 64:(b + 1) * 64], S_in[p0:p0 + 64, c, b, :], ident[p0:p0 + 64, p0:p0 + 64])
                        mm.then_inc(*s.step(f"in{c}"))
                        act(f"in{c}")
                    elif c == 1:
                        vec("S0")
                    pe.sem_inc(pe_passed, 1)
                    for h in range(H):
                        p0, b = hb(h)
                        mm = mul(bank(2)[p0:p0 + 64, (c * 2 + b) * 64:(c * 2 + b) * 64 + 64], per_head(GT, h)[:, c, :], per_head(ST, h))
                    mm.then_inc(*s.step(f"S{c}"))
                    for h in range(H):
                        p0, b = hb(h)
                        mm = mul(bank(5 + h % 2)[64 * c:64 * c + 64, b * 64:(b + 1) * 64], R2[p0:p0 + 64, b, 64 * c:64 * c + 64], per_head(ST, h))
                    mm.then_inc(*s.step(f"Y{c}s"))
                    if g["sample"]:
                        vec(f"S{c}")
                        pe.sem_inc(pe_passed, 1)
                        for h in range(H):
                            p0, b = hb(h)
                            mm = mul(bank(4)[p0:p0 + 64, 256 + b * 64:256 + (b + 1) * 64], per_head(ST, h), ident[p0:p0 + 64, p0:p0 + 64])
                        mm.then_inc(*s.step(f"out{c}"))
                        act(f"out{c}")
                vec("out")
                for b in range(2):
                    mm = pe.transpose(bank(3)[:, b * P:(b + 1) * P], y[:, 2 * b:2 * b + 2, :].rearrange("p h v -> p (h v)"), ident)
                mm.then_inc(*s.step("oT"))

            with pe.Fori(0, TILES) as i:
                body(main, i)
            pe.wait_ge(*main["vec"].at("S1", TILES - 1))
            for h in range(H):
                p0, b = hb(h)
                mm = pe.matmul(bank(4)[p0:p0 + 64, b * 64:(b + 1) * 64], per_head(ST, h), ident[p0:p0 + 64, p0:p0 + 64], start=True, stop=True, skip_group_check=True)
            mm.then_inc(wkv_turned, 1)
            pe.wait_ge(wkv_made, 1)
            pe.wait_ge(*main["vec"].at("out", TILES - 1))
            pe.wait_ge(*main["act"].at("oT", TILES - 1))
            with pe.Fori(0, S_TILES) as i:
                body(samp, i)

        @block.scalar
        def _(act):
            for g in (main, samp):
                g["act"].open(act)

            def body(g, i):
                s = g["act"]
                pe = lambda name: act.wait_ge(*g["pe"].at(name, i))
                vec = lambda name: act.wait_ge(*g["vec"].at(name, i))

                def run(name, out, src, func=ACT.Copy, **k):
                    act.activation(out, src, func, **k).then_inc(*s.step(name))

                vec("zs")
                act.wait_ge(*g["pe"].prev("lora", i))
                x6 = zs[:, 6, :, :].rearrange("p c t -> p (c t)")
                run("tanh", low[0:32, :], x6[0:32, :], ACT.Tanh)
                run("xa", low[32:64, :], x6[32:64, :])
                run("sig", low[64:128, :], x6[64:128, :], ACT.Sigmoid)
                pe("lora")
                act.wait_ge(*g["vec"].prev("yv", i))
                for b in range(2):
                    run(f"a{b}", a_sb[:, b, :], bank(1)[:, b * P:(b + 1) * P], ACT.Sigmoid, bias=chp[:, 0, b:b + 1])
                act.wait_ge(*g["vec"].prev("out", i))
                vec("u")
                run("g", g_sb[:, :], bank(3)[:, 0:256])
                run("sg", u[:, :], u[:, :], ACT.Sigmoid)
                pe("kn")
                run("skk", rn[:, :, :].rearrange("p b t -> p (b t)"), bank(1)[:, 256:512], ACT.Sqrt)
                pe("lp")
                run("pall", pall[:, :, :, :].rearrange("p b j t -> p (b j t)"), bank(2), ACT.Exp)
                run("pinv", pinv[:, :, :], bank(2).rearrange("p (b j t) -> p b j t", b=2, j=2)[:, :, 0, :], ACT.Exp, scale=-1.0)
                pe("tok")
                act.activation(tok[:, 0:2, :].rearrange("p a b -> p (a b)"), bank(3), ACT.Copy)
                run("tok", tok[:, 2:4, :].rearrange("p a b -> p (a b)"), bank(4))
                pe("X2")
                run("X2", X2[:, :, :], heads(2))
                pe("X4")
                run("X4", X[:, :, :], heads(6))
                pe("T16")
                pe("X8")
                run("T16", X[:, :, :], heads(6))
                pe("T32")
                pe("D3")
                run("T32", X2[:, :, :], heads(1))
                pe("WU")
                run("WU", WU[:, :, :], heads(6))
                pe("Y0")
                run("y0", y0[:, :, :], bank(0)[:, 0:256].rearrange("p (h v) -> p h v", h=H))
                pe("H")
                act.activation(Hs[:, :, 0, :], bank(3)[:, 0:128].rearrange("p (b v) -> p b v", b=2), ACT.Copy)
                run("H", Hs[:, :, 1, :], bank(4)[:, 0:128].rearrange("p (b v) -> p b v", b=2))
                if g["sample"]:
                    for c in range(2):
                        pe(f"in{c}")
                        run(f"in{c}", ST[:, :, :], bank(4)[:, 0:128].rearrange("p (b v) -> p b v", b=2))
                        pe(f"out{c}")
                        act.wait_ge(*g["so"][c].prev("s", i))
                        run(f"out{c}", S_out[:, c, :, :], bank(4)[:, 256:384].rearrange("p (b v) -> p b v", b=2))
                vec("var")
                run("std", var[:, :], var[:, :], ACT.Sqrt, scale=1.0 / C, bias=eps[:, :])
                pe("oT")
                act.wait_ge(*g["o"].prev("o", i))
                run("oT", oT_sb[:, :, :], bank(3)[:, 0:256].rearrange("p (b t) -> p b t", b=2))

            with act.Fori(0, TILES) as i:
                body(main, i)
            act.wait_ge(wkv_turned, 1)
            act.activation(S_out[:, 0, :, :], bank(4)[:, 0:128].rearrange("p (b v) -> p b v", b=2), ACT.Copy).then_inc(wkv_made, 1)
            act.wait_ge(wkv_st, 32)
            act.wait_ge(*main["o"].at("o", TILES - 1))
            with act.Fori(0, S_TILES) as i:
                body(samp, i)

        @block.vector
        def _(dve):
            for g in (main, samp):
                g["vec"].open(dve)

            def body(g, i):
                s = g["vec"]
                pe = lambda name: dve.wait_ge(*g["pe"].at(name, i))
                act = lambda name: dve.wait_ge(*g["act"].at(name, i))

                def after(name):
                    dve.wait_ge(*s.at(name, i))

                def tt(name, out, a, b, op):
                    dve.tensor_tensor(out, a, b, op).then_inc(*s.step(name))

                n = g["valid"]
                flat = lambda x: x.rearrange("p b t -> p (b t)")
                over = lambda m: m.unsqueeze(1).to_broadcast([P, H, P])
                cur = zin[:, :, :, 1:1 + n].rearrange("p c b t -> p b c t")
                before = zin[:, :, :, 0:n].rearrange("p c b t -> p b c t")
                dve.wait_ge(*g["z"].at("z", i))
                dve.wait_ge(*g["pe"].prev("tok", i))
                dve.wait_ge(*g["act"].prev("sig", i))
                for c in range(2):
                    op = dve.tensor_tensor(zd[:, :, c, 0:n], before[:, :, c, :], cur[:, :, c, :], ALU.subtract)
                op.then_inc(*s.step("zd"))
                after("zd")
                for c in range(2):
                    op = dve.tensor_tensor(zd[:, :, c, 0:n], zd[:, :, c, 0:n], mu[:, :].unsqueeze(2).to_broadcast([P, 7, n]), ALU.mult)
                op.then_inc(*s.step("zm"))
                after("zm")
                for c in range(2):
                    op = dve.tensor_tensor(zs[:, :, c, 0:n], zd[:, :, c, 0:n], cur[:, :, c, :], ALU.add)
                op.then_inc(*s.step("zs"))
                after("zs")
                zb = lambda b: zs[:, b, :, :].rearrange("p c t -> p (c t)")
                z2 = lambda b: zs[:, b:b + 2, :, :].rearrange("p b c t -> p (b c t)")
                for b in range(2):
                    dve.tensor_scalar(kraw[:, b, :], zb(2 + b), chp[:, 1, b:b + 1], None, ALU.mult).then_inc(*s.step(f"kr{b}"))
                after("kr1")
                dve.wait_ge(*g["pe"].prev("kn", i))
                tt("sqk", sqk[:, :, :], kraw[:, :, :], kraw[:, :, :], ALU.mult)
                pe("lora")
                tt("u", u[:, :], bank(0)[:, 0:256], w0[:, :], ALU.add)
                act("sg")
                dve.wait_ge(*g["pe"].prev("lp", i))
                dve.tensor_scalar(lw[:, :], u[:, :], cmask[:, 1:2] if g["sample"] else cmask[:, 0:1], None, ALU.mult).then_inc(*s.step("lw"))
                act("skk")
                dve.tensor_scalar(rn[:, :, :], rn[:, :, :], 1e-12, None, ALU.max).then_inc(*s.step("mx"))
                after("mx")
                dve.reciprocal(rn[:, :, :], rn[:, :, :]).then_inc(*s.step("rn"))
                after("rn")
                tt("kk", kk[:, :, :], kraw[:, :, :], rn[:, :, :], ALU.mult)
                act("a1")
                for b in range(2):
                    dve.tensor_scalar(kt[:, b, :], a_sb[:, b, :], 1.0, chp[:, 2, b:b + 1], ALU.subtract, ALU.mult).then_inc(*s.step(f"t{b}"))
                after("t1")
                dve.scalar_tensor_tensor(out=flat(kt[:, :, :]), in0=flat(kt[:, :, :]), scalar=1.0, in1=z2(2), op0=ALU.add, op1=ALU.mult).then_inc(*s.step("kt"))
                after("kk")
                tt("bb", a_sb[:, :, :], a_sb[:, :, :], kk[:, :, :], ALU.mult)
                act("pinv")
                after("kt")
                tt("R", RA[:, :, 0, :], zs[:, 0:2, :, :].rearrange("p b c t -> p b (c t)"), pall[:, :, 0, :], ALU.mult)
                tt("rk", flat(rk[:, :, :]), z2(0), flat(kt[:, :, :]), ALU.mult)
                dve.scalar_tensor_tensor(out=RA[:, :, 1, :], in0=kk[:, :, :], scalar=-1.0, in1=pall[:, :, 1, :], op0=ALU.mult, op1=ALU.mult).then_inc(*s.step("A"))
                after("bb")
                tt("B", Bc[:, :, :], a_sb[:, :, :], pinv[:, :, :], ALU.mult)
                tt("K", Kc[:, :, :], kt[:, :, :], pinv[:, :, :], ALU.mult)
                pe("bonus")
                dve.tensor_copy(bonus[:, :], bank(0)[:, 0:H]).then_inc(*s.step("bonus"))
                pe("L")
                parity = lambda x, q: x.rearrange("p (b two) t -> p b two t", two=2)[:, :, q, :]
                over2 = lambda m: m.unsqueeze(1).to_broadcast([P, 2, P])

                def lower(name, out, m):
                    for q in range(2):
                        op = dve.tensor_tensor(parity(out[:, :, :], q), bank(2 if q else 5)[:, 0:256].rearrange("p (b t) -> p b t", b=2), over2(m[:, :]), ALU.mult)
                    op.then_inc(*s.step(name))

                lower("X", X, x16)
                pe("BT")
                bt = lambda k, j: pb[k][:, :].rearrange("p (h j t) -> p h j t", h=2, j=2)[:, :, j, :]
                for q in range(2):
                    op = dve.tensor_tensor(parity(XT[:, :, :], q), bt(6 + q, 1), over2(x16T[:, :]), ALU.mult)
                op.then_inc(*s.step("XT"))
                after("XT")
                tt("T1", T[0][:, :, :], XT[:, :, :], over(ident), ALU.add)
                lower("O32", O32, o32)
                lower("O64", O64, o64)
                for q in range(2):
                    op = dve.tensor_tensor(parity(QB[:, :, :], q), bt(6 + q, 0), over2(tri[:, 0, :]), ALU.mult)
                op.then_inc(*s.step("QB"))
                pe("KT")
                for k in range(2):
                    op = dve.tensor_tensor(KM[:, :, :, :].rearrange("p (b two) j t -> p b two (j t)", two=2)[:, :, k, :], pb[k][:, :].rearrange("p (h x) -> p h x", h=2),
                                           tri[:, :, :].rearrange("p j t -> p (j t)").unsqueeze(1).to_broadcast([P, 2, 256]), ALU.mult)
                op.then_inc(*s.step("KM"))
                act("tok")
                dve.tensor_copy(AM[:, :, 0:64], tok[:, 0, :].rearrange("p (h k) -> p h k", h=H)).then_inc(*s.step("AM0"))
                pe("MV")
                dve.tensor_copy(AM[:, :, 64:128], bank(3)[:, 0:256].rearrange("p (h k) -> p h k", h=H)).then_inc(*s.step("MV"))
                pe("X2T")
                dve.tensor_copy(X2T[:, :, :], heads(5)).then_inc(*s.step("X2T"))
                pe("X4T")
                dve.tensor_copy(XT[:, :, :], heads(7)).then_inc(*s.step("X4T"))
                pe("D1")
                tt("T2", T[1][:, :, :], heads(0), T[0][:, :, :], ALU.add)
                pe("X8")
                dve.tensor_copy(X2[:, :, :], heads(1)).then_inc(*s.step("X8"))
                pe("D2")
                after("T2")
                tt("T3", T[0][:, :, :], heads(2), T[1][:, :, :], ALU.add)
                pe("D3")
                after("T3")
                tt("T4", T[1][:, :, :], heads(5), T[0][:, :, :], ALU.add)
                pe("P1")
                dve.tensor_copy(XT[:, :, :], heads(7)).then_inc(*s.step("P1"))
                pe("D4")
                after("T4")
                tt("T5", T[0][:, :, :], heads(0), T[1][:, :, :], ALU.add)
                pe("P2")
                dve.tensor_copy(X2T[:, :, :], heads(2)).then_inc(*s.step("P2"))
                pe("D5")
                after("T5")
                tt("T6", T[1][:, :, :], heads(5), T[0][:, :, :], ALU.add)
                pe("R2")
                tt("R2", R2[:, :, :], bank(7)[:, 0:256].rearrange("p (b t) -> p b t", b=2), RA[:, :, 0, :], ALU.add)
                pe("G")
                for c in range(2):
                    op = dve.tensor_copy(GT[:, :, c, :], bank(1 + c)[:, 0:128].rearrange("p (b v) -> p b v", b=2))
                op.then_inc(*s.step("G"))
                act("H")
                for c in range(2):
                    if g["sample"]:
                        act(f"in{c}")
                    elif c:
                        after("S0")
                    else:
                        dve.wait_ge(*s.prev("S1", i))
                    tt(f"St{c}", St[:, :, :], ST[:, :, :], Hs[:, :, c, :], ALU.add)
                    pe(f"S{c}")
                    after(f"St{c}")
                    tt(f"Sa{c}", St[:, :, :], bank(2)[:, c * 128:(c + 1) * 128].rearrange("p (b v) -> p b v", b=2), St[:, :, :], ALU.add)
                    after(f"Sa{c}")
                    pe(f"Y{c}s")
                    tt(f"S{c}", ST[:, :, :], St[:, :, :], pall[:, :, 0, 64 * c + 63:64 * c + 64].to_broadcast([P, 2, 64]), ALU.mult)
                act("y0")
                dve.wait_ge(*g["pe"].prev("oT", i))
                for q in range(2):
                    op = dve.tensor_tensor(parity(y[:, :, :], q), bank(5 + q)[:, 0:128].rearrange("p (b v) -> p b v", b=2), parity(y0[:, :, :], q), ALU.add)
                op.then_inc(*s.step("y"))
                after("y")
                dve.tensor_reduce(mean[:, :], y[:, :, :], AX.X, ALU.add).then_inc(*s.step("mean"))
                after("mean")
                dve.scalar_tensor_tensor(out=y[:, :, :], in0=mean[:, :].unsqueeze(2).to_broadcast([P, H, C]), scalar=-1.0 / C, in1=y[:, :, :],
                                         op0=ALU.mult, op1=ALU.add).then_inc(*s.step("yc"))
                after("yc")
                tt("yq", yq[:, :, :], y[:, :, :], y[:, :, :], ALU.mult)
                after("yq")
                dve.tensor_reduce(var[:, :], yq[:, :, :], AX.X, ALU.add).then_inc(*s.step("var"))
                act("std")
                dve.reciprocal(var[:, :], var[:, :]).then_inc(*s.step("rstd"))
                after("rstd")
                fl = lambda x: x.rearrange("p h v -> p (h v)")
                tt("yn", y[:, :, :], y[:, :, :], var[:, :].unsqueeze(2).to_broadcast([P, H, C]), ALU.mult)
                after("yn")
                tt("yg", fl(y[:, :, :]), fl(y[:, :, :]), ln_g[:, :], ALU.mult)
                after("yg")
                tt("yb", fl(y[:, :, :]), fl(y[:, :, :]), ln_b[:, :], ALU.add)
                tt("bv", yq[:, :, :], tok[:, 3, :].rearrange("p (h v) -> p h v", h=H), bonus[:, :].unsqueeze(2).to_broadcast([P, H, C]), ALU.mult)
                after("bv")
                tt("yv", y[:, :, :], y[:, :, :], yq[:, :, :], ALU.add)
                after("yv")
                act("g")
                tt("out", fl(y[:, :, :]), fl(y[:, :, :]), g_sb[:, :], ALU.mult)

            with dve.Fori(0, TILES) as i:
                body(main, i)
            dve.wait_ge(*main["pe"].at("oT", TILES - 1))
            dve.memset(zs[:, :, :, :], 0.0).then_inc(zcl, 1)
            dve.wait_ge(zcl, 1)
            with dve.Fori(0, S_TILES) as i:
                body(samp, i)


def conv_mix(nc, ident, t):
    with ExitStack() as ctx:
        def sb(name, shape):
            return ctx.enter_context(nc.sbuf_tensor("cv_" + name, shape, F32))

        CW, CB = 31, 2
        PAD = CW - 1
        ROWS = DEC_BATCH // 2 * PAD
        z = sb("z", [P, 2 * CB, NT])
        up = sb("up", [P, CB, PAD + SEQ])
        us = sb("us", [P, CB, DEC_BATCH, PAD + DEC_SEQ])
        c_sb = sb("c", [P, CB, NT])
        sq = sb("sq", [P, CB, 512])
        rs = sb("rs", [P, 2, 512])
        w = sb("w", [P, CB, CW])
        par = sb("par", [P, 3, CB])
        tails = sb("tails", [P, 2, CB, ROWS])
        st_in = sb("st_in", [ROWS, 2, CB * P])
        st_out = sb("st_out", [ROWS, 3, CB * P])
        mean_w = sb("mean_w", [P, P])
        eps = sb("eps", [P, 1])
        ps_t = ctx.enter_context(nc.psum_tensor("cv_pst", [P, 2, 512], F32))
        ps_m = ctx.enter_context(nc.psum_tensor("cv_psm", [P, 2, 512], F32))
        ps_v = ctx.enter_context(nc.psum_tensor("cv_psv", [P, 2, 512], F32))
        z_ld = [ctx.enter_context(nc.semaphore(f"cv_z_loaded{b}")) for b in range(CB)]
        par_ld = ctx.enter_context(nc.semaphore("cv_parameters_loaded"))
        st_ld = ctx.enter_context(nc.semaphore("cv_state_loaded"))
        const = ctx.enter_context(nc.semaphore("cv_constants"))
        stored = ctx.enter_context(nc.semaphore("cv_stored"))
        groups = [(g * 512, 512) for g in range(4)] + [(SEQ, TS)]

        pe_s = Steps(nc, ctx, "cv_pe", ["in0", "in1", "out0", "out1", "out2"] + [f"{k}{g}" for g in range(5) for k in ("m", "v")])
        act_s = Steps(nc, ctx, "cv_act", [f"sig{b}" for b in range(CB)] + ["in0", "in1"] + ["out0", "out1", "out2"] + [x for g in range(5) for x in (f"std{g}", f"s{g}0", f"s{g}1")])
        taps = [(b, j) for b in range(CB) for j in range(CW)]
        vec_s = Steps(nc, ctx, "cv_vec", [f"u{b}" for b in range(CB)] + ["tails"] + [f"c{b}_{j}" for b, j in taps]
                      + [x for g in range(5) for x in (f"cc{g}", f"sq{g}", f"rs{g}", f"yn{g}")])
        for s in (pe_s, act_s, vec_s):
            s.ahead = 0
        block = ctx.enter_context(nc.Block())

        @block.sync
        def _(sp):
            with nc.allow_non_contiguous_dma(reason="parameters by channel"):
                for b in range(CB):
                    sp.dma_start(w[:, b, :], t["conv_w"][:, b * P:(b + 1) * P].rearrange("w p -> p w")).then_inc(par_ld, 16)
                for j, name in enumerate(("conv_b", "conv_ln_g", "conv_ln_b")):
                    sp.dma_start(par[:, j, :], t[name].rearrange("(b p) -> p b", p=P)).then_inc(par_ld, 16)
            for b in range(CB):
                for j in range(2):
                    sp.dma_start(z[:, j * CB + b, :], t["zT"][7 + j * CB + b, :, 1:NT + 1]).then_inc(z_ld[b], 16)
            for j in range(2):
                sp.dma_start(st_in[:, j, :], t["state_conv"][4 * j:4 * j + 4, :, :].rearrange("b w c -> (b w) c")).then_inc(st_ld, 16)
            for g, (at, n) in enumerate(groups):
                sp.wait_ge(*act_s.at(f"s{g}1", 0))
                sp.dma_start(t["oT"][2:4, :, at:at + n].rearrange("b p t -> p b t"), c_sb[:, :, at:at + n]).then_inc(stored, 16)
            sp.wait_ge(*act_s.at("out2", 0))
            for j in range(2):
                sp.dma_start(t["conv_s"][4 * j:4 * j + 4, :, :].rearrange("b w c -> (b w) c"), st_out[:, j, :]).then_inc(stored, 16)
            sp.dma_start(t["conv_p"], st_out[0:PAD, 2, :]).then_inc(stored, 16)
            sp.wait_ge(stored, 16 * (len(groups) + 3))

        @block.gpsimd
        def _(pool):
            pool.memset(up[:, :, 0:PAD], 0.0).then_inc(const, 1)
            pool.memset(mean_w[:, :], 1.0 / (CB * P)).then_inc(const, 1)
            pool.memset(eps[:, :], 1e-5).then_inc(const, 1)

        @block.tensor
        def _(pe):
            pe.wait_ge(st_ld, 32)
            for j in range(2):
                for b in range(CB):
                    mm = pe.transpose(ps_t[:, j, b * P:b * P + ROWS], st_in[:, j, b * P:(b + 1) * P], ident[0:ROWS, 0:ROWS])
                mm.then_inc(*pe_s.step(f"in{j}"))
            pe.wait_ge(*act_s.at("in1", 0))
            pe.wait_ge(*vec_s.at("tails", 0))
            for j in range(3):
                if j == 2:
                    pe.wait_ge(*act_s.at("out0", 0))
                for b in range(CB):
                    src, n = (tails[:, j, b, :], ROWS) if j < 2 else (up[:, b, SEQ:SEQ + PAD], PAD)
                    mm = pe.transpose(ps_t[0:n, j % 2, b * P:(b + 1) * P], src, ident)
                mm.then_inc(*pe_s.step(f"out{j}"))
            pe.wait_ge(const, 3)
            pe.wait_ge(*vec_s.at(f"c1_{CW - 1}", 0))
            for g, (at, n) in enumerate(groups):
                if g >= 2:
                    pe.wait_ge(*vec_s.at(f"cc{g - 2}", 0))
                for b in range(CB):
                    mm = pe.matmul(ps_m[:, g % 2, 0:n], mean_w[:, :], c_sb[:, b, at:at + n], start=b == 0, stop=b == CB - 1)
                mm.then_inc(*pe_s.step(f"m{g}"))
                pe.wait_ge(*vec_s.at(f"sq{g}", 0))
                if g >= 2:
                    pe.wait_ge(*act_s.at(f"std{g - 2}", 0))
                for b in range(CB):
                    mm = pe.matmul(ps_v[:, g % 2, 0:n], mean_w[:, :], sq[:, b, 0:n], start=b == 0, stop=b == CB - 1)
                mm.then_inc(*pe_s.step(f"v{g}"))

        @block.scalar
        def _(act):
            for b in range(CB):
                act.wait_ge(z_ld[b], 32)
                act.activation(z[:, CB + b, :], z[:, CB + b, :], ACT.Sigmoid).then_inc(*act_s.step(f"sig{b}"))
            for j in range(2):
                act.wait_ge(*pe_s.at(f"in{j}", 0))
                act.activation(us[:, :, 4 * j:4 * j + 4, 0:PAD].rearrange("p b s w -> p b s w"),
                               ps_t[:, j, 0:CB * P].rearrange("p (b x) -> p b x", b=CB)[:, :, 0:ROWS].rearrange("p b (s w) -> p b s w", w=PAD),
                               ACT.Copy).then_inc(*act_s.step(f"in{j}"))
            for j in range(3):
                n = ROWS if j < 2 else PAD
                act.wait_ge(*pe_s.at(f"out{j}", 0))
                act.activation(st_out[0:n, j, :], ps_t[0:n, j % 2, 0:CB * P], ACT.Copy).then_inc(*act_s.step(f"out{j}"))
            act.wait_ge(const, 3)
            act.wait_ge(par_ld, 16 * 5)
            for g, (at, n) in enumerate(groups):
                act.wait_ge(*pe_s.at(f"v{g}", 0))
                if g >= 2:
                    act.wait_ge(*vec_s.at(f"yn{g - 2}", 0))
                act.activation(rs[:, g % 2, 0:n], ps_v[:, g % 2, 0:n], ACT.Sqrt, bias=eps[:, :]).then_inc(*act_s.step(f"std{g}"))
                act.wait_ge(*vec_s.at(f"yn{g}", 0))
                for b in range(CB):
                    act.activation(c_sb[:, b, at:at + n], c_sb[:, b, at:at + n], ACT.Silu, scale=par[:, 1, b:b + 1], bias=par[:, 2, b:b + 1]).then_inc(*act_s.step(f"s{g}{b}"))

        @block.vector
        def _(dve):
            dve.wait_ge(const, 3)
            dve.wait_ge(par_ld, 16 * 5)
            for b in range(CB):
                dve.wait_ge(*act_s.at(f"sig{b}", 0))
                dve.tensor_tensor(us[:, b, :, PAD:], z[:, b, SEQ:NT].rearrange("p (s t) -> p s t", t=DEC_SEQ), z[:, CB + b, SEQ:NT].rearrange("p (s t) -> p s t", t=DEC_SEQ), ALU.mult)
                dve.tensor_tensor(up[:, b, PAD:], z[:, b, 0:SEQ], z[:, CB + b, 0:SEQ], ALU.mult).then_inc(*vec_s.step(f"u{b}"))
            dve.wait_ge(*act_s.at("in1", 0))
            dve.wait_ge(*vec_s.at("u1", 0))
            for j in range(2):
                for b in range(CB):
                    op = dve.tensor_copy(tails[:, j, b, :].rearrange("p (s w) -> p s w", w=PAD), us[:, b, 4 * j:4 * j + 4, DEC_SEQ:DEC_SEQ + PAD])
            op.then_inc(*vec_s.step("tails"))
            for b, j in taps:
                if j:
                    dve.wait_ge(*vec_s.at(f"c{b}_{j - 1}", 0))
                for out, src in ((c_sb[:, b, SEQ:NT].rearrange("p (s t) -> p s t", t=DEC_SEQ), us[:, b, :, j:j + DEC_SEQ]), (c_sb[:, b, 0:SEQ], up[:, b, j:j + SEQ])):
                    if j == 0:
                        op = dve.tensor_scalar(out, src, w[:, b, 0:1], par[:, 0, b:b + 1], ALU.mult, ALU.add)
                    else:
                        op = dve.scalar_tensor_tensor(out=out, in0=src, scalar=w[:, b, j:j + 1], in1=out, op0=ALU.mult, op1=ALU.add)
                op.then_inc(*vec_s.step(f"c{b}_{j}"))
            for g, (at, n) in enumerate(groups):
                both = lambda x: x.unsqueeze(1).to_broadcast([P, CB, n])
                c = c_sb[:, :, at:at + n]
                dve.wait_ge(*pe_s.at(f"m{g}", 0))
                dve.tensor_tensor(c, c, both(ps_m[:, g % 2, 0:n]), ALU.subtract).then_inc(*vec_s.step(f"cc{g}"))
                dve.wait_ge(*vec_s.at(f"cc{g}", 0))
                if g:
                    dve.wait_ge(*pe_s.at(f"v{g - 1}", 0))
                dve.tensor_tensor(sq[:, :, 0:n], c, c, ALU.mult).then_inc(*vec_s.step(f"sq{g}"))
                dve.wait_ge(*act_s.at(f"std{g}", 0))
                dve.reciprocal(rs[:, g % 2, 0:n], rs[:, g % 2, 0:n]).then_inc(*vec_s.step(f"rs{g}"))
                dve.wait_ge(*vec_s.at(f"rs{g}", 0))
                dve.tensor_tensor(c, c, both(rs[:, g % 2, 0:n]), ALU.mult).then_inc(*vec_s.step(f"yn{g}"))


def bias_rows():
    dist = 255 - np.arange(BIAS_W)
    far = np.maximum(dist, 16).astype(np.float32)
    large = 16 + (np.log(far / np.float32(16)) / np.float32(np.log(8.0)) * np.float32(16)).astype(np.int32)
    bucket = np.where(dist < 16, np.maximum(dist, 0), np.minimum(large, N_BUCKETS - 1))
    row = np.arange(N_BUCKETS)[:, None]
    return (row == bucket).astype(np.float32) - (row == N_BUCKETS - 1).astype(np.float32)


def bias_table(nc, t):
    with ExitStack() as ctx:
        rel = ctx.enter_context(nc.sbuf_tensor("bt_rel", [N_BUCKETS, 8], F32))
        rows = ctx.enter_context(nc.sbuf_tensor("bt_rows", [N_BUCKETS, BIAS_W], F32))
        out = ctx.enter_context(nc.sbuf_tensor("bt_out", [8, BIAS_W], F32))
        ps = ctx.enter_context(nc.psum_tensor("bt_ps", [8, BIAS_W], F32))
        ld, mm, cp, st = [ctx.enter_context(nc.semaphore("bt_" + x)) for x in ("loaded", "multiplied", "copied", "stored")]
        block = ctx.enter_context(nc.Block())

        @block.sync
        def _(sp):
            sp.dma_start(rel[:, :], t["rel_bias"]).then_inc(ld, 16)
            sp.dma_start(rows[:, :], t["bias_rows"]).then_inc(ld, 16)
            sp.wait_ge(cp, 1)
            sp.dma_start(t["bias"], out[:, :].unsqueeze(1).to_broadcast([8, P, BIAS_W])).then_inc(st, 16)
            sp.wait_ge(st, 16)

        @block.tensor
        def _(pe):
            pe.wait_ge(ld, 32)
            pe.matmul(ps[:, :], rel[:, :], rows[:, :], start=True, stop=True).then_inc(mm, 1)

        @block.vector
        def _(dve):
            dve.wait_ge(mm, 1)
            dve.tensor_copy(out[:, :], ps[:, :]).then_inc(cp, 1)


def attention_prompt(nc, ident, t):
    with ExitStack() as ctx:
        def sb(name, shape):
            return ctx.enter_context(nc.sbuf_tensor("ap_" + name, shape, F32))

        QT = SEQ // P
        NH, D = 8, 64
        ROUNDS = 256 // 8
        OUT, GONE, LEAST = -1e30, -3e38, -3.4e38
        z = sb("z", [P, 2, N_ATT])
        gain = sb("gain", [P, 11, D])
        causal = sb("causal", [P, P])
        B = sb("B", [P, NH, 256])
        sq = sb("sq", [P, 11, D])
        ss = sb("ss", [P, 11])
        qkn = sb("qkn", [P, 2, 5, P])
        kin = sb("kin", [P, 2, 2, D])
        wi = sb("wi", [P, 4])
        eps = sb("eps", [P, 1])
        qT = sb("qT", [P, 2, 4, P])
        qiT = sb("qiT", [P, 2, P])
        kT = sb("kT", [P, SEQ])
        kiT = sb("kiT", [P, SEQ])
        V = sb("V", [P, QT, P])
        rl = sb("rl", [P, 4, 512])
        sc = sb("sc", [P, SEQ])
        best = sb("best", [P, 8])
        msk = sb("msk", [P, SEQ])
        near = sb("near", [P, 2, 256])
        lg = sb("lg", [P, NH, SEQ])
        mxs = sb("mxs", [P, NH, 6])
        neg = sb("neg", [P, NH])
        tot = sb("tot", [P, NH])
        PT = sb("PT", [P, 2, 512])
        o_sb = sb("o", [P, NH, D])
        oT_sb = sb("oT", [P, 4, P])
        pb = [ctx.enter_context(nc.psum_tensor(f"ap_ps{k}", [P, 512], F32)) for k in range(8)]
        par = ctx.enter_context(nc.semaphore("ap_parameters_loaded"))
        const = ctx.enter_context(nc.semaphore("ap_constants"))
        v_ld = ctx.enter_context(nc.semaphore("ap_v_loaded"))
        v_st = ctx.enter_context(nc.semaphore("ap_v_stored"))
        z_ld = [ctx.enter_context(nc.semaphore(f"ap_z_loaded{k}")) for k in range(2)]
        k_st = [ctx.enter_context(nc.semaphore(f"ap_k_stored{k}")) for k in range(2)]
        o_st = ctx.enter_context(nc.semaphore("ap_o_stored"))

        def chunks(n, size=512):
            return [(at, min(size, n - at)) for at in range(0, n, size)]

        def keys(i):
            return P * (i + 1)

        def logit_chunks(a):
            far = max(0, keys(a) - 256)
            return chunks(far) + [(far, keys(a) - far)]

        def groups(a):
            return [list(range(k, min(k + 4, a + 1))) for k in range(0, a + 1, 4)]

        def steps_of(engine, names):
            s = Steps(nc, ctx, "ap_" + engine, names)
            s.ahead = 0
            return s

        def pv_order(a):
            n = len(groups(a))
            out = [("P", 0)]
            for k in range(n):
                if k + 1 < n:
                    out.append(("P", k + 1))
                out.append(("V", k))
            return out

        pe_n, act_n, vec_n = [], [], []
        for i in range(QT + 1):
            a = i - 1
            if i < QT:
                pe_n += [f"Tq{i}", f"Tk{i}"] + [f"S{i}_{c}_{hp}" for c, _ in enumerate(chunks(keys(i))) for hp in range(2)]
                act_n += [f"sq{i}", f"std{i}", f"q{i}", f"k{i}"] + [f"R{i}_{c}_{h}" for c, _ in enumerate(chunks(keys(i))) for h in range(4)]
                vec_n += [f"{k}{i}" for k in ("ss", "r", "nq", "nk", "ni", "gq", "gi", "wi")]
                vec_n += [f"A{i}_{c}_{h}" for c, _ in enumerate(chunks(keys(i))) for h in range(4)] + [f"M{i}"]
            for h in range(NH):
                if a >= 0:
                    vec_n += [f"nb{a}_{h}"] + [f"L{a}_{h}_{c}" for c, _ in enumerate(logit_chunks(a))] + [f"ng{a}_{h}"]
                if 2 <= i < QT:
                    vec_n += [f"{k}{i}_{r}" for r in range(4 * h, 4 * h + 4) for k in ("mx", "mr")]
            if i < QT:
                vec_n += [f"mk{i}"]
            if a >= 0:
                vec_n += [f"rc{a}", f"on{a}"]
                for h in range(NH + 1):
                    if h < NH:
                        pe_n += [f"L{a}_{h}_{c}" for c, _ in enumerate(logit_chunks(a))]
                    if h:
                        pe_n += [f"{k}{a}_{h - 1}_{g}" for k, g in pv_order(a)]
                for h in range(NH):
                    act_n += [f"E{a}_{h}"] + [f"e{a}_{h}_{g}" for g, _ in enumerate(groups(a))]
                pe_n += [f"oT{a}"]
                act_n += [f"o{a}"]
        pe_s, act_s, vec_s = steps_of("pe", pe_n), steps_of("act", act_n), steps_of("vec", vec_n)

        def ring(names_of):
            flat = list(names_of)
            return {n: (k % 2, flat[k - 2] if k >= 2 else None) for k, n in enumerate(flat)}

        l_ring = ring([n for n in pe_n if n[0] == "L"])
        p_ring = ring([n for n in pe_n if n[0] == "P"])
        block = ctx.enter_context(nc.Block())

        @block.sync
        def _(sp):
            loads = [(gain[:, h, :], t["q_norm"].partition_broadcast(P)) for h in range(8)]
            loads += [(gain[:, 8 + h, :], t["k_norm"].partition_broadcast(P)) for h in range(2)] + [(gain[:, 10, :], t["kidx_norm"].partition_broadcast(P))]
            loads += [(B[:, :, :], bass.AP(t["bias"].tensor, P - 1, [[BIAS_W - 1, P], [P * BIAS_W, NH], [1, 256]]))]
            for dst, src in loads:
                sp.dma_start(dst, src).then_inc(par, 16)
            sp.dma_start(t["v_p"], t["za"][0:SEQ, 640:768]).then_inc(v_st, 16)
            for i in range(QT):
                if i >= 2:
                    sp.wait_ge(*pe_s.at(f"Tk{i - 2}", 0))
                    sp.wait_ge(*vec_s.at(f"wi{i - 2}", 0))
                sp.dma_start(z[:, i % 2, :], t["za"][i * P:(i + 1) * P, :]).then_inc(z_ld[i % 2], 16)
                if i == 0:
                    sp.dma_start(V[:, :, :], t["za"][0:SEQ, 640:768].rearrange("(i p) d -> p i d", p=P)).then_inc(v_ld, 16)
            sp.wait_ge(v_st, 16)

        @block.gpsimd
        def _(pool):
            pool.memset(eps[:, :], NORM_EPS).then_inc(const, 1)
            pool.memset(causal[:, :], 0.0).then_inc(const, 1)
            pool.wait_ge(const, 2)
            pool.affine_select(out=causal[:, :], in_=causal[:, :], compare_op=ALU.is_ge, fill=OUT, base=0, pattern=[[-1, P]], channel_multiplier=1).then_inc(const, 1)
            for i in range(QT + 1):
                if i < QT:
                    pool.wait_ge(*vec_s.at(f"gi{i}", 0))
                    pool.dma_start(t["k_p"][i * P:(i + 1) * P, :], qkn[:, i % 2, 4, :]).then_inc(k_st[i % 2], 16)
                    pool.dma_start(t["ki_p"][i * P:(i + 1) * P, :], kin[:, i % 2, 0, :]).then_inc(k_st[i % 2], 16)
                if i:
                    pool.wait_ge(*act_s.at(f"o{i - 1}", 0))
                    pool.dma_start(t["oT"][4:8, :, (i - 1) * P:i * P].rearrange("b p t -> p b t"), oT_sb[:, :, :]).then_inc(o_st, 16)
            for k in range(2):
                pool.wait_ge(k_st[k], 32 * (QT // 2))
            pool.wait_ge(o_st, 16 * QT)

        @block.tensor
        def _(pe):
            vec = lambda name: pe.wait_ge(*vec_s.at(name, 0))
            act = lambda name: pe.wait_ge(*act_s.at(name, 0))

            def mul(out, lhsT, rhs, start=True, stop=True):
                return pe.matmul(out, lhsT, rhs, start=start, stop=stop, skip_group_check=True)

            def logits(a, h):
                j, r = h % 4, slice(64 * (h // 4), 64 * (h // 4) + 64)
                for c, (at, n) in enumerate(logit_chunks(a)):
                    name = f"L{a}_{h}_{c}"
                    b, before = l_ring[name]
                    if before:
                        vec(before)
                    mul(pb[2 + b][:, 0:n], qT[r, a % 2, j, :], kT[r, at:at + n]).then_inc(*pe_s.step(name))

            def attend(a, h):
                for kind, g in pv_order(a):
                    name = f"{kind}{a}_{h}_{g}"
                    if kind == "P":
                        b, before = p_ring[name]
                        if before:
                            act("e" + before[1:])
                        act(f"E{a}_{h}")
                        for x, k in enumerate(groups(a)[g]):
                            mm = pe.transpose(pb[4 + b][:, x * P:(x + 1) * P], lg[:, h, k * P:(k + 1) * P], ident)
                    else:
                        b, _ = p_ring[f"P{a}_{h}_{g}"]
                        act(f"e{a}_{h}_{g}")
                        for x, k in enumerate(groups(a)[g]):
                            mm = mul(pb[6][:, h * D:(h + 1) * D], PT[:, b, x * P:(x + 1) * P], V[:, k, 64 * (h // 4):64 * (h // 4) + 64], k == 0, k == a)
                    mm.then_inc(*pe_s.step(name))

            pe.wait_ge(v_ld, 16)
            for i in range(QT + 1):
                a = i - 1
                if i < QT:
                    vec(f"gi{i}")
                    if a >= 1:
                        act(f"o{a - 1}")
                    if i:
                        act(f"k{i - 1}")
                    for b in range(4):
                        mm = pe.transpose(pb[7][:, b * P:(b + 1) * P], qkn[:, i % 2, b, :], ident)
                    mm.then_inc(*pe_s.step(f"Tq{i}"))
                    act(f"q{i}")
                    for b in range(2):
                        pe.transpose(pb[7][:, b * P:(b + 1) * P], z[:, i % 2, 768 + b * P:768 + (b + 1) * P], ident)
                    pe.transpose(pb[7][:, 2 * P:3 * P], qkn[:, i % 2, 4, :], ident)
                    pe.transpose(pb[7][:, 3 * P:4 * P], kin[:, i % 2, :, :].rearrange("p a d -> p (a d)"), ident).then_inc(*pe_s.step(f"Tk{i}"))
                    act(f"k{i}")
                    for c, (at, n) in enumerate(chunks(keys(i))):
                        for hp in range(2):
                            if c or hp:
                                act(f"R{i}_{c if hp else c - 1}_{1 if hp else 3}")
                            elif i:
                                act(f"R{i - 1}_{len(chunks(keys(i - 1))) - 1}_3")
                            for o in range(2):
                                mm = mul(pb[o][:, 0:n], qiT[64 * o:64 * o + 64, hp, :], kiT[64 * o:64 * o + 64, at:at + n])
                            mm.then_inc(*pe_s.step(f"S{i}_{c}_{hp}"))
                if a >= 0:
                    logits(a, 0)
                    for h in range(NH):
                        if h + 1 < NH:
                            logits(a, h + 1)
                        if h == 0 and a:
                            vec(f"on{a - 1}")
                        attend(a, h)
                    vec(f"on{a}")
                    for b in range(4):
                        mm = pe.transpose(pb[7][:, b * P:(b + 1) * P], o_sb[:, 2 * b:2 * b + 2, :].rearrange("p h d -> p (h d)"), ident)
                    mm.then_inc(*pe_s.step(f"oT{a}"))

        @block.scalar
        def _(act):
            pe = lambda name: act.wait_ge(*pe_s.at(name, 0))
            vec = lambda name: act.wait_ge(*vec_s.at(name, 0))
            act.wait_ge(const, 3)
            for i in range(QT + 1):
                a = i - 1
                if i < QT:
                    act.wait_ge(z_ld[i % 2], 16 * (i // 2 + 1))
                    if i:
                        vec(f"ss{i - 1}")
                    act.activation(sq[:, 0:10, :].rearrange("p a d -> p (a d)"), z[:, i % 2, 0:640], ACT.Square)
                    act.activation(sq[:, 10, :], z[:, i % 2, 1024:1088], ACT.Square).then_inc(*act_s.step(f"sq{i}"))
                    vec(f"ss{i}")
                    act.activation(ss[:, :], ss[:, :], ACT.Sqrt, scale=1.0 / D, bias=eps[:, :]).then_inc(*act_s.step(f"std{i}"))
                    pe(f"Tq{i}")
                    act.activation(qT[:, i % 2, :, :].rearrange("p b t -> p (b t)"), pb[7][:, :], ACT.Copy).then_inc(*act_s.step(f"q{i}"))
                    pe(f"Tk{i}")
                    act.activation(qiT[:, :, :].rearrange("p b t -> p (b t)"), pb[7][:, 0:256], ACT.Copy)
                    act.activation(kT[:, i * P:(i + 1) * P], pb[7][:, 256:384], ACT.Copy)
                    act.activation(kiT[:, i * P:(i + 1) * P], pb[7][:, 384:512], ACT.Copy).then_inc(*act_s.step(f"k{i}"))
                    for c, (at, n) in enumerate(chunks(keys(i))):
                        for h in range(4):
                            pe(f"S{i}_{c}_{h // 2}")
                            if c:
                                vec(f"A{i}_{c - 1}_{h}")
                            elif i:
                                vec(f"A{i - 1}_{len(chunks(keys(i - 1))) - 1}_{h}")
                            act.activation(rl[:, h, 0:n], pb[h % 2][:, 0:n], ACT.Relu).then_inc(*act_s.step(f"R{i}_{c}_{h}"))
                if a >= 0:
                    for h in range(NH):
                        vec(f"ng{a}_{h}")
                        if a:
                            vec(f"rc{a - 1}")
                        act.activation(lg[:, h, 0:keys(a)], lg[:, h, 0:keys(a)], ACT.Exp, bias=neg[:, h:h + 1], accum_out=tot[:, h:h + 1]).then_inc(*act_s.step(f"E{a}_{h}"))
                        for g, tiles in enumerate(groups(a)):
                            name = f"P{a}_{h}_{g}"
                            b, before = p_ring[name]
                            pe(name)
                            if before:
                                pe("V" + before[1:])
                            act.activation(PT[:, b, 0:len(tiles) * P], pb[4 + b][:, 0:len(tiles) * P], ACT.Copy).then_inc(*act_s.step(f"e{a}_{h}_{g}"))
                    pe(f"oT{a}")
                    if a:
                        act.wait_ge(o_st, 16 * a)
                    act.activation(oT_sb[:, :, :].rearrange("p b t -> p (b t)"), pb[7][:, :], ACT.Copy).then_inc(*act_s.step(f"o{a}"))

        @block.vector
        def _(dve):
            pe = lambda name: dve.wait_ge(*pe_s.at(name, 0))
            act = lambda name: dve.wait_ge(*act_s.at(name, 0))
            own = lambda name: dve.wait_ge(*vec_s.at(name, 0))
            heads = lambda x: x.unsqueeze(2).to_broadcast([P, 8, D])
            dve.wait_ge(par, 16 * 12)
            dve.wait_ge(const, 3)
            dve.tensor_scalar(gain[:, 0:8, :], gain[:, 0:8, :], D ** -0.5, None, ALU.mult).then_inc(const, 1)
            dve.wait_ge(const, 4)
            for i in range(QT + 1):
                a = i - 1
                if i < QT:
                    zi, qn = z[:, i % 2, :], qkn[:, i % 2, :, :]
                    act(f"sq{i}")
                    dve.tensor_reduce(ss[:, :], sq[:, :, :], AX.X, ALU.add).then_inc(*vec_s.step(f"ss{i}"))
                    act(f"std{i}")
                    dve.reciprocal(ss[:, :], ss[:, :]).then_inc(*vec_s.step(f"r{i}"))
                    own(f"r{i}")
                    if i >= 2:
                        dve.wait_ge(k_st[i % 2], 32 * (i // 2))
                        pe(f"Tk{i - 2}")
                    for n in range(2):
                        op = dve.tensor_tensor(qn[:, 0:4, n * D:(n + 1) * D], zi[:, n * 256:(n + 1) * 256].rearrange("p (j d) -> p j d", j=4),
                                               ss[:, 4 * n:4 * n + 4].unsqueeze(2).to_broadcast([P, 4, D]), ALU.mult)
                    op.then_inc(*vec_s.step(f"nq{i}"))
                    dve.tensor_tensor(qn[:, 4, :].rearrange("p (n d) -> p n d", n=2), zi[:, 512:640].rearrange("p (n d) -> p n d", n=2),
                                      ss[:, 8:10].unsqueeze(2).to_broadcast([P, 2, D]), ALU.mult).then_inc(*vec_s.step(f"nk{i}"))
                    dve.tensor_scalar(kin[:, i % 2, 1, :], zi[:, 1024:1088], ss[:, 10:11], None, ALU.mult).then_inc(*vec_s.step(f"ni{i}"))
                    own(f"nk{i}")
                    dve.tensor_tensor(qn.rearrange("p b d -> p (b d)"), qn.rearrange("p b d -> p (b d)"), gain[:, 0:10, :].rearrange("p h d -> p (h d)"), ALU.mult).then_inc(*vec_s.step(f"gq{i}"))
                    own(f"ni{i}")
                    dve.tensor_tensor(kin[:, i % 2, 0, :], kin[:, i % 2, 1, :], gain[:, 10, :], ALU.mult)
                    dve.tensor_tensor(kin[:, i % 2, 1, :], kin[:, i % 2, 1, :], gain[:, 10, :], ALU.mult).then_inc(*vec_s.step(f"gi{i}"))
                    dve.tensor_scalar(wi[:, :], zi[:, 1088:1092], 0.125 * 0.5, None, ALU.mult).then_inc(*vec_s.step(f"wi{i}"))
                    own(f"wi{i}")
                    for c, (at, n) in enumerate(chunks(keys(i))):
                        for h in range(4):
                            act(f"R{i}_{c}_{h}")
                            if h == 0:
                                op = dve.tensor_scalar(sc[:, at:at + n], rl[:, 0, 0:n], wi[:, 0:1], None, ALU.mult)
                            else:
                                own(f"A{i}_{c}_{h - 1}")
                                op = dve.scalar_tensor_tensor(out=sc[:, at:at + n], in0=rl[:, h, 0:n], scalar=wi[:, h:h + 1], in1=sc[:, at:at + n], op0=ALU.mult, op1=ALU.add)
                            op.then_inc(*vec_s.step(f"A{i}_{c}_{h}"))
                    own(f"A{i}_{c}_3")
                    dve.tensor_tensor(sc[:, i * P:(i + 1) * P], sc[:, i * P:(i + 1) * P], causal[:, :], ALU.add).then_inc(*vec_s.step(f"M{i}"))
                    own(f"M{i}")
                for h in range(NH):
                    if a >= 0:
                        cs = logit_chunks(a)
                        at, n = cs[-1]
                        dve.tensor_tensor(near[:, h % 2, 0:n], msk[:, at:at + n], B[:, h, 256 - n:256], ALU.add).then_inc(*vec_s.step(f"nb{a}_{h}"))
                        if a:
                            pe(f"P{a - 1}_{h}_{len(groups(a - 1)) - 1}")
                        for c, (at, n) in enumerate(cs):
                            pe(f"L{a}_{h}_{c}")
                            last = c == len(cs) - 1
                            if last:
                                own(f"nb{a}_{h}")
                            if c:
                                own(f"L{a}_{h}_{c - 1}")
                            add = near[:, h % 2, 0:n] if last else msk[:, at:at + n]
                            b = l_ring[f"L{a}_{h}_{c}"][0]
                            dve.tensor_tensor_reduce(lg[:, h, at:at + n], pb[2 + b][:, 0:n], add, 1.0, mxs[:, h, c - 1:c] if c else LEAST,
                                                     ALU.add, ALU.max, mxs[:, h, c:c + 1]).then_inc(*vec_s.step(f"L{a}_{h}_{c}"))
                        own(f"L{a}_{h}_{len(cs) - 1}")
                        dve.tensor_scalar(neg[:, h:h + 1], mxs[:, h, len(cs) - 1:len(cs)], -1.0, None, ALU.mult).then_inc(*vec_s.step(f"ng{a}_{h}"))
                    if 2 <= i < QT:
                        for r in range(4 * h, 4 * h + 4):
                            if r:
                                own(f"mr{i}_{r - 1}")
                            dve.max(best[:, :], sc[:, 0:keys(i)]).then_inc(*vec_s.step(f"mx{i}_{r}"))
                            own(f"mx{i}_{r}")
                            dve.match_replace(sc[:, 0:keys(i)], best[:, :], sc[:, 0:keys(i)], GONE).then_inc(*vec_s.step(f"mr{i}_{r}"))
                if i < QT:
                    if i >= 2:
                        own(f"mr{i}_{ROUNDS - 1}")
                        op = dve.tensor_scalar(msk[:, 0:keys(i)], sc[:, 0:keys(i)], -1e38, OUT, ALU.is_gt, ALU.mult)
                    else:
                        op = dve.tensor_scalar(msk[:, 0:keys(i)], sc[:, 0:keys(i)], -1e29, OUT, ALU.is_lt, ALU.mult)
                    op.then_inc(*vec_s.step(f"mk{i}"))
                    own(f"mk{i}")
                if a >= 0:
                    act(f"E{a}_{NH - 1}")
                    dve.reciprocal(tot[:, :], tot[:, :]).then_inc(*vec_s.step(f"rc{a}"))
                    own(f"rc{a}")
                    pe(f"V{a}_{NH - 1}_{len(groups(a)) - 1}")
                    if a:
                        pe(f"oT{a - 1}")
                    dve.tensor_tensor(o_sb[:, :, :], pb[6][:, :].rearrange("p (h d) -> p h d", h=NH), heads(tot[:, :]), ALU.mult).then_inc(*vec_s.step(f"on{a}"))


def sample_constants():
    step = np.arange(TS) % DEC_SEQ
    behind = np.where(np.arange(DEC_SEQ)[None, :] > step[:, None], -1e30, 0.0)
    row, b, t_ = np.arange(TS)[:, None, None, None], np.arange(DEC_BATCH)[None, :, None, None], np.arange(DEC_SEQ)[None, None, None, :]
    spread = (row == b * DEC_SEQ + t_) * np.ones((1, 1, 8, 1))
    return dict(behind=behind.astype(np.float32), spread=spread.reshape(TS, DEC_BATCH, TS).astype(np.float32),
                quarter=(np.arange(P) % 4).astype(np.float32).reshape(P, 1))


def attention_sample(nc, ident, t):
    NH, D, L, R = 8, 64, PAST + DEC_SEQ, PAST // P
    ROUNDS = 256 // 8
    OUT, GONE, LEAST = -1e30, -3e38, -3.4e38
    with ExitStack() as outer:
        def make(ctx, prefix):
            return lambda name, shape, dt=F32: ctx.enter_context(nc.sbuf_tensor(prefix + name, shape, dt))

        keep = make(outer, "as_")
        idx = keep("idx", [P, DEC_BATCH], I32)
        Q = keep("Q", [P, DEC_BATCH, NH, DEC_SEQ])
        kTn = keep("kTn", [P, TS])
        Vn = keep("Vn", [DEC_SEQ, DEC_BATCH, P])
        msk = keep("msk", [TS, L])
        spread = keep("spread", [TS, DEC_BATCH, TS])
        with ExitStack() as ctx:
            sb = make(ctx, "ai_")
            z = sb("z", [TS, N_ATT])
            gain = sb("gain", [TS, 11, D])
            behind = sb("behind", [TS, DEC_SEQ])
            quarter = sb("quarter", [P, 1])
            pages = sb("pages", [P, DEC_BATCH], I32)
            sq = sb("sq", [TS, 11, D])
            ss = sb("ss", [TS, 11])
            qkn = sb("qkn", [TS, 5, P])
            kin = sb("kin", [TS, 2, D])
            qid = sb("qid", [TS, 4, 2, D])
            wi = sb("wi", [TS, 4])
            eps = sb("eps", [TS, 1])
            Qi = sb("Qi", [P, 4, 320])
            kiN = sb("kiN", [P, 4, DEC_SEQ])
            raw = sb("raw", [P, 2, R * D])
            kp = sb("kp", [P, 2, R, P])
            kiT = sb("kiT", [P, 4, PAST])
            rl = sb("rl", [TS, 4, 512])
            sc = sb("sc", [TS, L])
            best = sb("best", [TS, 8])
            pb = [ctx.enter_context(nc.psum_tensor(f"ai_ps{k}", [P, 512], F32)) for k in range(8)]
            sem = lambda name: ctx.enter_context(nc.semaphore("ai_" + name))
            par, const, kv_st, idx_ok = sem("parameters_loaded"), sem("constants"), sem("new_kv_stored"), sem("index_ready")
            z_ld, vn_ld = sem("z_loaded"), sem("vn_loaded")
            raw_ld = [sem(f"kidx_loaded{k}") for k in range(2)]
            chunks = [(c * 512, 512) for c in range(PAST // 512)] + [(PAST, DEC_SEQ)]
            GR = R // 4

            def steps_of(engine, names):
                s = Steps(nc, ctx, "ai_" + engine, names)
                s.ahead = 0
                return s

            pe_s = steps_of("pe", ["Tq", "Tk", "Ti"] + [f"T{p}_{g}" for p in range(4) for g in range(GR)] + [f"S{c}_{h}" for c, _ in enumerate(chunks) for h in range(4)])
            act_s = steps_of("act", ["sq", "std", "Q", "k", "Qi"] + [f"T{p}_{g}" for p in range(4) for g in range(GR)] + [f"R{c}_{h}" for c, _ in enumerate(chunks) for h in range(4)])
            vec_s = steps_of("vec", ["ss", "r", "nq", "nk", "ni", "gq", "gi", "qid", "wi"] + [f"A{c}_{h}" for c, _ in enumerate(chunks) for h in range(4)]
                             + ["M"] + [f"{k}{r}" for r in range(ROUNDS) for k in ("mx", "mr")] + ["mk"])
            pool_s = steps_of("pool", [f"kp{b}" for b in range(DEC_BATCH)])
            block = nc.Block()
            with block:
                @block.sync
                def _(sp):
                    sp.dma_start(z[:, :], t["za"][SEQ:NT, :]).then_inc(z_ld, 16)
                    loads = [(gain[:, h, :], t["q_norm"].partition_broadcast(TS)) for h in range(8)]
                    loads += [(gain[:, 8 + h, :], t["k_norm"].partition_broadcast(TS)) for h in range(2)] + [(gain[:, 10, :], t["kidx_norm"].partition_broadcast(TS))]
                    loads += [(behind[:, :], t["behind"]), (spread[:, :, :], t["spread"]), (quarter[:, :], t["quarter"])]
                    with nc.allow_non_contiguous_dma(reason="page numbers"):
                        loads += [(pages[q:P:4, :], t["page_table"].rearrange("b j -> j b")) for q in range(4)]
                        for dst, src in loads:
                            sp.dma_start(dst, src).then_inc(par, 16)
                    sp.dma_start(Vn[:, :, :], t["za"][SEQ:NT, 640:768].rearrange("(b t) d -> t b d", t=DEC_SEQ)).then_inc(vn_ld, 16)
                    sp.dma_start(t["v_s"], t["za"][SEQ:NT, 640:768]).then_inc(kv_st, 16)
                    sp.wait_ge(*vec_s.at("gi", 0))
                    sp.dma_start(t["k_s"], qkn[:, 4, :]).then_inc(kv_st, 16)
                    sp.dma_start(t["ki_s"], kin[:, 0, :]).then_inc(kv_st, 16)
                    sp.wait_ge(kv_st, 48)
                    sp.wait_ge(vn_ld, 16)

                @block.gpsimd
                def _(pool):
                    pool.memset(eps[:, :], NORM_EPS).then_inc(const, 1)
                    pool.memset(Q[:, :, :, :], 0.0).then_inc(const, 1)
                    pool.memset(Qi[:, :, :], 0.0).then_inc(const, 1)
                    pool.wait_ge(idx_ok, 1)
                    kidx_rows = t["cache_kidx"].rearrange("n (q r) d -> (n q) (r d)", q=4)

                    def gather(b):
                        pool.indirect_dma_start(raw[:, b % 2, :], None, kidx_rows, bass.IndirectOffsetOnAxis(ap=idx[:, b:b + 1], axis=0)).then_inc(raw_ld[b % 2], 16)

                    gather(0)
                    for b in range(DEC_BATCH):
                        if b + 1 < DEC_BATCH:
                            if b:
                                pool.wait_ge(*pool_s.at(f"kp{b - 1}", 0))
                            gather(b + 1)
                        pool.wait_ge(raw_ld[b % 2], 16 * (b // 2 + 1))
                        if b >= 4:
                            pool.wait_ge(*pe_s.at(f"T{b // 2 - 2}_{GR - 1}", 0))
                        pool.tensor_copy(kp[:, (b // 2) % 2, :, (b % 2) * D:(b % 2 + 1) * D], raw[:, b % 2, :].rearrange("p (r d) -> p r d", d=D)).then_inc(*pool_s.step(f"kp{b}"))

                @block.tensor
                def _(pe):
                    vec = lambda name: pe.wait_ge(*vec_s.at(name, 0))
                    act = lambda name: pe.wait_ge(*act_s.at(name, 0))
                    i64 = ident[0:TS, 0:TS]
                    vec("gi")
                    for j in range(4):
                        mm = pe.transpose(pb[0][:, j * TS:(j + 1) * TS], qkn[:, j, :], i64)
                    mm.then_inc(*pe_s.step("Tq"))
                    pe.transpose(pb[1][:, 0:TS], qkn[:, 4, :], i64)
                    pe.transpose(pb[1][:, TS:2 * TS], kin[:, :, :].rearrange("p a d -> p (a d)"), i64).then_inc(*pe_s.step("Tk"))
                    vec("qid")
                    for h in range(4):
                        mm = pe.transpose(pb[2][:, h * TS:(h + 1) * TS], qid[:, h, :, :].rearrange("p a d -> p (a d)"), i64)
                    mm.then_inc(*pe_s.step("Ti"))
                    n = 0
                    for p in range(4):
                        pe.wait_ge(*pool_s.at(f"kp{2 * p + 1}", 0))
                        for g in range(GR):
                            if n >= 2:
                                q = n - 2
                                act(f"T{q // GR}_{q % GR}")
                            for x in range(4):
                                mm = pe.transpose(pb[3 + n % 2][:, x * P:(x + 1) * P], kp[:, p % 2, 4 * g + x, :], ident)
                            mm.then_inc(*pe_s.step(f"T{p}_{g}"))
                            n += 1
                    act(f"T3_{GR - 1}")
                    for c, (at, m) in enumerate(chunks):
                        for h in range(4):
                            if c:
                                act(f"R{c - 1}_{h}")
                            else:
                                act("Qi")
                            bank = [5, 6, 7, 0][h]
                            for p in range(4):
                                rhs = kiN[:, p, :] if at == PAST else kiT[:, p, at:at + m]
                                mm = pe.matmul(pb[bank][0:TS, 0:m], Qi[:, h, p * TS:(p + 1) * TS], rhs, start=p == 0, stop=p == 3)
                            mm.then_inc(*pe_s.step(f"S{c}_{h}"))

                @block.scalar
                def _(act):
                    pe = lambda name: act.wait_ge(*pe_s.at(name, 0))
                    vec = lambda name: act.wait_ge(*vec_s.at(name, 0))
                    act.wait_ge(const, 3)
                    act.wait_ge(z_ld, 16)
                    act.activation(sq[:, 0:10, :].rearrange("p a d -> p (a d)"), z[:, 0:640], ACT.Square)
                    act.activation(sq[:, 10, :], z[:, 1024:1088], ACT.Square).then_inc(*act_s.step("sq"))
                    vec("ss")
                    act.activation(ss[:, :], ss[:, :], ACT.Sqrt, scale=1.0 / D, bias=eps[:, :]).then_inc(*act_s.step("std"))
                    pe("Tq")
                    for n in range(2):
                        r = slice(64 * n, 64 * n + 64)
                        for j in range(4):
                            op = act.activation(Q[r, :, 4 * n + j, :], pb[0][r, j * TS:(j + 1) * TS].rearrange("p (b s) -> p b s", s=DEC_SEQ), ACT.Copy)
                    op.then_inc(*act_s.step("Q"))
                    pe("Tk")
                    act.activation(kTn[:, :], pb[1][:, 0:TS], ACT.Copy)
                    for n in range(2):
                        r = slice(64 * n, 64 * n + 64)
                        op = act.activation(kiN[r, :, :], pb[1][r, TS:2 * TS].rearrange("p (c two s) -> p c two s", two=2, s=DEC_SEQ)[:, :, n, :], ACT.Copy)
                    op.then_inc(*act_s.step("k"))
                    pe("Ti")
                    for n in range(2):
                        r = slice(64 * n, 64 * n + 64)
                        for h in range(4):
                            op = act.activation(Qi[r, h, :].rearrange("p (c x) -> p c x", x=80)[:, :, n * DEC_SEQ:(n + 1) * DEC_SEQ],
                                                pb[2][r, h * TS:(h + 1) * TS].rearrange("p (c two s) -> p c two s", two=2, s=DEC_SEQ)[:, :, n, :], ACT.Copy)
                    op.then_inc(*act_s.step("Qi"))
                    n = 0
                    for p in range(4):
                        for g in range(GR):
                            pe(f"T{p}_{g}")
                            act.activation(kiT[:, p, :].rearrange("k (q r) -> k r q", r=R)[:, 4 * g:4 * g + 4, :], pb[3 + n % 2][:, :].rearrange("k (r q) -> k r q", r=4), ACT.Copy).then_inc(*act_s.step(f"T{p}_{g}"))
                            n += 1
                    for c, (at, m) in enumerate(chunks):
                        for h in range(4):
                            pe(f"S{c}_{h}")
                            if c:
                                vec(f"A{c - 1}_{h}")
                            act.activation(rl[:, h, 0:m], pb[[5, 6, 7, 0][h]][0:TS, 0:m], ACT.Relu).then_inc(*act_s.step(f"R{c}_{h}"))

                @block.vector
                def _(dve):
                    act = lambda name: dve.wait_ge(*act_s.at(name, 0))
                    own = lambda name: dve.wait_ge(*vec_s.at(name, 0))
                    dve.wait_ge(par, 16 * 18)
                    dve.tensor_scalar(idx[:, :], pages[:, :], 4.0, quarter[:, 0:1], ALU.mult, ALU.add).then_inc(idx_ok, 1)
                    dve.wait_ge(const, 3)
                    dve.tensor_scalar(gain[:, 0:8, :], gain[:, 0:8, :], D ** -0.5, None, ALU.mult).then_inc(const, 1)
                    act("sq")
                    dve.tensor_reduce(ss[:, :], sq[:, :, :], AX.X, ALU.add).then_inc(*vec_s.step("ss"))
                    act("std")
                    dve.reciprocal(ss[:, :], ss[:, :]).then_inc(*vec_s.step("r"))
                    own("r")
                    for n in range(2):
                        op = dve.tensor_tensor(qkn[:, 0:4, n * D:(n + 1) * D], z[:, n * 256:(n + 1) * 256].rearrange("p (j d) -> p j d", j=4),
                                               ss[:, 4 * n:4 * n + 4].unsqueeze(2).to_broadcast([TS, 4, D]), ALU.mult)
                    op.then_inc(*vec_s.step("nq"))
                    dve.tensor_tensor(qkn[:, 4, :].rearrange("p (n d) -> p n d", n=2), z[:, 512:640].rearrange("p (n d) -> p n d", n=2),
                                      ss[:, 8:10].unsqueeze(2).to_broadcast([TS, 2, D]), ALU.mult).then_inc(*vec_s.step("nk"))
                    dve.tensor_scalar(kin[:, 1, :], z[:, 1024:1088], ss[:, 10:11], None, ALU.mult).then_inc(*vec_s.step("ni"))
                    own("nk")
                    dve.wait_ge(const, 4)
                    flat = qkn[:, :, :].rearrange("p b d -> p (b d)")
                    dve.tensor_tensor(flat, flat, gain[:, 0:10, :].rearrange("p h d -> p (h d)"), ALU.mult).then_inc(*vec_s.step("gq"))
                    own("ni")
                    dve.tensor_tensor(kin[:, 0, :], kin[:, 1, :], gain[:, 10, :], ALU.mult)
                    dve.tensor_tensor(kin[:, 1, :], kin[:, 1, :], gain[:, 10, :], ALU.mult).then_inc(*vec_s.step("gi"))
                    for n in range(2):
                        op = dve.tensor_copy(qid[:, :, n, :], z[:, 768:1024].rearrange("p (h d) -> p h d", h=4))
                    op.then_inc(*vec_s.step("qid"))
                    dve.tensor_scalar(wi[:, :], z[:, 1088:1092], 0.125 * 0.5, None, ALU.mult).then_inc(*vec_s.step("wi"))
                    own("wi")
                    for c, (at, m) in enumerate(chunks):
                        for h in range(4):
                            act(f"R{c}_{h}")
                            if h == 0:
                                op = dve.tensor_scalar(sc[:, at:at + m], rl[:, 0, 0:m], wi[:, 0:1], None, ALU.mult)
                            else:
                                own(f"A{c}_{h - 1}")
                                op = dve.scalar_tensor_tensor(out=sc[:, at:at + m], in0=rl[:, h, 0:m], scalar=wi[:, h:h + 1], in1=sc[:, at:at + m], op0=ALU.mult, op1=ALU.add)
                            op.then_inc(*vec_s.step(f"A{c}_{h}"))
                    own(f"A{len(chunks) - 1}_3")
                    dve.tensor_tensor(sc[:, PAST:L], sc[:, PAST:L], behind[:, :], ALU.add).then_inc(*vec_s.step("M"))
                    own("M")
                    for r in range(ROUNDS):
                        if r:
                            own(f"mr{r - 1}")
                        dve.max(best[:, :], sc[:, :]).then_inc(*vec_s.step(f"mx{r}"))
                        own(f"mx{r}")
                        dve.match_replace(sc[:, :], best[:, :], sc[:, :], GONE).then_inc(*vec_s.step(f"mr{r}"))
                    own(f"mr{ROUNDS - 1}")
                    dve.tensor_scalar(msk[:, :], sc[:, :], -1e38, OUT, ALU.is_gt, ALU.mult).then_inc(*vec_s.step("mk"))

        with ExitStack() as ctx:
            sb = make(ctx, "aa_")
            FAR = PAST - P
            B = sb("B", [TS, P + DEC_SEQ])
            kraw = sb("kraw", [P, R * P])
            v = sb("v", [P, 2, R * P])
            kT = sb("kT", [P, PAST])
            lg = sb("lg", [TS, L])
            PT = sb("PT", [P, 2, 8, TS])
            mxs = sb("mxs", [TS, 9])
            neg = sb("neg", [TS, 1])
            tot = sb("tot", [TS, 1])
            o_sb = sb("o", [TS, 2, D])
            o_all = sb("o_all", [TS, 512])
            oT_sb = sb("oT", [P, 4, TS])
            pb = [ctx.enter_context(nc.psum_tensor(f"aa_ps{k}", [P, 512], F32)) for k in range(8)]
            sem = lambda name: ctx.enter_context(nc.semaphore("aa_" + name))
            b_ld, all_ld, oT_st = sem("bias_loaded"), sem("outputs_loaded"), sem("oT_stored")
            k_ld, v_ld = sem("k_loaded"), [sem(f"v_loaded{k}") for k in range(2)]
            o_st = [sem(f"o_stored{k}") for k in range(2)]
            GR = R // 4
            chunks = [(c * 512, min(512, FAR - c * 512)) for c in range(-(-FAR // 512))] + [(FAR, P + DEC_SEQ)]
            NC_ = len(chunks)
            PG = [list(range(8 * g, 8 * g + 8)) for g in range(R // 8)] + [[R]]

            def steps_of(engine, names):
                s = Steps(nc, ctx, "aa_" + engine, names)
                s.ahead = 0
                return s

            n_pg = len(PG)
            pv = [("P", 0)] + [x for g in range(n_pg) for x in ([("P", g + 1)] if g + 1 < n_pg else []) + [("V", g)]]
            pe_s = steps_of("pe", [x for b in range(DEC_BATCH) for x in [f"T{b}_{g}" for g in range(GR)] + [f"L{b}_{c}" for c in range(NC_)] + [f"{k}{b}_{g}" for k, g in pv]] + ["oT"])
            act_s = steps_of("act", [x for b in range(DEC_BATCH) for x in [f"T{b}_{g}" for g in range(0, GR, 2)] + [f"E{b}"] + [f"e{b}_{g}" for g in range(n_pg)]] + ["oT"])
            vec_s = steps_of("vec", [x for b in range(DEC_BATCH) for x in [f"T{b}_{g}" for g in range(1, GR, 2)] + [f"L{b}_{c}" for c in range(NC_)] + [f"ng{b}", f"rc{b}", f"o{b}"]])
            block = nc.Block()
            with block:
                @block.sync
                def _(sp):
                    for h in range(NH):
                        sp.dma_start(B[h * DEC_SEQ:(h + 1) * DEC_SEQ, :], bass.AP(t["bias"].tensor, h * P * BIAS_W + P - 1, [[BIAS_W - 1, DEC_SEQ], [1, P + DEC_SEQ]])).then_inc(b_ld, 16)
                    for b in range(DEC_BATCH):
                        sp.wait_ge(*vec_s.at(f"o{b}", 0))
                        for h in range(NH):
                            sp.dma_start(t["oas"][b * DEC_SEQ:(b + 1) * DEC_SEQ, h * D:(h + 1) * D], o_sb[h * DEC_SEQ:(h + 1) * DEC_SEQ, b % 2, :]).then_inc(o_st[b % 2], 16)
                    for k in range(2):
                        sp.wait_ge(o_st[k], 16 * NH * DEC_BATCH // 2)
                    sp.dma_start(o_all[:, :], t["oas"]).then_inc(all_ld, 16)
                    sp.wait_ge(*act_s.at("oT", 0))
                    sp.dma_start(t["oT"][4:8, :, SEQ:NT].rearrange("b p t -> p b t"), oT_sb[:, :, :]).then_inc(oT_st, 16)
                    sp.wait_ge(oT_st, 16)

                @block.gpsimd
                def _(pool):
                    rows = lambda name: t[name].rearrange("n (q r) d -> (n q) (r d)", q=4)
                    for b in range(DEC_BATCH):
                        at = bass.IndirectOffsetOnAxis(ap=idx[:, b:b + 1], axis=0)
                        if b >= 2:
                            pool.wait_ge(*pe_s.at(f"V{b - 2}_{n_pg - 1}", 0))
                        pool.indirect_dma_start(v[:, b % 2, :], None, rows("cache_v"), at).then_inc(v_ld[b % 2], 16)
                        if b:
                            pool.wait_ge(*pe_s.at(f"T{b - 1}_{GR - 1}", 0))
                        pool.indirect_dma_start(kraw[:, :], None, rows("cache_k"), at).then_inc(k_ld, 16)

                @block.tensor
                def _(pe):
                    vec = lambda name: pe.wait_ge(*vec_s.at(name, 0))
                    act = lambda name: pe.wait_ge(*act_s.at(name, 0))
                    turned = lambda b, g: (vec if g % 2 else act)(f"T{b}_{g}")
                    nl = npt = 0
                    for b in range(DEC_BATCH):
                        pe.wait_ge(k_ld, 16 * (b + 1))
                        for g in range(GR):
                            if g >= 2:
                                turned(b, g - 2)
                            elif b:
                                turned(b - 1, GR - 2 + g)
                            for x in range(4):
                                r = 4 * g + x
                                mm = pe.transpose(pb[g % 2][:, x * P:(x + 1) * P], kraw[:, r * P:(r + 1) * P], ident)
                            mm.then_inc(*pe_s.step(f"T{b}_{g}"))
                        turned(b, GR - 2)
                        turned(b, GR - 1)
                        for c, (at, m) in enumerate(chunks):
                            if c >= 2:
                                vec(f"L{b}_{c - 2}")
                            elif b:
                                vec(f"L{b - 1}_{NC_ - 2 + c if NC_ % 2 == 0 else NC_ - 1 - c}")
                            out = pb[2 + c % 2]
                            parts = [(0, m, kT[:, at:at + m])] if c < NC_ - 1 else [(0, P, kT[:, FAR:PAST]), (P, DEC_SEQ, kTn[:, b * DEC_SEQ:(b + 1) * DEC_SEQ])]
                            for lo, n, keys in parts:
                                pe.matmul(out[0:TS, lo:lo + n], Q[:, b, :, :].rearrange("p h s -> p (h s)"), keys, start=True, stop=False, skip_group_check=True)
                                mm = pe.matmul(out[0:TS, lo:lo + n], spread[:, b, :], msk[:, at + lo:at + lo + n], start=False, stop=True, skip_group_check=True)
                            mm.then_inc(*pe_s.step(f"L{b}_{c}"))
                        pe.wait_ge(v_ld[b % 2], 16 * (b // 2 + 1))
                        if b:
                            vec(f"o{b - 1}")
                        for kind, g in pv:
                            bank = (b * n_pg + g) % 2
                            if kind == "P":
                                act(f"E{b}")
                                if g >= 2:
                                    act(f"e{b}_{g - 2}")
                                elif b:
                                    act(f"e{b - 1}_{n_pg - 1}")
                                for x, r in enumerate(PG[g]):
                                    if r < R:
                                        mm = pe.transpose(pb[4 + bank][:, x * TS:(x + 1) * TS], lg[:, r:PAST:R], ident[0:TS, 0:TS])
                                    else:
                                        mm = pe.transpose(pb[4 + bank][0:DEC_SEQ, 0:TS], lg[:, PAST:L], ident[0:TS, 0:TS])
                            else:
                                act(f"e{b}_{g}")
                                for x, r in enumerate(PG[g]):
                                    if r < R:
                                        mm = pe.matmul(pb[6][0:TS, 0:P], PT[:, bank, x, :], v[:, b % 2, r * P:(r + 1) * P], start=r == 0, stop=False)
                                    else:
                                        mm = pe.matmul(pb[6][0:TS, 0:P], PT[0:DEC_SEQ, bank, 0, :], Vn[:, b, :], start=False, stop=True)
                            mm.then_inc(*pe_s.step(f"{kind}{b}_{g}"))
                    pe.wait_ge(all_ld, 16)
                    for j in range(4):
                        mm = pe.transpose(pb[7][:, j * TS:(j + 1) * TS], o_all[:, j * P:(j + 1) * P], ident[0:TS, 0:TS])
                    mm.then_inc(*pe_s.step("oT"))

                def turn(engine, copy, b, g):
                    engine.wait_ge(*pe_s.at(f"T{b}_{g}", 0))
                    if b:
                        engine.wait_ge(*pe_s.at(f"L{b - 1}_{NC_ - 1}", 0))
                    return copy(kT[:, :].rearrange("k (q r) -> k r q", r=R)[:, 4 * g:4 * g + 4, :], pb[g % 2][:, :].rearrange("k (r q) -> k r q", r=4))

                @block.scalar
                def _(act):
                    pe = lambda name: act.wait_ge(*pe_s.at(name, 0))
                    for b in range(DEC_BATCH):
                        for g in range(0, GR, 2):
                            turn(act, lambda o, i: act.activation(o, i, ACT.Copy), b, g).then_inc(*act_s.step(f"T{b}_{g}"))
                        act.wait_ge(*vec_s.at(f"ng{b}", 0))
                        act.activation(lg[:, :], lg[:, :], ACT.Exp, bias=neg[:, :], accum_out=tot[:, :]).then_inc(*act_s.step(f"E{b}"))
                        for g, slots in enumerate(PG):
                            bank = (b * n_pg + g) % 2
                            pe(f"P{b}_{g}")
                            if b and g < 2:
                                pe(f"V{b - 1}_{n_pg - 1}")
                            elif g >= 2:
                                pe(f"V{b}_{g - 2}")
                            n = P if slots[0] < R else DEC_SEQ
                            act.activation(PT[0:n, bank, 0:len(slots), :].rearrange("p x r -> p (x r)"), pb[4 + bank][0:n, 0:len(slots) * TS], ACT.Copy).then_inc(*act_s.step(f"e{b}_{g}"))
                    pe("oT")
                    act.activation(oT_sb[:, :, :].rearrange("p b r -> p (b r)"), pb[7][:, 0:4 * TS], ACT.Copy).then_inc(*act_s.step("oT"))

                @block.vector
                def _(dve):
                    pe = lambda name: dve.wait_ge(*pe_s.at(name, 0))
                    own = lambda name: dve.wait_ge(*vec_s.at(name, 0))
                    dve.wait_ge(b_ld, 16 * NH)
                    for b in range(DEC_BATCH):
                        for g in range(1, GR, 2):
                            turn(dve, dve.tensor_copy, b, g).then_inc(*vec_s.step(f"T{b}_{g}"))
                        if b:
                            pe(f"P{b - 1}_{n_pg - 1}")
                        for c, (at, m) in enumerate(chunks):
                            pe(f"L{b}_{c}")
                            if c:
                                own(f"L{b}_{c - 1}")
                            src, out = pb[2 + c % 2][0:TS, 0:m], lg[:, at:at + m]
                            least = mxs[:, c - 1:c] if c else LEAST
                            if c < NC_ - 1:
                                op = dve.tensor_scalar(out, src, 0.0, least, ALU.add, ALU.max, accum_out=mxs[:, c:c + 1])
                            else:
                                op = dve.tensor_tensor_reduce(out, src, B[:, :], 1.0, least, ALU.add, ALU.max, mxs[:, c:c + 1])
                            op.then_inc(*vec_s.step(f"L{b}_{c}"))
                        own(f"L{b}_{NC_ - 1}")
                        if b:
                            dve.wait_ge(*act_s.at(f"E{b - 1}", 0))
                        dve.tensor_scalar(neg[:, :], mxs[:, NC_ - 1:NC_], -1.0, None, ALU.mult).then_inc(*vec_s.step(f"ng{b}"))
                        dve.wait_ge(*act_s.at(f"E{b}", 0))
                        dve.reciprocal(tot[:, :], tot[:, :]).then_inc(*vec_s.step(f"rc{b}"))
                        own(f"rc{b}")
                        pe(f"V{b}_{n_pg - 1}")
                        if b >= 2:
                            dve.wait_ge(o_st[b % 2], 16 * NH * (b // 2))
                        for n in range(2):
                            r = slice(32 * n, 32 * n + 32)
                            op = dve.tensor_scalar(o_sb[r, b % 2, :], pb[6][r, n * D:(n + 1) * D], tot[r, :], None, ALU.mult)
                        op.then_inc(*vec_s.step(f"o{b}"))


_SCRATCH = dict(zT=(CMB, P, NT + 1), za=(NT, N_ATT), oT=(KD, P, NT), x1=(NT, D_MODEL), h2T=(KD, P, NT), aT=(FB, P, NT), oas=(TS, 512), bias=(8, P, BIAS_W))
_OUTS = dict(
    y_p=(SEQ, 1024), y_s=(TS, 1024), k_p=(SEQ, 128), v_p=(SEQ, 128), ki_p=(SEQ, 64), wkv_p=(4, 64, 64), shift_p=(1, 896),
    conv_p=(30, 256), ffn_p=(2, D_FF), k_s=(TS, 128), v_s=(TS, 128), ki_s=(TS, 64), wkv_s=(8, 4, 64, 64), shift_s=(8, 896),
    conv_s=(8, 30, 256), ffn_s=(8, 2, D_FF))
_PHASES = ("in", "rw", "cv", "ap", "as", "out", "up", "down")


def build(nc, t, phases):
    with ExitStack() as ctx:
        ident_t = ctx.enter_context(nc.sbuf_tensor("ident", [P, P], F32))
        made = ctx.enter_context(nc.semaphore("ident_made"))
        ident = ident_t[:, :]
        make_identity(nc, ident, made)
        if "in" in phases:
            project_in(nc, ident, t["x_prompt"], t["x_sample"], t["norm_mix"], t["w_in"], t["zT"], t["za"])
        if "rw" in phases:
            rwkv(nc, ident, t)
        if "cv" in phases:
            conv_mix(nc, ident, t)
        if "ap" in phases or "as" in phases:
            bias_table(nc, t)
        if "ap" in phases:
            attention_prompt(nc, ident, t)
        if "as" in phases:
            attention_sample(nc, ident, t)
        if "out" in phases:
            mix_out(nc, ident, t["oT"], t["x_prompt"], t["x_sample"], t["w_out"], t["norm_ffn"], t["x1"], t["h2T"])
        if "up" in phases:
            ffn_up(nc, t["h2T"], t["ffn_up"], t["ffn_conv_w"], t["ffn_conv_b"], t["state_ffn"], t["aT"], t["ffn_p"], t["ffn_s"])
        if "down" in phases:
            ffn_down(nc, ident, t["aT"], t["x1"], t["ffn_down"], t["ple_norm"], t["ple_gate"], t["ple_proj"], t["p_prompt"],
                     t["p_sample"], t["y_p"], t["y_s"])


def declare_and_build(nc, inputs, phases=_PHASES, given=None):
    given = given or {}
    views = dict(x_prompt=(SEQ, D_MODEL), x_sample=(TS, D_MODEL), p_prompt=(SEQ, D_PLE), p_sample=(TS, D_PLE))
    arrays, t = {}, {}
    for name, a in inputs.items():
        a = np.ascontiguousarray(a)
        if name in views:
            a = a.reshape(views[name])
        elif name in ("cache_k", "cache_v"):
            a = a.reshape(a.shape[1], PAGE, P)
        elif name not in ("rel_bias", "page_table"):
            a = a.reshape(a.shape[1:])
        arrays["in_" + name] = a
        t[name] = nc.dram_tensor("in_" + name, a.shape, mybir.dt.from_np(a.dtype), kind="ExternalInput").ap()
    for name, a in dict(bias_rows=bias_rows(), **sample_constants()).items():
        arrays[name] = a
        t[name] = nc.dram_tensor(name, a.shape, F32, kind="ExternalInput").ap()
    for name, shape in _OUTS.items():
        t[name] = nc.dram_tensor("out_" + name, shape, F32, kind="ExternalOutput").ap()
    for name, shape in _SCRATCH.items():
        kind = "ExternalInput" if name in given else "Internal"
        if name in given:
            arrays[name] = given[name]
        t[name] = nc.dram_tensor(name, shape, F32, kind=kind).ap()
    build(nc, t, phases)
    return arrays


def kernel(**inputs):
    import concourse.bacc as bacc
    from concourse.bass_utils import run_bass_kernel_spmd as run

    nc = bacc.Bacc("TRN2", target_bir_lowering=False, num_devices=1)
    arrays = declare_and_build(nc, inputs)
    got = run(nc, [arrays], core_ids=[0]).results[0]
    shapes = [(1, SEQ, 1024), (8, 8, 1024), (1, 1, SEQ, 2, 64), (1, 1, SEQ, 2, 64), (1, 1, SEQ, 64), (1, 1, 4, 64, 64), (1, 1, 896),
              (1, 1, 30, 256), (1, 1, 2, D_FF), (1, 8, 8, 2, 64), (1, 8, 8, 2, 64), (1, 8, 8, 64), (1, 8, 4, 64, 64), (1, 8, 896),
              (1, 8, 30, 256), (1, 8, 2, D_FF)]
    return tuple(np.asarray(got["out_" + n]).reshape(s) for n, s in zip(_OUTS, shapes))
```

```python
from contextlib import ExitStack

import numpy as np

import concourse.bass as bass
from concourse import mybir

F32 = mybir.dt.float32
F32R = mybir.dt.float32r
I32 = mybir.dt.int32
ALU = mybir.AluOpType
ACT = mybir.ActivationFunctionType
AX = mybir.AxisListType

P = 128
D_MODEL = 1024
KD = D_MODEL // P
SEQ = 2048
DEC_BATCH = 8
DEC_SEQ = 8
TS = DEC_BATCH * DEC_SEQ
NT = SEQ + TS
GROUP = 512
GROUPS = SEQ // GROUP
N_RWKV = 896
N_CONV = 512
N_CM = N_RWKV + N_CONV
CMB = N_CM // P
N_ATT = 1092
N_IN = N_CM + N_ATT
D_FF = 2816
FB = D_FF // P
D_PLE = 256
PAGE = 128
N_PAGES = 32
PAST = PAGE * N_PAGES
NORM_EPS = 1e-6
N_BUCKETS = 32
BIAS_W = 384


def wait_loop(engine, passed, sem, value):
    engine.wait_ge(sem, value)
    engine.sem_inc(passed, 1)


class Steps:

    def __init__(self, nc, ctx, name, names, unit=1, before=None):
        self.sem = ctx.enter_context(nc.semaphore(name)) if ctx else nc.alloc_semaphore(name)
        self.names, self.unit, self.before = list(names), unit, before
        self.ahead = 1 if unit == 1 and before is None else 0
        self.told = 0

    def open(self, engine):
        engine.sem_inc(self.sem, len(self.names))

    def step(self, name):
        want = self.names[self.told % len(self.names)]
        assert want == name, (name, want)
        self.told += 1
        return self.sem, self.unit

    def at(self, name, i):
        n = len(self.names) * self.unit
        return self.sem, i * n + (self.ahead * n + (self.names.index(name) + 1) * self.unit)

    def prev(self, name, i, iterations=0):
        if self.before is not None:
            return self.before.at(name, iterations - 1)
        n = len(self.names) * self.unit
        value = (self.ahead - 1) * n + (self.names.index(name) + 1) * self.unit
        assert value >= 0, name
        return self.sem, i * n + value


def make_identity(nc, ident, made):
    block = nc.Block()
    with block:
        @block.gpsimd
        def _(pool):
            pool.memset(ident, 0.0).then_inc(made, 1)
            pool.wait_ge(made, 1)
            pool.affine_select(out=ident, in_=ident, compare_op=ALU.not_equal, fill=1.0, base=0,
                               pattern=[[-1, P]], channel_multiplier=1).then_inc(made, 1)
            pool.wait_ge(made, 2)


def project_in(nc, ident, x_prompt, x_sample, norm_mix, w_in, zT, za):
    with ExitStack() as ctx:
        def sb(name, shape):
            return ctx.enter_context(nc.sbuf_tensor(name, shape, F32))

        w = sb("pi_w", [P, KD, N_IN])
        gain = sb("pi_gain", [P, D_MODEL])
        xt = sb("pi_x", [P, 4, D_MODEL])
        sq = sb("pi_sq", [P, D_MODEL])
        ss = sb("pi_ss", [P, 4])
        std = sb("pi_std", [P, 4])
        rstd = sb("pi_rstd", [P, 4])
        hn = sb("pi_hn", [P, 4, D_MODEL])
        hT = sb("pi_hT", [P, KD, GROUP])
        zc_sb = sb("pi_zc", [P, 2, GROUP])
        za_sb = sb("pi_za", [P, 2, N_ATT])
        eps = sb("pi_eps", [P, 1])
        zero = sb("pi_zero", [P, CMB])
        psT = ctx.enter_context(nc.psum_tensor("pi_psT", [P, 2, KD, P], F32))
        psz = ctx.enter_context(nc.psum_tensor("pi_psz", [P, 4, GROUP], F32))
        w_cols = [0, 4 * P, 8 * P, N_CM, N_IN]
        w_in_s = [nc.alloc_semaphore(f"pi_w_loaded{k}") for k in range(len(w_cols) - 1)]
        g_in = nc.alloc_semaphore("pi_gain_loaded")
        const = nc.alloc_semaphore("pi_constants")
        zs = nc.alloc_semaphore("pi_zero_stored")

        att_cols = [(0, 512), (512, 512), (1024, N_ATT - 1024)]

        def plan(tag, tokens, before):
            subs = [(s, min(P, tokens - s * P)) for s in range(-(-tokens // P))]
            evac = [f"zc{c}" for c in range(CMB)] + [f"za{s}_{j}" for s, _ in subs for j in range(3)]
            b = before or {}
            return dict(
                tokens=tokens, subs=subs, evac=evac,
                x=[Steps(nc, None, f"pi_x_loaded{tag}{s}", ["x"], 16, b["x"][s] if b else None) for s, _ in subs],
                act=Steps(nc, None, f"pi_act{tag}", [f"{k}{s}" for s, _ in subs for k in ("sq", "std")] + [f"hT{s}" for s, _ in subs], 1, b.get("act")),
                vec=Steps(nc, None, f"pi_vec{tag}", [f"{k}{s}" for s, _ in subs for k in ("rstd", "hn")] + evac, 1, b.get("vec")),
                pe=Steps(nc, None, f"pi_pe{tag}", [f"T{s}" for s, _ in subs] + evac, 1, b.get("pe")),
                zc=[Steps(nc, None, f"pi_zc_stored{tag}{k}", ["s"], 16, None) for k in range(2)],
                za=[Steps(nc, None, f"pi_za_stored{tag}{k}", ["s"], 16, None) for k in range(2)],
            )

        main = plan("", GROUP, None)
        tail = plan("t", TS, main)
        nzc = [(CMB + 1) // 2, CMB // 2]

        block = ctx.enter_context(nc.Block())

        @block.sync
        def _(sp):
            sp.dma_start(gain[:, :], norm_mix.partition_broadcast(P)).then_inc(g_in, 16)

            def loads(g, i, src):
                for s, n in g["subs"]:
                    sp.wait_ge(*g["vec"].prev(f"hn{s}", i, GROUPS))
                    sp.dma_start(xt[0:n, s, :], src(s, n)).then_inc(*g["x"][s].step("x"))

            loads(main, 0, lambda s, n: x_prompt[s * P:s * P + n, :])
            for piece, lo, hi in zip(w_in_s, w_cols, w_cols[1:]):
                sp.dma_start(w[:, :, lo:hi], w_in.rearrange("(k p) n -> p k n", p=P)[:, :, lo:hi]).then_inc(piece, 16)
            with sp.Fori(1, GROUPS) as i:
                loads(main, i, lambda s, n: x_prompt[bass.ds(i * GROUP + s * P, n), :])
            loads(tail, 0, lambda s, n: x_sample[0:n, :])

        @block.gpsimd
        def _(pool):
            pool.memset(eps[:, :], NORM_EPS).then_inc(const, 1)
            pool.memset(zero[:, :], 0.0).then_inc(const, 1)
            pool.wait_ge(const, 2)
            with nc.allow_non_contiguous_dma(reason="one column"):
                pool.dma_start(zT[:, :, 0:1].rearrange("b p o -> p b o"), zero[:, :].unsqueeze(2)).then_inc(zs, 16)

            def stores(g, i, tok):
                n = g["tokens"]
                for c in range(CMB):
                    pool.wait_ge(*g["vec"].at(f"zc{c}", i))
                    pool.dma_start(zT[c, :, bass.ds(tok + 1, n)], zc_sb[:, c % 2, 0:n]).then_inc(g["zc"][c % 2].sem, 16)
                for s, m in g["subs"]:
                    pool.wait_ge(*g["vec"].at(f"za{s}_2", i))
                    pool.dma_start(za[bass.ds(tok + s * P, m), :], za_sb[0:m, s % 2, :]).then_inc(g["za"][s % 2].sem, 16)

            with pool.Fori(0, GROUPS) as i:
                stores(main, i, i * GROUP)
            stores(tail, 0, SEQ)
            pool.wait_ge(zs, 16)
            for k in range(2):
                pool.wait_ge(main["zc"][k].sem, 16 * GROUPS * nzc[k])
                pool.wait_ge(tail["zc"][k].sem, 16 * nzc[k])
                pool.wait_ge(main["za"][k].sem, 16 * GROUPS * 2)
            pool.wait_ge(tail["za"][0].sem, 16)

        @block.scalar
        def _(act):
            act.wait_ge(const, 2)
            main["act"].open(act)

            def body(g, i):
                a = g["act"]
                for s, n in g["subs"]:
                    act.wait_ge(*g["x"][s].at("x", i))
                    act.activation(sq[0:n, :], xt[0:n, s, :], ACT.Square, accum_out=ss[0:n, s:s + 1]).then_inc(*a.step(f"sq{s}"))
                    act.wait_ge(*a.at(f"sq{s}", i))
                    act.activation(std[0:n, s:s + 1], ss[0:n, s:s + 1], ACT.Sqrt, scale=1.0 / D_MODEL, bias=eps[0:n, :]).then_inc(*a.step(f"std{s}"))
                for s, n in g["subs"]:
                    act.wait_ge(*g["pe"].at(f"T{s}", i))
                    act.wait_ge(*g["pe"].prev(main["evac"][-1], i, GROUPS))
                    act.activation(hT[:, :, s * P:s * P + n], psT[:, s % 2, :, 0:n], ACT.Copy).then_inc(*a.step(f"hT{s}"))

            with act.Fori(0, GROUPS) as i:
                body(main, i)
            body(tail, 0)

        @block.tensor
        def _(pe):
            main["pe"].open(pe)

            def body(g, i):
                n_tok, t, v, a = g["tokens"], g["pe"], g["vec"], g["act"]
                for s, n in g["subs"]:
                    pe.wait_ge(*v.at(f"hn{s}", i))
                    if s >= 2:
                        pe.wait_ge(*a.at(f"hT{s - 2}", i))
                    else:
                        pe.wait_ge(*a.prev(f"hT{s + 2}", i, GROUPS))
                    for k in range(KD):
                        mm = pe.transpose(psT[:, s % 2, k, 0:n], hn[0:n, s, k * P:(k + 1) * P], ident[0:n, 0:n])
                    mm.then_inc(*t.step(f"T{s}"))
                pe.wait_ge(*a.at(f"hT{g['subs'][-1][0]}", i))
                for u, name in enumerate(g["evac"]):
                    bank = u % 4
                    if u * P in w_cols:
                        pe.wait_ge(w_in_s[w_cols.index(u * P)], 16)
                    if u >= 4:
                        pe.wait_ge(*v.at(g["evac"][u - 4], i))
                    else:
                        last = max(x for x in range(len(main["evac"])) if x % 4 == bank)
                        pe.wait_ge(*v.prev(main["evac"][last], i, GROUPS))
                    if name.startswith("zc"):
                        c = int(name[2:])
                        for k in range(KD):
                            mm = pe.matmul(psz[:, bank, 0:n_tok], w[:, k, c * P:(c + 1) * P], hT[:, k, 0:n_tok], start=(k == 0), stop=(k == KD - 1))
                    else:
                        s, j = map(int, name[2:].split("_"))
                        at, m = att_cols[j]
                        n = g["subs"][s][1]
                        for k in range(KD):
                            mm = pe.matmul(psz[0:n, bank, 0:m], hT[:, k, s * P:s * P + n], w[:, k, N_CM + at:N_CM + at + m], start=(k == 0), stop=(k == KD - 1))
                    mm.then_inc(*t.step(name))

            with pe.Fori(0, GROUPS) as i:
                body(main, i)
            body(tail, 0)

        @block.vector
        def _(dve):
            dve.wait_ge(g_in, 16)
            main["vec"].open(dve)

            def body(g, i, stored):
                n_tok, v, a = g["tokens"], g["vec"], g["act"]
                for s, n in g["subs"]:
                    dve.wait_ge(*a.at(f"std{s}", i))
                    dve.reciprocal(rstd[0:n, s:s + 1], std[0:n, s:s + 1]).then_inc(*v.step(f"rstd{s}"))
                    dve.wait_ge(*v.at(f"rstd{s}", i))
                    dve.wait_ge(*g["pe"].prev(f"T{s}", i, GROUPS))
                    dve.scalar_tensor_tensor(out=hn[0:n, s, :], in0=xt[0:n, s, :], scalar=rstd[0:n, s:s + 1], in1=gain[0:n, :],
                                             op0=ALU.mult, op1=ALU.mult).then_inc(*v.step(f"hn{s}"))
                for u, name in enumerate(g["evac"]):
                    bank = u % 4
                    dve.wait_ge(*g["pe"].at(name, i))
                    if name.startswith("zc"):
                        c = int(name[2:])
                        dve.wait_ge(*stored("zc", c % 2, c // 2))
                        dve.tensor_copy(zc_sb[:, c % 2, 0:n_tok], psz[:, bank, 0:n_tok]).then_inc(*v.step(name))
                    else:
                        s, j = map(int, name[2:].split("_"))
                        at, m = att_cols[j]
                        n = g["subs"][s][1]
                        if j == 0:
                            dve.wait_ge(*stored("za", s % 2, s // 2))
                        dve.tensor_copy(za_sb[0:n, s % 2, at:at + m], psz[0:n, bank, 0:m]).then_inc(*v.step(name))

            with dve.Fori(0, GROUPS) as i:
                per = dict(zc=nzc, za=[2, 2])
                body(main, i, lambda kind, k, j: (main[kind][k].sem, i * (16 * per[kind][k]) + 16 * j))

            def tail_stored(kind, k, j):
                per = dict(zc=nzc, za=[2, 2])
                if j == 0:
                    return main[kind][k].sem, 16 * GROUPS * per[kind][k]
                return tail[kind][k].sem, 16 * j
            body(tail, 0, tail_stored)


def mix_out(nc, ident, w_out, oT, x_prompt, x_sample, norm_ffn, x1, h2T):
    with ExitStack() as ctx:
        def sb(name, shape):
            return ctx.enter_context(nc.sbuf_tensor(name, shape, F32))

        w = sb("mo_w", [P, KD, D_MODEL])
        gain = sb("mo_gain", [P, D_MODEL])
        o_sb = sb("mo_o", [P, 2, KD, P])
        xt = sb("mo_x", [P, 2, D_MODEL])
        x1_sb = sb("mo_x1", [P, 2, D_MODEL])
        sq = sb("mo_sq", [P, D_MODEL])
        ss = sb("mo_ss", [P, 2])
        std = sb("mo_std", [P, 2])
        rstd = sb("mo_rstd", [P, 2])
        hn = sb("mo_hn", [P, 2, D_MODEL])
        hT = sb("mo_hT", [P, 2, KD, P])
        eps = sb("mo_eps", [P, 1])
        psm = ctx.enter_context(nc.psum_tensor("mo_psm", [P, 2, 2, 512], F32))
        psT = ctx.enter_context(nc.psum_tensor("mo_psT", [P, 2, KD, P], F32))
        pieces = [(k, k + 2) for k in range(0, KD, 2)]
        w_ld = [ctx.enter_context(nc.semaphore(f"mo_w_loaded{k}")) for k, _ in enumerate(pieces)]
        gain_ld = ctx.enter_context(nc.semaphore("mo_gain_loaded"))
        passed = ctx.enter_context(nc.semaphore("mo_waits_passed"))
        const = ctx.enter_context(nc.semaphore("mo_constants"))
        PAIRS = SEQ // P // 2

        def plan(tag, subs, before):
            b = before or {}
            st = lambda k, names, unit=1: Steps(nc, ctx, f"mo_{k}{tag}", names, unit, b.get(k))
            return dict(
                subs=subs,
                **{f"x{s}": st(f"x{s}", ["x", "o"], 16) for s, _ in subs},
                **{f"x1s{s}": st(f"x1s{s}", ["x1"], 16) for s, _ in subs},
                **{f"hs{s}": st(f"hs{s}", ["h"], 16) for s, _ in subs},
                pe=st("pe", [f"M{s}" for s, _ in subs] + [f"T{s}" for s, _ in subs]),
                act=st("act", [f"{k}{s}" for s, _ in subs for k in ("sq", "std")] + [f"hT{s}" for s, _ in subs]),
                vec=st("vec", [f"{k}{s}" for s, _ in subs for k in ("x1", "rstd", "hn")]),
            )

        main = plan("", [(0, P), (1, P)], None)
        tail = plan("t", [(0, TS)], main)
        block = ctx.enter_context(nc.Block())

        @block.sync
        def _(sp):
            FIRST = None

            def load_weights():
                for (lo, hi), sem in zip(pieces, w_ld):
                    sp.dma_start(w[:, lo:hi, :], w_out.rearrange("(k p) n -> p k n", p=P)[:, lo:hi, :]).then_inc(sem, 16)
                sp.dma_start(gain[:, :], norm_ffn.partition_broadcast(P)).then_inc(gain_ld, 16)

            def body(g, i, xsrc, tok):
                for s, n in g["subs"]:
                    src_o = oT[:, :, bass.ds(tok(s), n)].rearrange("k p t -> p k t")
                    src_x = xsrc(s, n)
                    if i is not FIRST:
                        wait_loop(sp, passed, *g["vec"].prev(f"x1{s}", i, PAIRS))
                    sp.dma_start(xt[0:n, s, :], src_x).then_inc(*g[f"x{s}"].step("x"))
                    if i is not FIRST:
                        wait_loop(sp, passed, *g["pe"].prev(f"M{s}", i, PAIRS))
                    sp.dma_start(o_sb[:, s, :, 0:n], src_o).then_inc(*g[f"x{s}"].step("o"))
                    if i is FIRST and s == 0:
                        load_weights()

            body(main, FIRST, lambda s, n: x_prompt[s * P:s * P + n, :], lambda s: s * P)
            with sp.Fori(1, PAIRS) as i:
                at = [sp.snap(i * 256 + s * P) for s in range(2)]
                body(main, i, lambda s, n: x_prompt[bass.ds(at[s], n), :], lambda s: at[s])
            body(tail, 0, lambda s, n: x_sample[0:n, :], lambda s: SEQ)

        @block.gpsimd
        def _(pool):
            pool.memset(eps[:, :], NORM_EPS).then_inc(const, 1)

            def body(g, i, tok):
                for s, n in g["subs"]:
                    pool.wait_ge(*g["vec"].at(f"x1{s}", i))
                    pool.dma_start(x1[bass.ds(tok + s * P, n), :], x1_sb[0:n, s, :]).then_inc(*g[f"x1s{s}"].step("x1"))
                    pool.wait_ge(*g["act"].at(f"hT{s}", i))
                    pool.dma_start(h2T[:, :, bass.ds(tok + s * P, n)].rearrange("k p t -> p k t"), hT[:, s, :, 0:n]).then_inc(*g[f"hs{s}"].step("h"))

            with pool.Fori(0, PAIRS) as i:
                body(main, i, i * 256)
            body(tail, 0, SEQ)
            for g, n in ((main, PAIRS), (tail, 1)):
                for s, _ in g["subs"]:
                    pool.wait_ge(*g[f"x1s{s}"].at("x1", n - 1))
                    pool.wait_ge(*g[f"hs{s}"].at("h", n - 1))

        @block.tensor
        def _(pe):
            main["pe"].open(pe)

            def body(g, i):
                for s, n in g["subs"]:
                    pe.wait_ge(*g[f"x{s}"].at("o", i))
                    pe.wait_ge(*g["vec"].prev(f"x1{s}", i, PAIRS))
                    for k in range(KD):
                        for (lo, _), sem in zip(pieces, w_ld):
                            if k == lo and s == 0:
                                pe.wait_ge(sem, 16)
                        for c in range(2):
                            mm = pe.matmul(psm[0:n, s, c, :], o_sb[:, s, k, 0:n], w[:, k, c * 512:(c + 1) * 512], start=(k == 0), stop=(k == KD - 1))
                    mm.then_inc(*g["pe"].step(f"M{s}"))
                for s, n in g["subs"]:
                    pe.wait_ge(*g["vec"].at(f"hn{s}", i))
                    pe.wait_ge(*g["act"].prev(f"hT{s}", i, PAIRS))
                    for k in range(KD):
                        mm = pe.transpose(psT[:, s, k, 0:n], hn[0:n, s, k * P:(k + 1) * P], ident[0:n, 0:n])
                    mm.then_inc(*g["pe"].step(f"T{s}"))

            with pe.Fori(0, PAIRS) as i:
                body(main, i)
            body(tail, 0)

        @block.scalar
        def _(act):
            main["act"].open(act)
            act.wait_ge(const, 1)

            def body(g, i):
                a = g["act"]
                for s, n in g["subs"]:
                    act.wait_ge(*g["vec"].at(f"x1{s}", i))
                    act.activation(sq[0:n, :], x1_sb[0:n, s, :], ACT.Square, accum_out=ss[0:n, s:s + 1]).then_inc(*a.step(f"sq{s}"))
                    act.wait_ge(*a.at(f"sq{s}", i))
                    act.activation(std[0:n, s:s + 1], ss[0:n, s:s + 1], ACT.Sqrt, scale=1.0 / D_MODEL, bias=eps[0:n, :]).then_inc(*a.step(f"std{s}"))
                for s, n in g["subs"]:
                    act.wait_ge(*g["pe"].at(f"T{s}", i))
                    act.wait_ge(*g[f"hs{s}"].prev("h", i, PAIRS))
                    act.activation(hT[:, s, :, 0:n], psT[:, s, :, 0:n], ACT.Copy).then_inc(*a.step(f"hT{s}"))

            with act.Fori(0, PAIRS) as i:
                body(main, i)
            body(tail, 0)

        @block.vector
        def _(dve):
            main["vec"].open(dve)
            dve.wait_ge(gain_ld, 16)

            def body(g, i):
                v = g["vec"]
                for s, n in g["subs"]:
                    dve.wait_ge(*g["pe"].at(f"M{s}", i))
                    dve.wait_ge(*g[f"x{s}"].at("o", i))
                    dve.wait_ge(*g[f"x1s{s}"].prev("x1", i, PAIRS))
                    dve.wait_ge(*g["act"].prev(f"sq{s}", i, PAIRS))
                    dve.tensor_tensor(x1_sb[0:n, s, :], psm[0:n, s, :, :].rearrange("p a b -> p (a b)"), xt[0:n, s, :], ALU.add).then_inc(*v.step(f"x1{s}"))
                    dve.wait_ge(*g["act"].at(f"std{s}", i))
                    dve.reciprocal(rstd[0:n, s:s + 1], std[0:n, s:s + 1]).then_inc(*v.step(f"rstd{s}"))
                    dve.wait_ge(*v.at(f"rstd{s}", i))
                    dve.wait_ge(*g["pe"].prev(f"T{s}", i, PAIRS))
                    dve.scalar_tensor_tensor(out=hn[0:n, s, :], in0=x1_sb[0:n, s, :], scalar=rstd[0:n, s:s + 1], in1=gain[0:n, :],
                                             op0=ALU.mult, op1=ALU.mult).then_inc(*v.step(f"hn{s}"))

            with dve.Fori(0, PAIRS) as i:
                body(main, i)
            body(tail, 0)


def ffn_up(nc, h2T, up, conv_w, conv_b, state_ffn, aT, ffn_p, ffn_s):
    with ExitStack() as ctx:
        def sb(name, shape):
            return ctx.enter_context(nc.sbuf_tensor(name, shape, F32))

        W1 = DEC_SEQ + 2
        h_hi = ctx.enter_context(nc.sbuf_tensor("fu_h_hi", [P, KD, NT], F32R))
        h_lo = ctx.enter_context(nc.sbuf_tensor("fu_h_lo", [P, KD, NT], F32R))
        w_hi = ctx.enter_context(nc.sbuf_tensor("fu_w_hi", [P, 2, 2, KD, P], F32R))
        w_lo = ctx.enter_context(nc.sbuf_tensor("fu_w_lo", [P, 2, 2, KD, P], F32R))
        w_raw = sb("fu_w_raw", [P, 2, KD, P])
        cw = sb("fu_cw", [P, 2, 4])
        gpre = sb("fu_gpre", [P, 2, SEQ + 2])
        gprs = sb("fu_gprs", [P, 2, DEC_BATCH, W1])
        gate = sb("fu_gate", [P, 2, NT])
        h_raw = [x[:, :, :].rearrange("p b t -> p (b t)")[:, 0:KD * 512].rearrange("p (k t) -> p k t", k=KD) for x in (gpre, gate)]
        ps = ctx.enter_context(nc.psum_tensor("fu_ps", [P, 8, 512], F32))
        h_ld = [ctx.enter_context(nc.semaphore(f"fu_h_loaded{g}")) for g in range(5)]
        const = ctx.enter_context(nc.semaphore("fu_constants"))
        passed = ctx.enter_context(nc.semaphore("fu_waits_passed"))
        groups = [(g * 512, 512) for g in range(4)] + [(SEQ, TS)]
        PAIRS = FB // 2
        uses = [(b, kind, g) for b in range(2) for kind in ("g", "v") for g in range(5)]
        bank_of = {u: n % 8 for n, u in enumerate(uses)}
        order = [f"{k}{b}{g}" for b, k, g in uses]

        def before_of(n):
            same = [m for m in range(len(uses)) if m % 8 == n % 8]
            at = same.index(n)
            return (order[same[at - 1]], at == 0)

        pe_s = Steps(nc, ctx, "fu_pe", order)
        act_s = Steps(nc, ctx, "fu_act", [x for b in range(2) for x in [f"g{b}{g}" for g in range(5)] + [f"gelu{b}"]])
        vec_s = Steps(nc, ctx, "fu_vec", [x for b in range(2) for x in [f"c{b}{j}" for j in range(6)] + [f"v{b}{g}" for g in range(5)]])
        w_s = [Steps(nc, ctx, f"fu_w_loaded{b}", ["w"], 16 * 6) for b in range(2)]
        for s in w_s:
            s.ahead = 0
        a_s = [Steps(nc, ctx, f"fu_a_stored{b}", ["a"], 16) for b in range(2)]
        hi_s = Steps(nc, ctx, "fu_w_high", ["0", "1"])
        lo_s = Steps(nc, ctx, "fu_w_low", ["0", "1"])
        h_hi_s = Steps(nc, ctx, "fu_h_high", [str(g) for g in range(5)])
        h_lo_s = Steps(nc, ctx, "fu_h_low", [str(g) for g in range(5)])
        for s in (hi_s, lo_s, h_hi_s, h_lo_s):
            s.ahead = 0
        f_s = [Steps(nc, ctx, f"fu_state_stored{b}", ["f"], 48) for b in range(2)]
        for s in f_s:
            s.ahead = 0
        block = ctx.enter_context(nc.Block())

        @block.sync
        def _(sp):
            def load_h(g):
                at, n = groups[g]
                if g >= 2:
                    sp.wait_ge(*h_lo_s.at(str(g - 2), 0))
                sp.dma_start(h_raw[g % 2][:, :, 0:n], h2T[:, :, at:at + n].rearrange("k p t -> p k t")).then_inc(h_ld[g], 16)

            up_k = up.rearrange("(k p) n -> p k n", p=P)

            def load_block(b, at, at_v, i):
                if b or i is not None:
                    wait_loop(sp, passed, *(lo_s.at("0", 0 if i is None else i) if b else lo_s.prev("1", i)))
                if i is not None:
                    wait_loop(sp, passed, *pe_s.prev(f"v{b}4", i))
                    wait_loop(sp, passed, *vec_s.prev(f"c{b}5", i))
                sp.dma_start(w_raw[:, 0, :, :], up_k[:, :, bass.ds(at, P)]).then_inc(w_s[b].sem, 16)
                sp.dma_start(w_raw[:, 1, :, :], up_k[:, :, bass.ds(at_v, P)]).then_inc(w_s[b].sem, 16)
                sp.dma_start(cw[:, b, 0:3], conv_w[:, bass.ds(at, P)].rearrange("w c -> c w")).then_inc(w_s[b].sem, 16)
                sp.dma_start(cw[:, b, 3:4], conv_b[bass.ds(at, P)].unsqueeze(1)).then_inc(w_s[b].sem, 16)
                if i is not None:
                    sp.wait_ge(*f_s[b].prev("f", i))
                for j in range(2):
                    sp.dma_start(gprs[:, b, :, j], state_ffn[:, j, bass.ds(at, P)].rearrange("b c -> c b")).then_inc(w_s[b].sem, 16)

            with nc.allow_non_contiguous_dma(reason="channel-major taps and states"):
                load_block(0, 0, D_FF, None)
                for g in range(5):
                    load_h(g)
                load_block(1, P, D_FF + P, None)
                with sp.Fori(1, PAIRS) as i:
                    at_b = [sp.snap(i * 256 + b * P) for b in range(2)]
                    at_v = [sp.snap(i * 256 + (b * P + D_FF)) for b in range(2)]
                    for b in range(2):
                        load_block(b, at_b[b], at_v[b], i)

        @block.gpsimd
        def _(pool):
            pool.wait_ge(*h_lo_s.at("4", 0))
            pool.memset(gpre[:, :, 0:2], 0.0).then_inc(const, 1)
            with nc.allow_non_contiguous_dma(reason="channel-major states"), pool.Fori(0, PAIRS) as i:
                for b in range(2):
                    at = i * 256 + b * P
                    pool.wait_ge(*act_s.at(f"g{b}4", i))
                    pool.dma_start(ffn_p[:, bass.ds(at, P)].rearrange("w c -> c w"), gpre[:, b, SEQ:SEQ + 2]).then_inc(f_s[b].sem, 16)
                    for j in range(2):
                        pool.dma_start(ffn_s[:, j, bass.ds(at, P)].rearrange("b c -> c b"), gprs[:, b, :, DEC_SEQ + j]).then_inc(f_s[b].sem, 16)
                    pool.wait_ge(*vec_s.at(f"v{b}4", i))
                    pool.dma_start(aT[bass.ds(i * 2 + b, 1), :, :].rearrange("o p t -> (o p) t"), gate[:, b, :]).then_inc(*a_s[b].step("a"))
            for b in range(2):
                pool.wait_ge(*a_s[b].at("a", PAIRS - 1))
                pool.wait_ge(*f_s[b].at("f", PAIRS - 1))

        @block.tensor
        def _(pe):
            pe_s.open(pe)
            with pe.Fori(0, PAIRS) as i:
                for n, (b, kind, g) in enumerate(uses):
                    if kind == "g" and g == 0:
                        pe.wait_ge(*lo_s.at(str(b), i))
                    if kind == "g" and b == 0:
                        pe.wait_ge(*h_lo_s.at(str(g), 0))
                    last, earlier = before_of(n)
                    reader = act_s if last[0] == "g" else vec_s
                    pe.wait_ge(*(reader.prev(last, i) if earlier else reader.at(last, i)))
                    at, m = groups[g]
                    q = 0 if kind == "g" else 1
                    out = ps[:, bank_of[b, kind, g], 0:m]
                    for k in range(KD):
                        wh, wl = w_hi[:, b, q, k, :], w_lo[:, b, q, k, :]
                        hh, hl = h_hi[:, k, at:at + m], h_lo[:, k, at:at + m]
                        pe.matmul(out, wl, hh, start=(k == 0), stop=False)
                        pe.matmul(out, wh, hl, start=False, stop=False)
                        mm = pe.matmul(out, wh, hh, start=False, stop=(k == KD - 1))
                    mm.then_inc(*pe_s.step(order[n]))

        @block.scalar
        def _(act):
            act_s.open(act)

            def high(b, i):
                act.wait_ge(*w_s[b].at("w", i))
                act.activation(w_hi[:, b, :, :, :].rearrange("p q k c -> p (q k c)"), w_raw[:, :, :, :].rearrange("p q k c -> p (q k c)"), ACT.Copy).then_inc(*hi_s.step(str(b)))

            high(0, 0)
            for g, (at, m) in enumerate(groups):
                act.wait_ge(h_ld[g], 16)
                act.activation(h_hi[:, :, at:at + m], h_raw[g % 2][:, :, 0:m], ACT.Copy).then_inc(*h_hi_s.step(str(g)))
            act.wait_ge(const, 1)

            def body(i, last):
                for b in range(2):
                    act.wait_ge(*vec_s.prev(f"c{b}5", i))
                    act.wait_ge(*f_s[b].prev("f", i))
                    for g in range(5):
                        act.wait_ge(*pe_s.at(f"g{b}{g}", i))
                        src = ps[:, bank_of[b, "g", g], 0:groups[g][1]]
                        if g < 4:
                            dst = gpre[:, b, 2 + g * 512:2 + (g + 1) * 512]
                        else:
                            dst, src = gprs[:, b, :, 2:W1], src.rearrange("p (b t) -> p b t", t=DEC_SEQ)
                        act.activation(dst, src, ACT.Copy).then_inc(*act_s.step(f"g{b}{g}"))
                    act.wait_ge(*vec_s.at(f"c{b}5", i))
                    act.activation(gate[:, b, :], gate[:, b, :], ACT.Gelu).then_inc(*act_s.step(f"gelu{b}"))
                    if b == 0:
                        high(1, i)
                    elif not last:
                        high(0, i + 1)

            with act.Fori(0, PAIRS - 1) as i:
                body(i, False)
            body(PAIRS - 1, True)

        @block.vector
        def _(dve):
            vec_s.open(dve)

            def low(b, i):
                dve.wait_ge(*hi_s.at(str(b), i))
                flat = lambda x: x[:, b, :, :, :].rearrange("p q k c -> p (q k c)")
                dve.tensor_tensor(flat(w_lo), w_raw[:, :, :, :].rearrange("p q k c -> p (q k c)"), flat(w_hi).bitcast(F32), ALU.subtract).then_inc(*lo_s.step(str(b)))

            low(0, 0)
            for g, (at, m) in enumerate(groups):
                dve.wait_ge(*h_hi_s.at(str(g), 0))
                dve.tensor_tensor(h_lo[:, :, at:at + m], h_raw[g % 2][:, :, 0:m], h_hi[:, :, at:at + m].bitcast(F32), ALU.subtract).then_inc(*h_lo_s.step(str(g)))

            def body(i, last):
                for b in range(2):
                    dve.wait_ge(*w_s[b].at("w", i))
                    dve.wait_ge(*act_s.at(f"g{b}4", i))
                    dve.wait_ge(*vec_s.prev(f"v{b}4", i))
                    dve.wait_ge(*a_s[b].prev("a", i))
                    tap = lambda j: cw[:, b, j:j + 1]
                    parts = [(gate[:, b, 0:SEQ], lambda j: gpre[:, b, j:j + SEQ]),
                             (gate[:, b, SEQ:NT].rearrange("p (b t) -> p b t", t=DEC_SEQ), lambda j: gprs[:, b, :, j:j + DEC_SEQ])]
                    for j in range(3):
                        for q, (out, src) in enumerate(parts):
                            if j == 0:
                                op = dve.tensor_scalar(out, src(0), tap(0), tap(3), ALU.mult, ALU.add)
                            else:
                                dve.wait_ge(*vec_s.at(f"c{b}{2 * j + q - 2}", i))
                                op = dve.scalar_tensor_tensor(out=out, in0=src(j), scalar=tap(j), in1=out, op0=ALU.mult, op1=ALU.add)
                            op.then_inc(*vec_s.step(f"c{b}{2 * j + q}"))
                    dve.wait_ge(*act_s.at(f"gelu{b}", i))
                    for g, (at, m) in enumerate(groups):
                        dve.wait_ge(*pe_s.at(f"v{b}{g}", i))
                        if g == 3:
                            if b == 0:
                                low(1, i)
                            elif not last:
                                low(0, i + 1)
                        dve.tensor_tensor(gate[:, b, at:at + m], ps[:, bank_of[b, "v", g], 0:m], gate[:, b, at:at + m], ALU.mult).then_inc(*vec_s.step(f"v{b}{g}"))

            with dve.Fori(0, PAIRS - 1) as i:
                body(i, False)
            body(PAIRS - 1, True)


def ffn_down(nc, ident, aT, x1, down, ple_norm, ple_gate, ple_proj, p_prompt, p_sample, y_p, y_s):
    with ExitStack() as ctx:
        def sb(name, shape):
            return ctx.enter_context(nc.sbuf_tensor(name, shape, F32))

        KP = D_PLE // P
        w = sb("fd_w", [P, FB, D_MODEL])
        pieces = [(k, min(k + 4, FB)) for k in [0, 2] + list(range(4, FB, 4))]
        pieces = [(lo, min([hi] + [x for x, _ in pieces if x > lo])) for lo, hi in pieces]
        wg = sb("fd_wg", [P, KD, D_MODEL])
        wp = sb("fd_wp", [P, KP, D_MODEL])
        gain = sb("fd_gain", [P, D_MODEL])
        a_sb = sb("fd_a", [P, 2, FB, P])
        pt = sb("fd_p", [P, 2, D_PLE])
        pT = sb("fd_pT", [P, KP, P])
        x2 = sb("fd_x2", [P, 2, D_MODEL])
        sg = sb("fd_sg", [P, D_MODEL])
        ss = sb("fd_ss", [P, 2])
        std = sb("fd_std", [P, 2])
        rstd = sb("fd_rstd", [P, 2])
        hn = sb("fd_hn", [P, 2, D_MODEL])
        hT = sb("fd_hT", [P, KD, P])
        eps = sb("fd_eps", [P, 1])
        psf = ctx.enter_context(nc.psum_tensor("fd_psf", [P, 2, 2, 512], F32))
        psT = ctx.enter_context(nc.psum_tensor("fd_psT", [P, KD, P], F32))
        psg = ctx.enter_context(nc.psum_tensor("fd_psg", [P, 2, 512], F32))
        psl = psT[:, :, :].rearrange("p (c k) t -> p c (k t)", c=2)
        const = ctx.enter_context(nc.semaphore("fd_constants"))
        w_ld = [ctx.enter_context(nc.semaphore(f"fd_w_loaded{k}")) for k, _ in enumerate(pieces)]
        ple_ld = ctx.enter_context(nc.semaphore("fd_ple_loaded"))
        passed = ctx.enter_context(nc.semaphore("fd_waits_passed"))
        PAIRS = SEQ // P // 2

        def plan(tag, subs, before):
            b = before or {}
            st = lambda k, names, unit=1: Steps(nc, ctx, f"fd_{k}{tag}", names, unit, b.get(k))
            return dict(
                subs=subs,
                **{f"a{s}": st(f"a{s}", ["a"], 16) for s, _ in subs},
                **{f"x{s}": st(f"x{s}", ["x"], 16) for s, _ in subs},
                **{f"p{s}": st(f"p{s}", ["p"], 16) for s, _ in subs},
                **{f"y{s}": st(f"y{s}", ["y"], 16) for s, _ in subs},
                pe=st("pe", [f"F{s}" for s, _ in subs] + [f"{k}{s}" for s, _ in subs for k in ("P", "T", "G", "L")]),
                act=st("act", [f"{k}{s}" for s, _ in subs for k in ("sq", "std")] + [f"{k}{s}" for s, _ in subs for k in ("pT", "hT", "sg")]),
                vec=st("vec", [f"{k}{s}" for s, _ in subs for k in ("x2", "rstd", "hn")] + [f"{k}{s}" for s, _ in subs for k in ("m", "y")]),
            )

        main = plan("", [(0, P), (1, P)], None)
        tail = plan("t", [(0, TS)], main)
        block = ctx.enter_context(nc.Block())

        @block.sync
        def _(sp):
            def load_weights():
                for (lo, hi), sem in zip(pieces, w_ld):
                    sp.dma_start(w[:, lo:hi, :], down.rearrange("(k p) n -> p k n", p=P)[:, lo:hi, :]).then_inc(sem, 16)
                sp.dma_start(gain[:, :], ple_norm.partition_broadcast(P)).then_inc(ple_ld, 16)
                sp.dma_start(wg[:, :, :], ple_gate.rearrange("(k p) n -> p k n", p=P)).then_inc(ple_ld, 16)
                sp.dma_start(wp[:, :, :], ple_proj.rearrange("(k p) n -> p k n", p=P)).then_inc(ple_ld, 16)

            FIRST = None

            def body(g, i, tok, psrc):
                for s, n in g["subs"]:
                    src_a = aT[:, :, bass.ds(tok(s), n)].rearrange("k p t -> p k t")
                    src_p, src_x = psrc(s, n), x1[bass.ds(tok(s), n), :]
                    if i is not FIRST:
                        wait_loop(sp, passed, *g["pe"].prev(f"F{s}", i, PAIRS))
                    sp.dma_start(a_sb[:, s, :, 0:n], src_a).then_inc(*g[f"a{s}"].step("a"))
                    if i is FIRST and s == 0:
                        load_weights()
                    if i is not FIRST:
                        wait_loop(sp, passed, *g["pe"].prev(f"P{s}", i, PAIRS))
                    sp.dma_start(pt[0:n, s, :], src_p).then_inc(*g[f"p{s}"].step("p"))
                    if i is not FIRST:
                        sp.wait_ge(*g[f"y{s}"].prev("y", i, PAIRS))
                    sp.dma_start(x2[0:n, s, :], src_x).then_inc(*g[f"x{s}"].step("x"))

            body(main, FIRST, lambda s: s * P, lambda s, n: p_prompt[s * P:s * P + n, :])
            with sp.Fori(1, PAIRS) as i:
                at = [sp.snap(i * 256 + s * P) for s in range(2)]
                body(main, i, lambda s: at[s], lambda s, n: p_prompt[bass.ds(at[s], n), :])
            body(tail, 0, lambda s: SEQ, lambda s, n: p_sample[0:n, :])

        @block.gpsimd
        def _(pool):
            pool.memset(eps[:, :], NORM_EPS).then_inc(const, 1)

            def body(g, i, dst):
                for s, n in g["subs"]:
                    pool.wait_ge(*g["vec"].at(f"y{s}", i))
                    pool.dma_start(dst(s, n), x2[0:n, s, :]).then_inc(*g[f"y{s}"].step("y"))

            with pool.Fori(0, PAIRS) as i:
                body(main, i, lambda s, n: y_p[bass.ds(i * 256 + s * P, n), :])
            body(tail, 0, lambda s, n: y_s[0:n, :])
            for g, n in ((main, PAIRS), (tail, 1)):
                for s, _ in g["subs"]:
                    pool.wait_ge(*g[f"y{s}"].at("y", n - 1))

        @block.tensor
        def _(pe):
            main["pe"].open(pe)

            def body(g, i):
                t, v, a = g["pe"], g["vec"], g["act"]
                for s, n in g["subs"]:
                    pe.wait_ge(*g[f"a{s}"].at("a", i))
                    pe.wait_ge(*v.prev(f"x2{s}", i, PAIRS))
                    for k in range(FB):
                        for (lo, _), sem in zip(pieces, w_ld):
                            if k == lo and s == 0:
                                pe.wait_ge(sem, 16)
                        for c in range(2):
                            mm = pe.matmul(psf[0:n, s, c, :], a_sb[:, s, k, 0:n], w[:, k, c * 512:(c + 1) * 512], start=(k == 0), stop=(k == FB - 1))
                    mm.then_inc(*t.step(f"F{s}"))
                for s, n in g["subs"]:
                    last = g["subs"][-1][0] if s else None
                    pe.wait_ge(*g[f"p{s}"].at("p", i))
                    pe.wait_ge(*(v.at("m0", i) if s else v.prev("m1", i, PAIRS)))
                    for k in range(KP):
                        mm = pe.transpose(psT[:, k, 0:n], pt[0:n, s, k * P:(k + 1) * P], ident[0:n, 0:n])
                    mm.then_inc(*t.step(f"P{s}"))
                    pe.wait_ge(*v.at(f"hn{s}", i))
                    pe.wait_ge(*a.at(f"pT{s}", i))
                    for k in range(KD):
                        mm = pe.transpose(psT[:, k, 0:n], hn[0:n, s, k * P:(k + 1) * P], ident[0:n, 0:n])
                    mm.then_inc(*t.step(f"T{s}"))
                    pe.wait_ge(*a.at(f"hT{s}", i))
                    pe.wait_ge(*(a.at("sg0", i) if s else a.prev("sg1", i, PAIRS)))
                    pe.wait_ge(ple_ld, 48)
                    for c in range(2):
                        for k in range(KD):
                            mm = pe.matmul(psg[0:n, c, :], hT[:, k, 0:n], wg[:, k, c * 512:(c + 1) * 512], start=(k == 0), stop=(k == KD - 1))
                    mm.then_inc(*t.step(f"G{s}"))
                    for c in range(2):
                        for k in range(KP):
                            mm = pe.matmul(psl[0:n, c, :], pT[:, k, 0:n], wp[:, k, c * 512:(c + 1) * 512], start=(k == 0), stop=(k == KP - 1))
                    mm.then_inc(*t.step(f"L{s}"))

            with pe.Fori(0, PAIRS) as i:
                body(main, i)
            body(tail, 0)

        @block.scalar
        def _(act):
            main["act"].open(act)
            act.wait_ge(const, 1)

            def body(g, i):
                a = g["act"]
                for s, n in g["subs"]:
                    act.wait_ge(*g["vec"].at(f"x2{s}", i))
                    if s == 0:
                        act.wait_ge(*g["vec"].prev("y1", i, PAIRS))
                    else:
                        act.wait_ge(*a.at("std0", i))
                    act.activation(sg[0:n, :], x2[0:n, s, :], ACT.Square, accum_out=ss[0:n, s:s + 1]).then_inc(*a.step(f"sq{s}"))
                    act.wait_ge(*a.at(f"sq{s}", i))
                    act.activation(std[0:n, s:s + 1], ss[0:n, s:s + 1], ACT.Sqrt, scale=1.0 / D_MODEL, bias=eps[0:n, :]).then_inc(*a.step(f"std{s}"))
                for s, n in g["subs"]:
                    act.wait_ge(*g["pe"].at(f"P{s}", i))
                    act.wait_ge(*(g["pe"].at("L0", i) if s else g["pe"].prev("L1", i, PAIRS)))
                    act.activation(pT[:, :, 0:n], psT[:, 0:KP, 0:n], ACT.Copy).then_inc(*a.step(f"pT{s}"))
                    act.wait_ge(*g["pe"].at(f"T{s}", i))
                    act.activation(hT[:, :, 0:n], psT[:, :, 0:n], ACT.Copy).then_inc(*a.step(f"hT{s}"))
                    act.wait_ge(*g["pe"].at(f"G{s}", i))
                    if s:
                        act.wait_ge(*g["vec"].at("y0", i))
                    act.activation(sg[0:n, :], psg[0:n, :, :].rearrange("p a b -> p (a b)"), ACT.Sigmoid).then_inc(*a.step(f"sg{s}"))

            with act.Fori(0, PAIRS) as i:
                body(main, i)
            body(tail, 0)

        @block.vector
        def _(dve):
            main["vec"].open(dve)
            dve.wait_ge(ple_ld, 48)

            def body(g, i):
                v = g["vec"]
                for s, n in g["subs"]:
                    dve.wait_ge(*g["pe"].at(f"F{s}", i))
                    dve.wait_ge(*g[f"x{s}"].at("x", i))
                    dve.tensor_tensor(x2[0:n, s, :], psf[0:n, s, :, :].rearrange("p a b -> p (a b)"), x2[0:n, s, :], ALU.add).then_inc(*v.step(f"x2{s}"))
                    dve.wait_ge(*g["act"].at(f"std{s}", i))
                    dve.reciprocal(rstd[0:n, s:s + 1], std[0:n, s:s + 1]).then_inc(*v.step(f"rstd{s}"))
                    dve.wait_ge(*v.at(f"rstd{s}", i))
                    dve.wait_ge(*g["pe"].prev(f"T{s}", i, PAIRS))
                    dve.scalar_tensor_tensor(out=hn[0:n, s, :], in0=x2[0:n, s, :], scalar=rstd[0:n, s:s + 1], in1=gain[0:n, :],
                                             op0=ALU.mult, op1=ALU.mult).then_inc(*v.step(f"hn{s}"))
                for s, n in g["subs"]:
                    dve.wait_ge(*g["pe"].at(f"L{s}", i))
                    dve.wait_ge(*g["act"].at(f"sg{s}", i))
                    dve.tensor_tensor(sg[0:n, :], psl[0:n, :, :].rearrange("p a b -> p (a b)"), sg[0:n, :], ALU.mult).then_inc(*v.step(f"m{s}"))
                    dve.wait_ge(*v.at(f"m{s}", i))
                    dve.tensor_tensor(x2[0:n, s, :], x2[0:n, s, :], sg[0:n, :], ALU.add).then_inc(*v.step(f"y{s}"))

            with dve.Fori(0, PAIRS) as i:
                body(main, i)
            body(tail, 0)


def rwkv(nc, ident, t, cv):
    with ExitStack() as ctx:
        def sb(name, shape):
            return ctx.enter_context(nc.sbuf_tensor("rw_" + name, shape, F32))

        C, H = 64, 4
        EPS = 64e-5
        tri = sb("tri", [P, 2, P])
        x16 = sb("x16", [P, P])
        x32 = sb("x32", [P, P])
        x64 = sb("x64", [P, P])
        o32 = sb("o32", [P, P])
        o64 = sb("o64", [P, P])
        x16T = sb("x16T", [P, P])
        headones = sb("headones", [P, P])
        cmask = sb("cmask", [P, 2])
        mu = sb("mu", [P, 7])
        w0 = sb("w0", [P, 256])
        chp = sb("chp", [P, 3, 2])
        rk_w = sb("rk_w", [P, 2, H])
        ln_g = sb("ln_g", [P, 256])
        ln_b = sb("ln_b", [P, 256])
        lora = sb("lora", [P, 256])
        eps = sb("eps", [P, 1])
        zin = sb("zin", [P, 2, 7, C + 1])
        zd = sb("zd", [P, 7, 2, C])
        zs = sb("zs", [P, 7, 2, C])
        low = sb("low", [P, P])
        u = sb("u", [P, 256])
        lw = sb("lw", [P, 256])
        g_sb = sb("g", [P, 256])
        a_sb = sb("a", [P, 2, P])
        kraw = sb("kraw", [P, 2, P])
        sqk = sb("sqk", [P, 2, P])
        rn = sb("rn", [P, 2, P])
        kk = sb("kk", [P, 2, P])
        kt = sb("kt", [P, 2, P])
        pall = sb("pall", [P, 2, 2, P])
        pinv = sb("pinv", [P, 2, P])
        RA = sb("RA", [P, 2, 2, P])
        Bc = sb("Bc", [P, 2, P])
        Kc = sb("Kc", [P, 2, P])
        rk = sb("rk", [P, 2, P])
        tok = sb("tok", [P, 4, 256])
        bonus = sb("bonus", [P, H])
        X = sb("X", [P, H, P])
        XT = sb("XT", [P, H, P])
        O32 = sb("O32", [P, H, P])
        O64 = sb("O64", [P, H, P])
        QB = sb("QB", [P, H, P])
        KM = sb("KM", [P, H, 2, P])
        X2 = sb("X2", [P, H, P])
        X2T = sb("X2T", [P, H, P])
        T = [sb(f"T{j}", [P, H, P]) for j in range(2)]
        AM = sb("AM", [P, H, P])
        WU = sb("WU", [P, H, P])
        R2 = sb("R2", [P, 2, P])
        y0 = sb("y0", [P, H, C])
        GT = sb("GT", [P, 2, 2, C])
        Hs = sb("Hs", [P, 2, 2, C])
        ST = sb("ST", [P, 2, C])
        St = sb("St", [P, 2, C])
        S_in = sb("S_in", [P, 2, 2, C])
        S_out = sb("S_out", [P, 2, 2, C])
        sel8 = sb("sel8", [P, 2])
        y = sb("y", [P, H, C])
        yq = sb("yq", [P, H, C])
        mean = sb("mean", [P, H])
        var = sb("var", [P, H])
        oT_sb = sb("oT", [P, 2, P])
        pb = [ctx.enter_context(nc.psum_tensor(f"rw_ps{k}", [P, 512], F32)) for k in range(8)]
        bank = lambda k: pb[k][:, :]
        heads = lambda k: pb[k][:, :].rearrange("p (h t) -> p h t", h=H)
        par = ctx.enter_context(nc.semaphore("rw_parameters_loaded"))
        const = ctx.enter_context(nc.semaphore("rw_constants"))
        shift_st = ctx.enter_context(nc.semaphore("rw_shift_stored"))
        passed, pe_passed, wkv_turned, wkv_made, zcl = [ctx.enter_context(nc.semaphore("rw_" + x)) for x in ("waits_passed", "pe_waits_passed", "state_turned", "state_out_made", "zs_cleared")]
        wkv_st = ctx.enter_context(nc.semaphore("rw_wkv_stored"))
        NPAR = 17
        TILES = SEQ // P
        S_TILES = DEC_BATCH // 2

        ACT_STEPS = ["tanh", "xa", "sig", "a0", "a1", "g", "sg", "skk", "pall", "pinv", "tok", "X2", "X4", "T16", "T32",
                     "WU", "y0", "H", "std", "oT"]
        VEC_STEPS = ["zd", "zm", "zs", "kr0", "kr1", "sqk", "u", "lw", "mx", "rn", "kk", "t0", "t1", "kt", "bb", "R", "rk", "A", "B", "K",
                     "bonus", "X", "XT", "T1", "O32", "O64", "QB", "KM", "AM0", "MV", "X2T", "X4T", "T2", "X8", "T3", "T4", "P1", "T5", "P2", "T6", "R2", "G",
                     "St0", "Sa0", "S0", "St1", "Sa1", "S1",
                     "y", "mean", "yc", "yq", "var", "rstd", "yn", "yg", "yb", "bv", "yv", "out"]
        PE_STEPS = ["lora", "kn", "lp", "tok", "bonus", "L", "BT", "KT", "MV", "X2", "X2T", "X4", "X4T", "D1", "X8", "D2", "D3", "T16", "P1", "D4",
                    "T32", "P2", "D5", "WU", "R2", "Y0", "G", "H", "S0", "Y0s", "S1", "Y1s", "oT"]

        def plan(tag, sample):
            act_steps, pe_steps, vec_steps = list(ACT_STEPS), list(PE_STEPS), list(VEC_STEPS)
            if sample:
                for c in range(2):
                    pe_steps.insert(pe_steps.index(f"S{c}"), f"in{c}")
                    act_steps.insert(act_steps.index("std"), f"in{c}")
                    pe_steps.insert(pe_steps.index(f"Y{c}s") + 1, f"out{c}")
                    act_steps.insert(act_steps.index("std"), f"out{c}")
            return dict(
                sample=sample, valid=DEC_SEQ if sample else C,
                z=Steps(nc, ctx, f"rw_z_loaded{tag}", ["z"], 64 if sample else 32),
                o=Steps(nc, ctx, f"rw_o_stored{tag}", ["o"], 32 if sample else 16),
                s=Steps(nc, ctx, f"rw_state_loaded{tag}", ["s"], 64),
                so=[Steps(nc, ctx, f"rw_state_stored{tag}{c}", ["s"], 16) for c in range(2)],
                act=Steps(nc, ctx, f"rw_act{tag}", act_steps), pe=Steps(nc, ctx, f"rw_pe{tag}", pe_steps),
                vec=Steps(nc, ctx, f"rw_vec{tag}", vec_steps))

        main, samp = plan("", False), plan("s", True)
        for g in (main, samp):
            for k in ("z", "o", "s"):
                g[k].ahead = 0
        samp["so"] = [Steps(nc, ctx, f"rw_state_out{c}", ["s"], 32) for c in range(2)]
        for s in samp["so"]:
            s.ahead = 0

        taps, taps_s = [Steps(nc, ctx, "rw_conv_taps" + tag, CONV_STEPS) for tag in ("", "_s")]
        for s in (taps, taps_s):
            s.ahead = 0

        setup = nc.Block()
        with ExitStack() as conv_ctx, setup:
            conv = conv_inputs(nc, ident, t, cv, pb[0:2], conv_ctx)
            setup.tensor(conv["tensor"])
            setup.scalar(conv["scalar"])
            setup.vector(conv["vector"])

            @setup.sync
            def _(sp):
                conv["sync"](sp)
                with nc.allow_non_contiguous_dma(reason="parameters by channel"):
                    loads = ((mu[:, :], t["mu_shift"].rearrange("(b p) -> p b", p=P)), (w0[:, :], t["w0"].partition_broadcast(P)),
                             (chp[:, 0, :], t["a0"].rearrange("(b p) -> p b", p=P)), (chp[:, 1, :], t["k_k"].rearrange("(b p) -> p b", p=P)),
                             (chp[:, 2, :], t["k_a"].rearrange("(b p) -> p b", p=P)), (ln_g[:, :], t["lnx_g"].partition_broadcast(P)),
                             (ln_b[:, :], t["lnx_b"].partition_broadcast(P)), (lora[0:32, :], t["w_lora"]), (lora[32:64, :], t["a_lora"]),
                             (lora[64:128, :], t["g_lora"]))
                    for dst, src in loads:
                        sp.dma_start(dst, src).then_inc(par, 16)
                    sp.wait_ge(const, 1)
                    for h in range(H):
                        sp.dma_start(rk_w[64 * (h % 2):64 * (h % 2) + 64, h // 2, h:h + 1], t["r_k"][h, :].unsqueeze(1)).then_inc(par, 16)
                    sp.dma_start(t["shift_p"].rearrange("o (b p) -> b p o", p=P), t["zT"][0:7, :, SEQ:SEQ + 1]).then_inc(shift_st, 16)
                    for b in range(7):
                        sp.dma_start(t["shift_s"][:, b * P:(b + 1) * P].rearrange("j p -> p j"),
                                     t["zT"][b, :, SEQ + 1:NT + 1].rearrange("p (j s) -> p j s", s=DEC_SEQ)[:, :, DEC_SEQ - 1]).then_inc(shift_st, 16)
                sp.wait_ge(par, 16 * (len(loads) + H))
                sp.wait_ge(shift_st, 16 * 8)
                conv["sync_last"](sp)

            @setup.gpsimd
            def _(pool):
                conv["gpsimd"](pool)
                n = 0

                def own(op):
                    nonlocal n
                    n += 1
                    op.then_inc(const, 1)
                    pool.wait_ge(const, n)

                def select(m, pattern, base, mult, op=ALU.is_ge):
                    own(pool.affine_select(out=m, in_=m, compare_op=op, fill=0.0, base=base, pattern=pattern, channel_multiplier=mult))

                def same_block(m, size):
                    select(m, [[-size, P // size], [0, size]], 0, 1)
                    select(m, [[size, P // size], [0, size]], size - 1, -1)

                own(pool.memset(rk_w[:, :, :], 0.0))
                for m in (x16, x32, x64, x16T, headones):
                    own(pool.memset(m[:, :], 1.0))
                own(pool.memset(tri[:, :, :], 1.0))
                own(pool.memset(cmask[:, :], -float(np.exp(-0.5))))
                own(pool.memset(eps[:, :], EPS))
                own(pool.memset(zs[:, :, :, :], 0.0))
                own(pool.memset(ST[:, :, :], 0.0))
                for m, size in ((x16, 16), (x32, 32), (x64, 64)):
                    same_block(m[:, :], size)
                    select(m[:, :], [[-1, P]], 0, 1, ALU.is_gt)
                same_block(x16T[:, :], 16)
                select(x16T[:, :], [[1, P]], 0, -1, ALU.is_gt)
                same_block(headones[:, :], 64)
                for j in range(2):
                    same_block(tri[:, j, :], C)
                    select(tri[:, j, :], [[1, P]], 0, -1, ALU.is_gt if j else ALU.is_ge)
                own(pool.tensor_tensor(o32[:, :], x32[:, :], x16[:, :], ALU.subtract))
                own(pool.tensor_tensor(o64[:, :], x64[:, :], x32[:, :], ALU.subtract))
                own(pool.memset(cmask[:, 1:2], 0.0))
                for c in range(2):
                    own(pool.affine_select(out=sel8[:, c:c + 1], in_=cmask[:, 0:1], compare_op=ALU.is_ge, fill=0.0, base=-64 * c, pattern=[[0, 1]], channel_multiplier=1))
                    own(pool.affine_select(out=sel8[:, c:c + 1], in_=sel8[:, c:c + 1], compare_op=ALU.is_ge, fill=0.0, base=64 * c + DEC_SEQ - 1, pattern=[[0, 1]], channel_multiplier=-1))
                own(pool.tensor_tensor(cmask[:, 1:2], sel8[:, 0:1], sel8[:, 1:2], ALU.add))

        products = ctx.enter_context(nc.sbuf_tensor("cv_products", [P, CONV_B, SEQ], F32))
        block = ctx.enter_context(nc.Block())

        @block.sync
        def _(sp):
            def load(at):
                for c in range(2):
                    sp.dma_start(zin[:, c, :, :], t["zT"][0:7, :, bass.ds(at + c * C, C + 1)].rearrange("b p t -> p b t")).then_inc(main["z"].sem, 16)

            def store(at):
                sp.dma_start(t["oT"][0:2, :, bass.ds(at, P)].rearrange("b p t -> p b t"), oT_sb[:, :, :]).then_inc(main["o"].sem, 16)

            load(0)
            with sp.Fori(0, TILES - 1) as i:
                at, after = sp.snap(i * P), sp.snap(i * P + P)
                wait_loop(sp, passed, *main["vec"].at("zs", i))
                load(after)
                wait_loop(sp, passed, *main["act"].at("oT", i))
                store(at)
            sp.wait_ge(*main["act"].at("oT", TILES - 1))
            store((TILES - 1) * P)
            sp.wait_ge(*main["vec"].at("zs", TILES - 1))
            with nc.allow_non_contiguous_dma(reason="states by channel"), sp.Fori(0, S_TILES) as i:
                wait_loop(sp, passed, *samp["vec"].prev("zs", i))
                for c in range(2):
                    sp.dma_start(zin[:, c, :, 0], t["state_shift"][bass.ds(i * 2 + c, 1), :].rearrange("o (b p) -> p (o b)", p=P)).then_inc(samp["z"].sem, 16)
                    sp.dma_start(zin[:, c, :, 1:1 + DEC_SEQ], t["zT"][0:7, :, bass.ds(i * 16 + (1 + SEQ + c * DEC_SEQ), DEC_SEQ)].rearrange("b p t -> p b t")).then_inc(samp["z"].sem, 16)
                wait_loop(sp, passed, *samp["pe"].prev("in1", i))
                for c in range(2):
                    for hp in range(2):
                        sp.dma_start(S_in[64 * hp:64 * hp + 64, c, :, :],
                                     t["state_wkv"][bass.ds(i * 2 + c, 1), :, :, :].rearrange("o (b two) v k -> two v (o b) k", two=2)[hp]).then_inc(samp["s"].sem, 16)

        @block.gpsimd
        def _(pool):
            rows = lambda x: x.rearrange("p (s t) -> p s t", t=DEC_SEQ)
            conv_taps(pool, cv, taps_s, lambda b: rows(products[:, b, 0:TS]), lambda b: rows(cv["c"][:, b, SEQ:NT]), lambda b, j: cv["us"][:, b, :, j:j + DEC_SEQ])
            conv_taps(pool, cv, taps, lambda b: products[:, b, :], lambda b: cv["c"][:, b, 0:SEQ], lambda b, j: cv["up"][:, b, j:j + SEQ])
            pool.wait_ge(wkv_made, 1)
            for hp in range(2):
                pool.dma_start(t["wkv_p"].rearrange("(b two) v k -> two v b k", two=2)[hp], S_out[64 * hp:64 * hp + 64, 0, :, :]).then_inc(wkv_st, 16)
            with pool.Fori(0, S_TILES) as i:
                for c in range(2):
                    pool.wait_ge(*samp["act"].at(f"out{c}", i))
                    for hp in range(2):
                        pool.dma_start(t["wkv_s"][bass.ds(i * 2 + c, 1), :, :, :].rearrange("o (b two) v k -> two v (o b) k", two=2)[hp],
                                       S_out[64 * hp:64 * hp + 64, c, :, :]).then_inc(samp["so"][c].sem, 16)
                pool.wait_ge(*samp["act"].at("oT", i))
                for c in range(2):
                    pool.dma_start(t["oT"][0:2, :, bass.ds(i * 16 + (SEQ + c * DEC_SEQ), DEC_SEQ)].rearrange("b p t -> p b t"),
                                   oT_sb[:, :, c * C:c * C + DEC_SEQ]).then_inc(samp["o"].sem, 16)
            pool.wait_ge(wkv_st, 32)
            pool.wait_ge(*main["o"].at("o", TILES - 1))
            pool.wait_ge(*samp["o"].at("o", S_TILES - 1))
            for c in range(2):
                pool.wait_ge(*samp["so"][c].at("s", S_TILES - 1))

        hb = lambda h: (64 * (h % 2), h // 2)

        def per_head(x, h):
            p0, b = hb(h)
            return x[p0:p0 + 64, b]

        @block.tensor
        def _(pe):
            for g in (main, samp):
                g["pe"].open(pe)

            def body(g, i):
                s = g["pe"]
                act = lambda name: pe.wait_ge(*g["act"].at(name, i))
                vec = lambda name: pe.wait_ge(*g["vec"].at(name, i))

                def each(name, k, make):
                    for h in range(H):
                        mm = make(heads(k)[:, h, :], h)
                    mm.then_inc(*s.step(name))

                def mul(out, lhsT, rhs, start=True, stop=True):
                    return pe.matmul(out, lhsT, rhs, start=start, stop=stop, skip_group_check=True)

                pe.wait_ge(*g["vec"].prev("out", i))
                pe.wait_ge(*g["act"].prev("oT", i))
                for name in ("tanh", "xa", "sig"):
                    act(name)
                mul(bank(0)[:, 0:256], low[0:32, :], lora[0:32, :])
                mul(bank(3)[:, 0:256], low[64:128, :], lora[64:128, :])
                for b in range(2):
                    mm = mul(bank(1)[:, b * P:(b + 1) * P], lora[32:64, b * P:(b + 1) * P], low[32:64, :])
                mm.then_inc(*s.step("lora"))
                vec("sqk")
                act("a1")
                mul(bank(1)[:, 256:512], headones[:, :], sqk[:, :, :].rearrange("p b t -> p (b t)")).then_inc(*s.step("kn"))
                vec("lw")
                for b in range(2):
                    mm = mul(bank(2)[:, b * 256:(b + 1) * 256], lw[:, b * P:(b + 1) * P], tri[:, :, :].rearrange("p j t -> p (j t)"))
                mm.then_inc(*s.step("lp"))
                for name in ("A", "B", "K"):
                    vec(name)
                for j, src in enumerate((lambda b: RA[:, b, 1, :], lambda b: Bc[:, b, :], lambda b: Kc[:, b, :],
                                         lambda b: zs[:, 4 + b, :, :].rearrange("p c t -> p (c t)"))):
                    for b in range(2):
                        mm = pe.transpose(bank(3 + j // 2)[:, (j % 2) * 256 + b * P:(j % 2) * 256 + (b + 1) * P], src(b), ident)
                mm.then_inc(*s.step("tok"))
                vec("rk")
                act("g")
                for b in range(2):
                    mm = mul(bank(0)[:, 0:H], rk[:, b, :], rk_w[:, b, :], b == 0, b == 1)
                mm.then_inc(*s.step("bonus"))
                for h in range(H):
                    mm = mul(bank(2 if h % 2 else 5)[:, (h // 2) * P:(h // 2 + 1) * P], RA[hb(h)[0]:hb(h)[0] + 64, hb(h)[1], 1, :], per_head(Bc, h))
                mm.then_inc(*s.step("L"))
                two = lambda k, h: bank(k + h % 2)[:, (h // 2) * 256:(h // 2) * 256 + 256]
                ra = lambda h: RA[hb(h)[0]:hb(h)[0] + 64, hb(h)[1], :, :].rearrange("p j t -> p (j t)")
                for h in range(H):
                    mm = mul(two(6, h), per_head(Bc, h), ra(h))
                mm.then_inc(*s.step("BT"))
                vec("bonus")
                vec("rn")
                for h in range(H):
                    mm = mul(two(0, h), per_head(Kc, h), ra(h))
                mm.then_inc(*s.step("KT"))
                vec("KM")
                act("tok")
                for h in range(H):
                    mm = mul(bank(3)[:, h * 64:h * 64 + 64], KM[:, h, 1, :], tok[:, 3, h * 64:(h + 1) * 64])
                mm.then_inc(*s.step("MV"))
                vec("O64")
                each("X2", 2, lambda out, h: mul(out, XT[:, h, :], X[:, h, :]))
                each("X2T", 5, lambda out, h: mul(out, X[:, h, :], XT[:, h, :]))
                act("X2")
                vec("X2T")
                each("X4", 6, lambda out, h: mul(out, X2T[:, h, :], X2[:, h, :]))
                each("X4T", 7, lambda out, h: mul(out, X2[:, h, :], X2T[:, h, :]))
                each("D1", 0, lambda out, h: mul(out, X2[:, h, :], T[0][:, h, :]))
                act("X4")
                vec("X4T")
                each("X8", 1, lambda out, h: mul(out, XT[:, h, :], X[:, h, :]))
                vec("T2")
                each("D2", 2, lambda out, h: mul(out, X[:, h, :], T[1][:, h, :]))
                vec("X8")
                vec("T3")
                each("D3", 5, lambda out, h: mul(out, X2[:, h, :], T[0][:, h, :]))
                vec("T4")
                each("T16", 6, lambda out, h: pe.transpose(out, T[1][:, h, :], ident))
                each("P1", 7, lambda out, h: mul(out, O32[:, h, :], T[1][:, h, :]))
                act("T16")
                vec("P1")
                each("D4", 0, lambda out, h: mul(out, X[:, h, :], XT[:, h, :]))
                vec("T5")
                each("T32", 1, lambda out, h: pe.transpose(out, T[0][:, h, :], ident))
                each("P2", 2, lambda out, h: mul(out, O64[:, h, :], T[0][:, h, :]))
                act("T32")
                vec("P2")
                each("D5", 5, lambda out, h: mul(out, X2[:, h, :], X2T[:, h, :]))
                vec("T6")
                vec("MV")
                each("WU", 6, lambda out, h: mul(out, T[1][:, h, :], AM[:, h, :]))
                act("WU")
                for h in range(H):
                    p0, b = hb(h)
                    mm = mul(bank(7)[p0:p0 + 64, b * P:(b + 1) * P], WU[:, h, 0:64], QB[:, h, :])
                mm.then_inc(*s.step("R2"))
                for h in range(H):
                    out = bank(0)[:, h * 64:(h + 1) * 64]
                    mul(out, QB[:, h, :], WU[:, h, 64:128], True, False)
                    mm = mul(out, KM[:, h, 0, :], tok[:, 3, h * 64:(h + 1) * 64], False, True)
                mm.then_inc(*s.step("Y0"))
                for h in range(H):
                    p0, b = hb(h)
                    for c in range(2):
                        r = slice(64 * c, 64 * c + 64)
                        mm = mul(bank(1 + c)[p0:p0 + 64, b * 64:b * 64 + 64], WU[r, h, 0:64], tok[r, 1, h * 64:(h + 1) * 64])
                mm.then_inc(*s.step("G"))
                for h in range(H):
                    p0, b = hb(h)
                    for c in range(2):
                        r = slice(64 * c, 64 * c + 64)
                        out = bank(3 + c)[p0:p0 + 64, b * 64:b * 64 + 64]
                        mul(out, tok[r, 1, h * 64:(h + 1) * 64], WU[r, h, 64:128], True, False)
                        mm = mul(out, tok[r, 2, h * 64:(h + 1) * 64], tok[r, 3, h * 64:(h + 1) * 64], False, True)
                mm.then_inc(*s.step("H"))
                vec("G")
                vec("R2")
                act("H")
                if not g["sample"]:
                    pe.wait_ge(*g["vec"].prev("S1", i))
                for c in range(2):
                    if g["sample"]:
                        pe.wait_ge(*g["s"].at("s", i))
                        if c == 1:
                            act("in0")
                        pe.sem_inc(pe_passed, 1)
                        for h in range(H):
                            p0, b = hb(h)
                            mm = mul(bank(4)[p0:p0 + 64, b * 64:(b + 1) * 64], S_in[p0:p0 + 64, c, b, :], ident[p0:p0 + 64, p0:p0 + 64])
                        mm.then_inc(*s.step(f"in{c}"))
                        act(f"in{c}")
                    elif c == 1:
                        vec("S0")
                    pe.sem_inc(pe_passed, 1)
                    for h in range(H):
                        p0, b = hb(h)
                        mm = mul(bank(2)[p0:p0 + 64, (c * 2 + b) * 64:(c * 2 + b) * 64 + 64], per_head(GT, h)[:, c, :], per_head(ST, h))
                    mm.then_inc(*s.step(f"S{c}"))
                    for h in range(H):
                        p0, b = hb(h)
                        mm = mul(bank(5 + h % 2)[64 * c:64 * c + 64, b * 64:(b + 1) * 64], R2[p0:p0 + 64, b, 64 * c:64 * c + 64], per_head(ST, h))
                    mm.then_inc(*s.step(f"Y{c}s"))
                    if g["sample"]:
                        vec(f"S{c}")
                        pe.sem_inc(pe_passed, 1)
                        for h in range(H):
                            p0, b = hb(h)
                            mm = mul(bank(4)[p0:p0 + 64, 256 + b * 64:256 + (b + 1) * 64], per_head(ST, h), ident[p0:p0 + 64, p0:p0 + 64])
                        mm.then_inc(*s.step(f"out{c}"))
                        act(f"out{c}")
                vec("out")
                for b in range(2):
                    mm = pe.transpose(bank(3)[:, b * P:(b + 1) * P], y[:, 2 * b:2 * b + 2, :].rearrange("p h v -> p (h v)"), ident)
                mm.then_inc(*s.step("oT"))

            with pe.Fori(0, TILES) as i:
                body(main, i)
            pe.wait_ge(*main["vec"].at("S1", TILES - 1))
            for h in range(H):
                p0, b = hb(h)
                mm = pe.matmul(bank(4)[p0:p0 + 64, b * 64:(b + 1) * 64], per_head(ST, h), ident[p0:p0 + 64, p0:p0 + 64], start=True, stop=True, skip_group_check=True)
            mm.then_inc(wkv_turned, 1)
            pe.wait_ge(wkv_made, 1)
            pe.wait_ge(*main["vec"].at("out", TILES - 1))
            pe.wait_ge(*main["act"].at("oT", TILES - 1))
            with pe.Fori(0, S_TILES) as i:
                body(samp, i)

        @block.scalar
        def _(act):
            for g in (main, samp):
                g["act"].open(act)

            def body(g, i):
                s = g["act"]
                pe = lambda name: act.wait_ge(*g["pe"].at(name, i))
                vec = lambda name: act.wait_ge(*g["vec"].at(name, i))

                def run(name, out, src, func=ACT.Copy, **k):
                    act.activation(out, src, func, **k).then_inc(*s.step(name))

                vec("zs")
                act.wait_ge(*g["pe"].prev("lora", i))
                x6 = zs[:, 6, :, :].rearrange("p c t -> p (c t)")
                run("tanh", low[0:32, :], x6[0:32, :], ACT.Tanh)
                run("xa", low[32:64, :], x6[32:64, :])
                run("sig", low[64:128, :], x6[64:128, :], ACT.Sigmoid)
                pe("lora")
                act.wait_ge(*g["vec"].prev("yv", i))
                for b in range(2):
                    run(f"a{b}", a_sb[:, b, :], bank(1)[:, b * P:(b + 1) * P], ACT.Sigmoid, bias=chp[:, 0, b:b + 1])
                act.wait_ge(*g["vec"].prev("out", i))
                vec("u")
                run("g", g_sb[:, :], bank(3)[:, 0:256])
                run("sg", u[:, :], u[:, :], ACT.Sigmoid)
                pe("kn")
                run("skk", rn[:, :, :].rearrange("p b t -> p (b t)"), bank(1)[:, 256:512], ACT.Sqrt)
                pe("lp")
                run("pall", pall[:, :, :, :].rearrange("p b j t -> p (b j t)"), bank(2), ACT.Exp)
                run("pinv", pinv[:, :, :], bank(2).rearrange("p (b j t) -> p b j t", b=2, j=2)[:, :, 0, :], ACT.Exp, scale=-1.0)
                pe("tok")
                act.activation(tok[:, 0:2, :].rearrange("p a b -> p (a b)"), bank(3), ACT.Copy)
                run("tok", tok[:, 2:4, :].rearrange("p a b -> p (a b)"), bank(4))
                pe("X2")
                run("X2", X2[:, :, :], heads(2))
                pe("X4")
                run("X4", X[:, :, :], heads(6))
                pe("T16")
                pe("X8")
                run("T16", X[:, :, :], heads(6))
                pe("T32")
                pe("D3")
                run("T32", X2[:, :, :], heads(1))
                pe("WU")
                run("WU", WU[:, :, :], heads(6))
                pe("Y0")
                run("y0", y0[:, :, :], bank(0)[:, 0:256].rearrange("p (h v) -> p h v", h=H))
                pe("H")
                act.activation(Hs[:, :, 0, :], bank(3)[:, 0:128].rearrange("p (b v) -> p b v", b=2), ACT.Copy)
                run("H", Hs[:, :, 1, :], bank(4)[:, 0:128].rearrange("p (b v) -> p b v", b=2))
                if g["sample"]:
                    for c in range(2):
                        pe(f"in{c}")
                        run(f"in{c}", ST[:, :, :], bank(4)[:, 0:128].rearrange("p (b v) -> p b v", b=2))
                        pe(f"out{c}")
                        act.wait_ge(*g["so"][c].prev("s", i))
                        run(f"out{c}", S_out[:, c, :, :], bank(4)[:, 256:384].rearrange("p (b v) -> p b v", b=2))
                vec("var")
                run("std", var[:, :], var[:, :], ACT.Sqrt, scale=1.0 / C, bias=eps[:, :])
                pe("oT")
                act.wait_ge(*g["o"].prev("o", i))
                run("oT", oT_sb[:, :, :], bank(3)[:, 0:256].rearrange("p (b t) -> p b t", b=2))

            with act.Fori(0, TILES) as i:
                body(main, i)
            act.wait_ge(wkv_turned, 1)
            act.activation(S_out[:, 0, :, :], bank(4)[:, 0:128].rearrange("p (b v) -> p b v", b=2), ACT.Copy).then_inc(wkv_made, 1)
            act.wait_ge(wkv_st, 32)
            act.wait_ge(*main["o"].at("o", TILES - 1))
            with act.Fori(0, S_TILES) as i:
                body(samp, i)

        @block.vector
        def _(dve):
            for g in (main, samp):
                g["vec"].open(dve)

            def body(g, i):
                s = g["vec"]
                pe = lambda name: dve.wait_ge(*g["pe"].at(name, i))
                act = lambda name: dve.wait_ge(*g["act"].at(name, i))

                def after(name):
                    dve.wait_ge(*s.at(name, i))

                def tt(name, out, a, b, op):
                    dve.tensor_tensor(out, a, b, op).then_inc(*s.step(name))

                n = g["valid"]
                flat = lambda x: x.rearrange("p b t -> p (b t)")
                over = lambda m: m.unsqueeze(1).to_broadcast([P, H, P])
                cur = zin[:, :, :, 1:1 + n].rearrange("p c b t -> p b c t")
                before = zin[:, :, :, 0:n].rearrange("p c b t -> p b c t")
                dve.wait_ge(*g["z"].at("z", i))
                dve.wait_ge(*g["pe"].prev("tok", i))
                dve.wait_ge(*g["act"].prev("sig", i))
                for c in range(2):
                    op = dve.tensor_tensor(zd[:, :, c, 0:n], before[:, :, c, :], cur[:, :, c, :], ALU.subtract)
                op.then_inc(*s.step("zd"))
                after("zd")
                for c in range(2):
                    op = dve.tensor_tensor(zd[:, :, c, 0:n], zd[:, :, c, 0:n], mu[:, :].unsqueeze(2).to_broadcast([P, 7, n]), ALU.mult)
                op.then_inc(*s.step("zm"))
                after("zm")
                for c in range(2):
                    op = dve.tensor_tensor(zs[:, :, c, 0:n], zd[:, :, c, 0:n], cur[:, :, c, :], ALU.add)
                op.then_inc(*s.step("zs"))
                after("zs")
                zb = lambda b: zs[:, b, :, :].rearrange("p c t -> p (c t)")
                z2 = lambda b: zs[:, b:b + 2, :, :].rearrange("p b c t -> p (b c t)")
                for b in range(2):
                    dve.tensor_scalar(kraw[:, b, :], zb(2 + b), chp[:, 1, b:b + 1], None, ALU.mult).then_inc(*s.step(f"kr{b}"))
                after("kr1")
                dve.wait_ge(*g["pe"].prev("kn", i))
                tt("sqk", sqk[:, :, :], kraw[:, :, :], kraw[:, :, :], ALU.mult)
                pe("lora")
                tt("u", u[:, :], bank(0)[:, 0:256], w0[:, :], ALU.add)
                act("sg")
                dve.wait_ge(*g["pe"].prev("lp", i))
                dve.tensor_scalar(lw[:, :], u[:, :], cmask[:, 1:2] if g["sample"] else cmask[:, 0:1], None, ALU.mult).then_inc(*s.step("lw"))
                act("skk")
                dve.tensor_scalar(rn[:, :, :], rn[:, :, :], 1e-12, None, ALU.max).then_inc(*s.step("mx"))
                after("mx")
                dve.reciprocal(rn[:, :, :], rn[:, :, :]).then_inc(*s.step("rn"))
                after("rn")
                tt("kk", kk[:, :, :], kraw[:, :, :], rn[:, :, :], ALU.mult)
                act("a1")
                for b in range(2):
                    dve.tensor_scalar(kt[:, b, :], a_sb[:, b, :], 1.0, chp[:, 2, b:b + 1], ALU.subtract, ALU.mult).then_inc(*s.step(f"t{b}"))
                after("t1")
                dve.scalar_tensor_tensor(out=flat(kt[:, :, :]), in0=flat(kt[:, :, :]), scalar=1.0, in1=z2(2), op0=ALU.add, op1=ALU.mult).then_inc(*s.step("kt"))
                after("kk")
                tt("bb", a_sb[:, :, :], a_sb[:, :, :], kk[:, :, :], ALU.mult)
                act("pinv")
                after("kt")
                tt("R", RA[:, :, 0, :], zs[:, 0:2, :, :].rearrange("p b c t -> p b (c t)"), pall[:, :, 0, :], ALU.mult)
                tt("rk", flat(rk[:, :, :]), z2(0), flat(kt[:, :, :]), ALU.mult)
                dve.scalar_tensor_tensor(out=RA[:, :, 1, :], in0=kk[:, :, :], scalar=-1.0, in1=pall[:, :, 1, :], op0=ALU.mult, op1=ALU.mult).then_inc(*s.step("A"))
                after("bb")
                tt("B", Bc[:, :, :], a_sb[:, :, :], pinv[:, :, :], ALU.mult)
                tt("K", Kc[:, :, :], kt[:, :, :], pinv[:, :, :], ALU.mult)
                pe("bonus")
                dve.tensor_copy(bonus[:, :], bank(0)[:, 0:H]).then_inc(*s.step("bonus"))
                pe("L")
                parity = lambda x, q: x.rearrange("p (b two) t -> p b two t", two=2)[:, :, q, :]
                over2 = lambda m: m.unsqueeze(1).to_broadcast([P, 2, P])

                def lower(name, out, m):
                    for q in range(2):
                        op = dve.tensor_tensor(parity(out[:, :, :], q), bank(2 if q else 5)[:, 0:256].rearrange("p (b t) -> p b t", b=2), over2(m[:, :]), ALU.mult)
                    op.then_inc(*s.step(name))

                lower("X", X, x16)
                pe("BT")
                bt = lambda k, j: pb[k][:, :].rearrange("p (h j t) -> p h j t", h=2, j=2)[:, :, j, :]
                for q in range(2):
                    op = dve.tensor_tensor(parity(XT[:, :, :], q), bt(6 + q, 1), over2(x16T[:, :]), ALU.mult)
                op.then_inc(*s.step("XT"))
                after("XT")
                tt("T1", T[0][:, :, :], XT[:, :, :], over(ident), ALU.add)
                lower("O32", O32, o32)
                lower("O64", O64, o64)
                for q in range(2):
                    op = dve.tensor_tensor(parity(QB[:, :, :], q), bt(6 + q, 0), over2(tri[:, 0, :]), ALU.mult)
                op.then_inc(*s.step("QB"))
                pe("KT")
                for k in range(2):
                    op = dve.tensor_tensor(KM[:, :, :, :].rearrange("p (b two) j t -> p b two (j t)", two=2)[:, :, k, :], pb[k][:, :].rearrange("p (h x) -> p h x", h=2),
                                           tri[:, :, :].rearrange("p j t -> p (j t)").unsqueeze(1).to_broadcast([P, 2, 256]), ALU.mult)
                op.then_inc(*s.step("KM"))
                act("tok")
                dve.tensor_copy(AM[:, :, 0:64], tok[:, 0, :].rearrange("p (h k) -> p h k", h=H)).then_inc(*s.step("AM0"))
                pe("MV")
                dve.tensor_copy(AM[:, :, 64:128], bank(3)[:, 0:256].rearrange("p (h k) -> p h k", h=H)).then_inc(*s.step("MV"))
                pe("X2T")
                dve.tensor_copy(X2T[:, :, :], heads(5)).then_inc(*s.step("X2T"))
                pe("X4T")
                dve.tensor_copy(XT[:, :, :], heads(7)).then_inc(*s.step("X4T"))
                pe("D1")
                tt("T2", T[1][:, :, :], heads(0), T[0][:, :, :], ALU.add)
                pe("X8")
                dve.tensor_copy(X2[:, :, :], heads(1)).then_inc(*s.step("X8"))
                pe("D2")
                after("T2")
                tt("T3", T[0][:, :, :], heads(2), T[1][:, :, :], ALU.add)
                pe("D3")
                after("T3")
                tt("T4", T[1][:, :, :], heads(5), T[0][:, :, :], ALU.add)
                pe("P1")
                dve.tensor_copy(XT[:, :, :], heads(7)).then_inc(*s.step("P1"))
                pe("D4")
                after("T4")
                tt("T5", T[0][:, :, :], heads(0), T[1][:, :, :], ALU.add)
                pe("P2")
                dve.tensor_copy(X2T[:, :, :], heads(2)).then_inc(*s.step("P2"))
                pe("D5")
                after("T5")
                tt("T6", T[1][:, :, :], heads(5), T[0][:, :, :], ALU.add)
                pe("R2")
                tt("R2", R2[:, :, :], bank(7)[:, 0:256].rearrange("p (b t) -> p b t", b=2), RA[:, :, 0, :], ALU.add)
                pe("G")
                for c in range(2):
                    op = dve.tensor_copy(GT[:, :, c, :], bank(1 + c)[:, 0:128].rearrange("p (b v) -> p b v", b=2))
                op.then_inc(*s.step("G"))
                act("H")
                for c in range(2):
                    if g["sample"]:
                        act(f"in{c}")
                    elif c:
                        after("S0")
                    else:
                        dve.wait_ge(*s.prev("S1", i))
                    tt(f"St{c}", St[:, :, :], ST[:, :, :], Hs[:, :, c, :], ALU.add)
                    pe(f"S{c}")
                    after(f"St{c}")
                    tt(f"Sa{c}", St[:, :, :], bank(2)[:, c * 128:(c + 1) * 128].rearrange("p (b v) -> p b v", b=2), St[:, :, :], ALU.add)
                    after(f"Sa{c}")
                    pe(f"Y{c}s")
                    tt(f"S{c}", ST[:, :, :], St[:, :, :], pall[:, :, 0, 64 * c + 63:64 * c + 64].to_broadcast([P, 2, 64]), ALU.mult)
                act("y0")
                dve.wait_ge(*g["pe"].prev("oT", i))
                for q in range(2):
                    op = dve.tensor_tensor(parity(y[:, :, :], q), bank(5 + q)[:, 0:128].rearrange("p (b v) -> p b v", b=2), parity(y0[:, :, :], q), ALU.add)
                op.then_inc(*s.step("y"))
                after("y")
                dve.tensor_reduce(mean[:, :], y[:, :, :], AX.X, ALU.add).then_inc(*s.step("mean"))
                after("mean")
                dve.scalar_tensor_tensor(out=y[:, :, :], in0=mean[:, :].unsqueeze(2).to_broadcast([P, H, C]), scalar=-1.0 / C, in1=y[:, :, :],
                                         op0=ALU.mult, op1=ALU.add).then_inc(*s.step("yc"))
                after("yc")
                tt("yq", yq[:, :, :], y[:, :, :], y[:, :, :], ALU.mult)
                after("yq")
                dve.tensor_reduce(var[:, :], yq[:, :, :], AX.X, ALU.add).then_inc(*s.step("var"))
                act("std")
                dve.reciprocal(var[:, :], var[:, :]).then_inc(*s.step("rstd"))
                after("rstd")
                fl = lambda x: x.rearrange("p h v -> p (h v)")
                tt("yn", y[:, :, :], y[:, :, :], var[:, :].unsqueeze(2).to_broadcast([P, H, C]), ALU.mult)
                after("yn")
                tt("yg", fl(y[:, :, :]), fl(y[:, :, :]), ln_g[:, :], ALU.mult)
                after("yg")
                tt("yb", fl(y[:, :, :]), fl(y[:, :, :]), ln_b[:, :], ALU.add)
                tt("bv", yq[:, :, :], tok[:, 3, :].rearrange("p (h v) -> p h v", h=H), bonus[:, :].unsqueeze(2).to_broadcast([P, H, C]), ALU.mult)
                after("bv")
                tt("yv", y[:, :, :], y[:, :, :], yq[:, :, :], ALU.add)
                after("yv")
                act("g")
                tt("out", fl(y[:, :, :]), fl(y[:, :, :]), g_sb[:, :], ALU.mult)

            with dve.Fori(0, TILES) as i:
                body(main, i)
            dve.wait_ge(*main["pe"].at("oT", TILES - 1))
            dve.memset(zs[:, :, :, :], 0.0).then_inc(zcl, 1)
            dve.wait_ge(zcl, 1)
            with dve.Fori(0, S_TILES) as i:
                body(samp, i)


CONV_W, CONV_B = 31, 2


def conv_buffers(nc, ctx):
    sb = lambda name, shape: ctx.enter_context(nc.sbuf_tensor("cv_" + name, shape, F32))
    pad = CONV_W - 1
    return dict(up=sb("up", [P, CONV_B, pad + SEQ]), us=sb("us", [P, CONV_B, DEC_BATCH, pad + DEC_SEQ]), c=sb("c", [P, CONV_B, NT]),
                w=sb("w", [P, CONV_B, CONV_W]), par=sb("par", [P, 3, CONV_B]))


def conv_inputs(nc, ident, t, cv, ps_t, ctx):
    def sb(name, shape):
        return ctx.enter_context(nc.sbuf_tensor("cv_" + name, shape, F32))

    CW, CB = CONV_W, CONV_B
    PAD = CW - 1
    ROWS = DEC_BATCH // 2 * PAD
    up, us, w, par = cv["up"], cv["us"], cv["w"], cv["par"]
    z = sb("z", [P, 2 * CB, NT])
    tails = sb("tails", [P, 2, CB, ROWS])
    st_in = sb("st_in", [ROWS, 2, CB * P])
    st_out = sb("st_out", [ROWS, 3, CB * P])
    z_ld = [ctx.enter_context(nc.semaphore(f"cv_z_loaded{b}")) for b in range(CB)]
    par_ld = ctx.enter_context(nc.semaphore("cv_parameters_loaded"))
    st_ld = ctx.enter_context(nc.semaphore("cv_state_loaded"))
    stored = ctx.enter_context(nc.semaphore("cv_state_stored"))
    pe_s = Steps(nc, ctx, "cv_in_pe", ["in0", "in1", "out0", "out1", "out2"])
    act_s = Steps(nc, ctx, "cv_in_act", [f"sig{b}" for b in range(CB)] + ["in0", "in1", "out0", "out1", "out2"])
    vec_s = Steps(nc, ctx, "cv_in_vec", [f"u{b}" for b in range(CB)] + ["tails"])
    for s in (pe_s, act_s, vec_s):
        s.ahead = 0

    def sync(sp):
        with nc.allow_non_contiguous_dma(reason="parameters by channel"):
            for b in range(CB):
                sp.dma_start(w[:, b, :], t["conv_w"][:, b * P:(b + 1) * P].rearrange("w p -> p w")).then_inc(par_ld, 16)
            for j, name in enumerate(("conv_b", "conv_ln_g", "conv_ln_b")):
                sp.dma_start(par[:, j, :], t[name].rearrange("(b p) -> p b", p=P)).then_inc(par_ld, 16)
        for b in range(CB):
            for j in range(2):
                sp.dma_start(z[:, j * CB + b, :], t["zT"][7 + j * CB + b, :, 1:NT + 1]).then_inc(z_ld[b], 16)
        for j in range(2):
            sp.dma_start(st_in[:, j, :], t["state_conv"][4 * j:4 * j + 4, :, :].rearrange("b w c -> (b w) c")).then_inc(st_ld, 16)

    def sync_last(sp):
        sp.wait_ge(*act_s.at("out2", 0))
        for j in range(2):
            sp.dma_start(t["conv_s"][4 * j:4 * j + 4, :, :].rearrange("b w c -> (b w) c"), st_out[:, j, :]).then_inc(stored, 16)
        sp.dma_start(t["conv_p"], st_out[0:PAD, 2, :]).then_inc(stored, 16)
        sp.wait_ge(par_ld, 16 * 5)
        sp.wait_ge(stored, 16 * 3)

    def gpsimd(pool):
        pool.memset(up[:, :, 0:PAD], 0.0)

    def tensor(pe):
        pe.wait_ge(st_ld, 32)
        for j in range(2):
            for b in range(CB):
                mm = pe.transpose(ps_t[j][:, b * P:b * P + ROWS], st_in[:, j, b * P:(b + 1) * P], ident[0:ROWS, 0:ROWS])
            mm.then_inc(*pe_s.step(f"in{j}"))
        pe.wait_ge(*act_s.at("in1", 0))
        pe.wait_ge(*vec_s.at("tails", 0))
        for j in range(3):
            if j == 2:
                pe.wait_ge(*act_s.at("out0", 0))
            for b in range(CB):
                src, n = (tails[:, j, b, :], ROWS) if j < 2 else (up[:, b, SEQ:SEQ + PAD], PAD)
                mm = pe.transpose(ps_t[j % 2][0:n, b * P:(b + 1) * P], src, ident)
            mm.then_inc(*pe_s.step(f"out{j}"))

    def scalar(act):
        for b in range(CB):
            act.wait_ge(z_ld[b], 32)
            act.activation(z[:, CB + b, :], z[:, CB + b, :], ACT.Sigmoid).then_inc(*act_s.step(f"sig{b}"))
        for j in range(2):
            act.wait_ge(*pe_s.at(f"in{j}", 0))
            act.activation(us[:, :, 4 * j:4 * j + 4, 0:PAD].rearrange("p b s w -> p b s w"),
                           ps_t[j][:, 0:CB * P].rearrange("p (b x) -> p b x", b=CB)[:, :, 0:ROWS].rearrange("p b (s w) -> p b s w", w=PAD),
                           ACT.Copy).then_inc(*act_s.step(f"in{j}"))
        for j in range(3):
            n = ROWS if j < 2 else PAD
            act.wait_ge(*pe_s.at(f"out{j}", 0))
            act.activation(st_out[0:n, j, :], ps_t[j % 2][0:n, 0:CB * P], ACT.Copy).then_inc(*act_s.step(f"out{j}"))

    def vector(dve):
        for b in range(CB):
            dve.wait_ge(*act_s.at(f"sig{b}", 0))
            dve.tensor_tensor(us[:, b, :, PAD:], z[:, b, SEQ:NT].rearrange("p (s t) -> p s t", t=DEC_SEQ), z[:, CB + b, SEQ:NT].rearrange("p (s t) -> p s t", t=DEC_SEQ), ALU.mult)
            dve.tensor_tensor(up[:, b, PAD:], z[:, b, 0:SEQ], z[:, CB + b, 0:SEQ], ALU.mult).then_inc(*vec_s.step(f"u{b}"))
        dve.wait_ge(*act_s.at("in1", 0))
        dve.wait_ge(*vec_s.at("u1", 0))
        for j in range(2):
            for b in range(CB):
                op = dve.tensor_copy(tails[:, j, b, :].rearrange("p (s w) -> p s w", w=PAD), us[:, b, 4 * j:4 * j + 4, DEC_SEQ:DEC_SEQ + PAD])
        op.then_inc(*vec_s.step("tails"))

    return dict(sync=sync, sync_last=sync_last, gpsimd=gpsimd, tensor=tensor, scalar=scalar, vector=vector)


CONV_STEPS = [f"{k}{b}_{j}" for j in range(CONV_W) for b in range(CONV_B) for k in ("product", "sum")]


def conv_taps(pool, cv, steps, product_of, out_of, src_of):
    for j in range(CONV_W):
        for b in range(CONV_B):
            out, src, product, tap = out_of(b), src_of(b, j), product_of(b), cv["w"][:, b, j:j + 1]
            if j == 0:
                pool.tensor_scalar(product, src, tap, None, ALU.mult).then_inc(*steps.step(f"product{b}_{j}"))
                pool.wait_ge(*steps.at(f"product{b}_{j}", 0))
                pool.tensor_scalar(out, product, cv["par"][:, 0, b:b + 1], None, ALU.add).then_inc(*steps.step(f"sum{b}_{j}"))
            else:
                pool.tensor_scalar(product, src, tap, None, ALU.mult).then_inc(*steps.step(f"product{b}_{j}"))
                pool.wait_ge(*steps.at(f"product{b}_{j}", 0))
                pool.tensor_tensor(out, out, product, ALU.add).then_inc(*steps.step(f"sum{b}_{j}"))


def conv_finish(nc, t, cv):
    with ExitStack() as ctx:
        def sb(name, shape):
            return ctx.enter_context(nc.sbuf_tensor("cf_" + name, shape, F32))

        CB = CONV_B
        c_sb, par = cv["c"], cv["par"]
        sq = sb("sq", [P, CB, 512])
        rs = sb("rs", [P, 2, 512])
        mean_w = sb("mean_w", [P, P])
        eps = sb("eps", [P, 1])
        ps_m = ctx.enter_context(nc.psum_tensor("cf_psm", [P, 2, 512], F32))
        ps_v = ctx.enter_context(nc.psum_tensor("cf_psv", [P, 2, 512], F32))
        const = ctx.enter_context(nc.semaphore("cf_constants"))
        stored = ctx.enter_context(nc.semaphore("cf_stored"))
        groups = [(g * 512, 512) for g in range(4)] + [(SEQ, TS)]
        pe_s = Steps(nc, ctx, "cf_pe", [f"{k}{g}" for g in range(5) for k in ("m", "v")])
        act_s = Steps(nc, ctx, "cf_act", [x for g in range(5) for x in (f"std{g}", f"s{g}0", f"s{g}1")])
        vec_s = Steps(nc, ctx, "cf_vec", [x for g in range(5) for x in (f"cc{g}", f"sq{g}", f"rs{g}", f"yn{g}")])
        for s in (pe_s, act_s, vec_s):
            s.ahead = 0
        block = ctx.enter_context(nc.Block())

        @block.sync
        def _(sp):
            for g, (at, n) in enumerate(groups):
                sp.wait_ge(*act_s.at(f"s{g}1", 0))
                sp.dma_start(t["oT"][2:4, :, at:at + n].rearrange("b p t -> p b t"), c_sb[:, :, at:at + n]).then_inc(stored, 16)
            sp.wait_ge(stored, 16 * len(groups))

        @block.gpsimd
        def _(pool):
            pool.memset(mean_w[:, :], 1.0 / (CB * P)).then_inc(const, 1)
            pool.memset(eps[:, :], 1e-5).then_inc(const, 1)

        @block.tensor
        def _(pe):
            pe.wait_ge(const, 2)
            for g, (at, n) in enumerate(groups):
                if g >= 2:
                    pe.wait_ge(*vec_s.at(f"cc{g - 2}", 0))
                for b in range(CB):
                    mm = pe.matmul(ps_m[:, g % 2, 0:n], mean_w[:, :], c_sb[:, b, at:at + n], start=b == 0, stop=b == CB - 1)
                mm.then_inc(*pe_s.step(f"m{g}"))
                pe.wait_ge(*vec_s.at(f"sq{g}", 0))
                if g >= 2:
                    pe.wait_ge(*act_s.at(f"std{g - 2}", 0))
                for b in range(CB):
                    mm = pe.matmul(ps_v[:, g % 2, 0:n], mean_w[:, :], sq[:, b, 0:n], start=b == 0, stop=b == CB - 1)
                mm.then_inc(*pe_s.step(f"v{g}"))

        @block.scalar
        def _(act):
            act.wait_ge(const, 2)
            for g, (at, n) in enumerate(groups):
                act.wait_ge(*pe_s.at(f"v{g}", 0))
                if g >= 2:
                    act.wait_ge(*vec_s.at(f"yn{g - 2}", 0))
                act.activation(rs[:, g % 2, 0:n], ps_v[:, g % 2, 0:n], ACT.Sqrt, bias=eps[:, :]).then_inc(*act_s.step(f"std{g}"))
                act.wait_ge(*vec_s.at(f"yn{g}", 0))
                for b in range(CB):
                    act.activation(c_sb[:, b, at:at + n], c_sb[:, b, at:at + n], ACT.Silu, scale=par[:, 1, b:b + 1], bias=par[:, 2, b:b + 1]).then_inc(*act_s.step(f"s{g}{b}"))

        @block.vector
        def _(dve):
            for g, (at, n) in enumerate(groups):
                both = lambda x: x.unsqueeze(1).to_broadcast([P, CB, n])
                c = c_sb[:, :, at:at + n]
                dve.wait_ge(*pe_s.at(f"m{g}", 0))
                dve.tensor_tensor(c, c, both(ps_m[:, g % 2, 0:n]), ALU.subtract).then_inc(*vec_s.step(f"cc{g}"))
                dve.wait_ge(*vec_s.at(f"cc{g}", 0))
                if g:
                    dve.wait_ge(*pe_s.at(f"v{g - 1}", 0))
                dve.tensor_tensor(sq[:, :, 0:n], c, c, ALU.mult).then_inc(*vec_s.step(f"sq{g}"))
                dve.wait_ge(*act_s.at(f"std{g}", 0))
                dve.reciprocal(rs[:, g % 2, 0:n], rs[:, g % 2, 0:n]).then_inc(*vec_s.step(f"rs{g}"))
                dve.wait_ge(*vec_s.at(f"rs{g}", 0))
                dve.tensor_tensor(c, c, both(rs[:, g % 2, 0:n]), ALU.mult).then_inc(*vec_s.step(f"yn{g}"))


def bias_rows():
    dist = 255 - np.arange(BIAS_W)
    far = np.maximum(dist, 16).astype(np.float32)
    large = 16 + (np.log(far / np.float32(16)) / np.float32(np.log(8.0)) * np.float32(16)).astype(np.int32)
    bucket = np.where(dist < 16, np.maximum(dist, 0), np.minimum(large, N_BUCKETS - 1))
    row = np.arange(N_BUCKETS)[:, None]
    return (row == bucket).astype(np.float32) - (row == N_BUCKETS - 1).astype(np.float32)


def bias_table(nc, t):
    with ExitStack() as ctx:
        rel = ctx.enter_context(nc.sbuf_tensor("bt_rel", [N_BUCKETS, 8], F32))
        rows = ctx.enter_context(nc.sbuf_tensor("bt_rows", [N_BUCKETS, BIAS_W], F32))
        out = ctx.enter_context(nc.sbuf_tensor("bt_out", [8, BIAS_W], F32))
        ps = ctx.enter_context(nc.psum_tensor("bt_ps", [8, BIAS_W], F32))
        ld, mm, cp, st = [ctx.enter_context(nc.semaphore("bt_" + x)) for x in ("loaded", "multiplied", "copied", "stored")]
        block = ctx.enter_context(nc.Block())

        @block.sync
        def _(sp):
            sp.dma_start(rel[:, :], t["rel_bias"]).then_inc(ld, 16)
            sp.dma_start(rows[:, :], t["bias_rows"]).then_inc(ld, 16)
            sp.wait_ge(cp, 1)
            sp.dma_start(t["bias"], out[:, :].unsqueeze(1).to_broadcast([8, P, BIAS_W])).then_inc(st, 16)
            sp.wait_ge(st, 16)

        @block.tensor
        def _(pe):
            pe.wait_ge(ld, 32)
            pe.matmul(ps[:, :], rel[:, :], rows[:, :], start=True, stop=True).then_inc(mm, 1)

        @block.vector
        def _(dve):
            dve.wait_ge(mm, 1)
            dve.tensor_copy(out[:, :], ps[:, :]).then_inc(cp, 1)


def attention_prompt(nc, ident, t):
    with ExitStack() as ctx:
        def sb(name, shape):
            return ctx.enter_context(nc.sbuf_tensor("ap_" + name, shape, F32))

        QT = SEQ // P
        NH, D = 8, 64
        ROUNDS = 256 // 8
        OUT, GONE, LEAST = -1e30, -3e38, -3.4e38
        z = sb("z", [P, 2, N_ATT])
        gain = sb("gain", [P, 11, D])
        causal = sb("causal", [P, P])
        B = sb("B", [P, NH, 256])
        sq = sb("sq", [P, 11, D])
        ss = sb("ss", [P, 11])
        qkn = sb("qkn", [P, 2, 5, P])
        kin = sb("kin", [P, 2, 2, D])
        wi = sb("wi", [P, 4])
        eps = sb("eps", [P, 1])
        qT = sb("qT", [P, 3, 4, P])
        qiT = sb("qiT", [P, 2, P])
        kT = sb("kT", [P, SEQ])
        kiT = sb("kiT", [P, SEQ])
        V = sb("V", [P, QT, P])
        rl = sb("rl", [P, 4, 512])
        sc = sb("sc", [P, 2, SEQ])
        best = sb("best", [P, 8])
        msk = sb("msk", [P, SEQ])
        near = sb("near", [P, 2, 256])
        lg = sb("lg", [P, NH, SEQ])
        mxs = sb("mxs", [P, NH, 6])
        neg = sb("neg", [P, NH])
        tot = sb("tot", [P, 2, NH])
        PT = sb("PT", [P, 2, 512])
        o_sb = sb("o", [P, NH, D])
        oT_sb = sb("oT", [P, 4, P])
        pb = [ctx.enter_context(nc.psum_tensor(f"ap_ps{k}", [P, 512], F32)) for k in range(8)]
        par = ctx.enter_context(nc.semaphore("ap_parameters_loaded"))
        const = ctx.enter_context(nc.semaphore("ap_constants"))
        v_ld = ctx.enter_context(nc.semaphore("ap_v_loaded"))
        v_st = ctx.enter_context(nc.semaphore("ap_v_stored"))
        z_ld = [ctx.enter_context(nc.semaphore(f"ap_z_loaded{k}")) for k in range(2)]
        k_st = [ctx.enter_context(nc.semaphore(f"ap_k_stored{k}")) for k in range(2)]
        o_st = ctx.enter_context(nc.semaphore("ap_o_stored"))

        def chunks(n, size=512):
            return [(at, min(size, n - at)) for at in range(0, n, size)]

        def keys(i):
            return P * (i + 1)

        def logit_chunks(a):
            return chunks(keys(a))

        def pieces(a):
            far = max(0, keys(a) - 256)
            out = []
            for c, (at, n) in enumerate(logit_chunks(a)):
                for lo, hi, close in ((at, min(at + n, far), False), (max(at, far), at + n, True)):
                    if hi > lo:
                        out.append((c, lo, hi - lo, close))
            return out

        def groups(a):
            return [list(range(k, min(k + 4, a + 1))) for k in range(0, a + 1, 4)]

        def steps_of(engine, names):
            s = Steps(nc, ctx, "ap_" + engine, names)
            s.ahead = 0
            return s

        def pv_order(a):
            n = len(groups(a))
            out = [("P", 0)]
            for k in range(n):
                if k + 1 < n:
                    out.append(("P", k + 1))
                out.append(("V", k))
            return out

        def slots():
            for i in range(-1, QT + 1):
                for h in range(NH):
                    yield i, h, (i - 1 if i >= 1 else None), (i + 1 if i + 1 < QT else None)

        def scored(n, h, first):
            return h - first if n is not None and 0 <= h - first < len(chunks(keys(n))) else None

        TURN, SCORE, WEIGH = 2, 3, 4
        pe_n, act_n, vec_n = [], [], []
        for i, h, a, n in slots():
            if a is not None:
                if a == 0 and h == 0:
                    pe_n += ["L0_0_0"]
                a2, h2 = (a, h + 1) if h + 1 < NH else (a + 1, 0)
                if a2 < QT:
                    pe_n += [f"L{a2}_{h2}_{c}" for c, _ in enumerate(logit_chunks(a2))]
                if h == 0 and a:
                    pe_n += [f"oT{a - 1}"]
                pe_n += [f"{k}{a}_{h}_{g}" for k, g in pv_order(a)]
                act_n += [f"E{a}_{h}"] + ([f"o{a - 1}"] if h == 0 and a else []) + [f"e{a}_{h}_{g}" for g, _ in enumerate(groups(a))]
                vec_n += [f"nb{a}_{h}"] + [f"x{a}_{h}_{k}" for k, _ in enumerate(pieces(a))] + [f"ng{a}_{h}"]
                if h == 0 and a:
                    vec_n += [f"rc{a - 1}", f"on{a - 1}"]
            if n is not None:
                if h == TURN:
                    pe_n += [f"Tq{n}", f"Tk{n}"]
                    vec_n += [f"{k}{n}" for k in ("r", "nq", "nk", "ni", "gq", "gi", "wi")]
                act_n += {0: [f"sq{n}"], 1: [f"std{n}"], TURN: [f"q{n}", f"k{n}"]}.get(h, [])
                if h == 1:
                    vec_n += [f"ss{n}"]
                c = scored(n, h, SCORE)
                if c is not None:
                    pe_n += [f"S{n}_{c}_{hp}" for hp in range(2)]
                    act_n += [f"R{n}_{c}_{x}" for x in range(4)]
                c = scored(n, h, WEIGH)
                if c is not None:
                    vec_n += [f"A{n}_{c}_{x}" for x in range(4)]
                if h == NH - 1:
                    vec_n += [f"M{n}"]
            if 2 <= i < QT:
                vec_n += [f"{k}{i}_{r}" for r in range(4 * h, 4 * h + 4) for k in ("mx", "mr")]
            if h == NH - 1 and 0 <= i < QT:
                vec_n += [f"mk{i}"]
        pe_n += [f"oT{QT - 1}"]
        act_n += [f"o{QT - 1}"]
        vec_n += [f"rc{QT - 1}", f"on{QT - 1}"]
        pe_s, act_s, vec_s = steps_of("pe", pe_n), steps_of("act", act_n), steps_of("vec", vec_n)

        def ring(names_of, size):
            flat = list(names_of)
            return {n: (k % size, flat[k - size] if k >= size else None) for k, n in enumerate(flat)}

        l_ring = ring([n for n in pe_n if n[0] == "L"], 4)
        p_ring = ring([n for n in pe_n if n[0] == "P"], 2)
        def read(name):
            a, h, c = map(int, name[1:].split("_"))
            return f"x{a}_{h}_{max(k for k, piece in enumerate(pieces(a)) if piece[0] == c)}"

        block = ctx.enter_context(nc.Block())

        @block.sync
        def _(sp):
            loads = [(gain[:, h, :], t["q_norm"].partition_broadcast(P)) for h in range(8)]
            loads += [(gain[:, 8 + h, :], t["k_norm"].partition_broadcast(P)) for h in range(2)] + [(gain[:, 10, :], t["kidx_norm"].partition_broadcast(P))]
            loads += [(B[:, :, :], bass.AP(t["bias"].tensor, P - 1, [[BIAS_W - 1, P], [P * BIAS_W, NH], [1, 256]]))]
            for dst, src in loads:
                sp.dma_start(dst, src).then_inc(par, 16)
            sp.dma_start(t["v_p"], t["za"][0:SEQ, 640:768]).then_inc(v_st, 16)
            for i in range(QT):
                if i >= 2:
                    sp.wait_ge(*pe_s.at(f"Tk{i - 2}", 0))
                    sp.wait_ge(*vec_s.at(f"wi{i - 2}", 0))
                sp.dma_start(z[:, i % 2, :], t["za"][i * P:(i + 1) * P, :]).then_inc(z_ld[i % 2], 16)
                if i == 0:
                    sp.dma_start(V[:, :, :], t["za"][0:SEQ, 640:768].rearrange("(i p) d -> p i d", p=P)).then_inc(v_ld, 16)
            sp.wait_ge(v_st, 16)

        @block.gpsimd
        def _(pool):
            pool.memset(eps[:, :], NORM_EPS).then_inc(const, 1)
            pool.memset(causal[:, :], 0.0).then_inc(const, 1)
            pool.wait_ge(const, 2)
            pool.affine_select(out=causal[:, :], in_=causal[:, :], compare_op=ALU.is_ge, fill=OUT, base=0, pattern=[[-1, P]], channel_multiplier=1).then_inc(const, 1)
            for i in range(-1, QT + 2):
                if 0 <= i - 2:
                    pool.wait_ge(*act_s.at(f"o{i - 2}", 0))
                    pool.dma_start(t["oT"][4:8, :, (i - 2) * P:(i - 1) * P].rearrange("b p t -> p b t"), oT_sb[:, :, :]).then_inc(o_st, 16)
                if i + 1 < QT:
                    n = i + 1
                    pool.wait_ge(*vec_s.at(f"gi{n}", 0))
                    pool.dma_start(t["k_p"][n * P:(n + 1) * P, :], qkn[:, n % 2, 4, :]).then_inc(k_st[n % 2], 16)
                    pool.dma_start(t["ki_p"][n * P:(n + 1) * P, :], kin[:, n % 2, 0, :]).then_inc(k_st[n % 2], 16)
            for k in range(2):
                pool.wait_ge(k_st[k], 32 * (QT // 2))
            pool.wait_ge(o_st, 16 * QT)

        @block.tensor
        def _(pe):
            vec = lambda name: pe.wait_ge(*vec_s.at(name, 0))
            act = lambda name: pe.wait_ge(*act_s.at(name, 0))

            def mul(out, lhsT, rhs, start=True, stop=True):
                return pe.matmul(out, lhsT, rhs, start=start, stop=stop, skip_group_check=True)

            def logits(a, h):
                j, r = h % 4, slice(64 * (h // 4), 64 * (h // 4) + 64)
                for c, (at, n) in enumerate(logit_chunks(a)):
                    name = f"L{a}_{h}_{c}"
                    b, before = l_ring[name]
                    if before:
                        vec(read(before))
                    mul(pb[b][:, 0:n], qT[r, a % 3, j, :], kT[r, at:at + n]).then_inc(*pe_s.step(name))

            def attend(a, h):
                for kind, g in pv_order(a):
                    name = f"{kind}{a}_{h}_{g}"
                    if kind == "P":
                        b, before = p_ring[name]
                        if before:
                            act("e" + before[1:])
                        act(f"E{a}_{h}")
                        for x, k in enumerate(groups(a)[g]):
                            mm = pe.transpose(pb[4 + b][:, x * P:(x + 1) * P], lg[:, h, k * P:(k + 1) * P], ident)
                    else:
                        b, _ = p_ring[f"P{a}_{h}_{g}"]
                        act(f"e{a}_{h}_{g}")
                        for x, k in enumerate(groups(a)[g]):
                            mm = mul(pb[6][:, h * D:(h + 1) * D], PT[:, b, x * P:(x + 1) * P], V[:, k, 64 * (h // 4):64 * (h // 4) + 64], k == 0, k == a)
                    mm.then_inc(*pe_s.step(name))

            def turn_outputs(a):
                vec(f"on{a}")
                for b in range(4):
                    mm = pe.transpose(pb[7][:, b * P:(b + 1) * P], o_sb[:, 2 * b:2 * b + 2, :].rearrange("p h d -> p (h d)"), ident)
                mm.then_inc(*pe_s.step(f"oT{a}"))

            pe.wait_ge(v_ld, 16)
            scores = None
            for i, h, a, n in slots():
                if a is not None:
                    if a == 0 and h == 0:
                        logits(0, 0)
                    if h + 1 < NH:
                        logits(a, h + 1)
                    elif a + 1 < QT:
                        logits(a + 1, 0)
                    if h == 0 and a:
                        turn_outputs(a - 1)
                    if scores:
                        act(scores)
                    attend(a, h)
                if n is not None and h == TURN:
                    vec(f"gi{n}")
                    if a:
                        act(f"o{a - 1}")
                    if n:
                        act(f"k{n - 1}")
                    for b in range(4):
                        mm = pe.transpose(pb[7][:, b * P:(b + 1) * P], qkn[:, n % 2, b, :], ident)
                    mm.then_inc(*pe_s.step(f"Tq{n}"))
                    act(f"q{n}")
                    for b in range(2):
                        pe.transpose(pb[7][:, b * P:(b + 1) * P], z[:, n % 2, 768 + b * P:768 + (b + 1) * P], ident)
                    pe.transpose(pb[7][:, 2 * P:3 * P], qkn[:, n % 2, 4, :], ident)
                    pe.transpose(pb[7][:, 3 * P:4 * P], kin[:, n % 2, :, :].rearrange("p a d -> p (a d)"), ident).then_inc(*pe_s.step(f"Tk{n}"))
                    act(f"k{n}")
                c = scored(n, h, SCORE)
                if c is not None:
                    at, m = chunks(keys(n))[c]
                    scores = f"R{n}_{c}_3"
                    for hp in range(2):
                        if c or hp:
                            act(f"R{n}_{c if hp else c - 1}_{1 if hp else 3}")
                        elif n:
                            act(f"R{n - 1}_{len(chunks(keys(n - 1))) - 1}_3")
                        for o in range(2):
                            mm = mul(pb[4 + o][:, 0:m], qiT[64 * o:64 * o + 64, hp, :], kiT[64 * o:64 * o + 64, at:at + m])
                        mm.then_inc(*pe_s.step(f"S{n}_{c}_{hp}"))
            turn_outputs(QT - 1)

        @block.scalar
        def _(act):
            pe = lambda name: act.wait_ge(*pe_s.at(name, 0))
            vec = lambda name: act.wait_ge(*vec_s.at(name, 0))
            act.wait_ge(const, 3)
            def store_outputs(a):
                pe(f"oT{a}")
                if a:
                    act.wait_ge(o_st, 16 * a)
                act.activation(oT_sb[:, :, :].rearrange("p b t -> p (b t)"), pb[7][:, :], ACT.Copy).then_inc(*act_s.step(f"o{a}"))

            for i, h, a, n in slots():
                if a is not None:
                    vec(f"ng{a}_{h}")
                    if a >= 2:
                        vec(f"rc{a - 2}")
                    act.activation(lg[:, h, 0:keys(a)], lg[:, h, 0:keys(a)], ACT.Exp, bias=neg[:, h:h + 1], accum_out=tot[:, a % 2, h:h + 1]).then_inc(*act_s.step(f"E{a}_{h}"))
                    if h == 0 and a:
                        store_outputs(a - 1)
                    for g, tiles in enumerate(groups(a)):
                        name = f"P{a}_{h}_{g}"
                        b, before = p_ring[name]
                        pe(name)
                        if before:
                            pe("V" + before[1:])
                        act.activation(PT[:, b, 0:len(tiles) * P], pb[4 + b][:, 0:len(tiles) * P], ACT.Copy).then_inc(*act_s.step(f"e{a}_{h}_{g}"))
                if n is not None and h == 0:
                    act.wait_ge(z_ld[n % 2], 16 * (n // 2 + 1))
                    if n:
                        vec(f"ss{n - 1}")
                    act.activation(sq[:, 0:10, :].rearrange("p a d -> p (a d)"), z[:, n % 2, 0:640], ACT.Square)
                    act.activation(sq[:, 10, :], z[:, n % 2, 1024:1088], ACT.Square).then_inc(*act_s.step(f"sq{n}"))
                if n is not None and h == 1:
                    vec(f"ss{n}")
                    act.activation(ss[:, :], ss[:, :], ACT.Sqrt, scale=1.0 / D, bias=eps[:, :]).then_inc(*act_s.step(f"std{n}"))
                if n is not None and h == TURN:
                    pe(f"Tq{n}")
                    act.activation(qT[:, n % 3, :, :].rearrange("p b t -> p (b t)"), pb[7][:, :], ACT.Copy).then_inc(*act_s.step(f"q{n}"))
                    pe(f"Tk{n}")
                    act.activation(qiT[:, :, :].rearrange("p b t -> p (b t)"), pb[7][:, 0:256], ACT.Copy)
                    act.activation(kT[:, n * P:(n + 1) * P], pb[7][:, 256:384], ACT.Copy)
                    act.activation(kiT[:, n * P:(n + 1) * P], pb[7][:, 384:512], ACT.Copy).then_inc(*act_s.step(f"k{n}"))
                c = scored(n, h, SCORE)
                if c is not None:
                    m = chunks(keys(n))[c][1]
                    for x in range(4):
                        pe(f"S{n}_{c}_{x // 2}")
                        if c:
                            vec(f"A{n}_{c - 1}_{x}")
                        elif n:
                            vec(f"A{n - 1}_{len(chunks(keys(n - 1))) - 1}_{x}")
                        act.activation(rl[:, x, 0:m], pb[4 + x % 2][:, 0:m], ACT.Relu).then_inc(*act_s.step(f"R{n}_{c}_{x}"))
            store_outputs(QT - 1)

        @block.vector
        def _(dve):
            pe = lambda name: dve.wait_ge(*pe_s.at(name, 0))
            act = lambda name: dve.wait_ge(*act_s.at(name, 0))
            own = lambda name: dve.wait_ge(*vec_s.at(name, 0))
            heads = lambda x: x.unsqueeze(2).to_broadcast([P, 8, D])
            dve.wait_ge(par, 16 * 12)
            dve.wait_ge(const, 3)
            dve.tensor_scalar(gain[:, 0:8, :], gain[:, 0:8, :], D ** -0.5, None, ALU.mult).then_inc(const, 1)
            dve.wait_ge(const, 4)
            def outputs(a):
                act(f"E{a}_{NH - 1}")
                dve.reciprocal(tot[:, a % 2, :], tot[:, a % 2, :]).then_inc(*vec_s.step(f"rc{a}"))
                own(f"rc{a}")
                pe(f"V{a}_{NH - 1}_{len(groups(a)) - 1}")
                if a:
                    pe(f"oT{a - 1}")
                dve.tensor_tensor(o_sb[:, :, :], pb[6][:, :].rearrange("p (h d) -> p h d", h=NH), heads(tot[:, a % 2, :]), ALU.mult).then_inc(*vec_s.step(f"on{a}"))

            for i, h, a, n in slots():
                if a is not None:
                    ps = pieces(a)
                    far = max(0, keys(a) - 256)
                    m = keys(a) - far
                    dve.tensor_tensor(near[:, h % 2, 0:m], msk[:, far:far + m], B[:, h, 256 - m:256], ALU.add).then_inc(*vec_s.step(f"nb{a}_{h}"))
                    if a:
                        pe(f"P{a - 1}_{h}_{len(groups(a - 1)) - 1}")
                    for k, (c, at, m, close) in enumerate(ps):
                        pe(f"L{a}_{h}_{c}")
                        if close:
                            own(f"nb{a}_{h}")
                        if k:
                            own(f"x{a}_{h}_{k - 1}")
                        add = near[:, h % 2, at - far:at - far + m] if close else msk[:, at:at + m]
                        b = l_ring[f"L{a}_{h}_{c}"][0]
                        dve.tensor_tensor_reduce(lg[:, h, at:at + m], pb[b][:, at - 512 * c:at - 512 * c + m], add, 1.0, mxs[:, h, k - 1:k] if k else LEAST,
                                                 ALU.add, ALU.max, mxs[:, h, k:k + 1]).then_inc(*vec_s.step(f"x{a}_{h}_{k}"))
                    own(f"x{a}_{h}_{len(ps) - 1}")
                    dve.tensor_scalar(neg[:, h:h + 1], mxs[:, h, len(ps) - 1:len(ps)], -1.0, None, ALU.mult).then_inc(*vec_s.step(f"ng{a}_{h}"))
                    if h == 0 and a:
                        outputs(a - 1)
                if n is not None and h == 1:
                    act(f"sq{n}")
                    dve.tensor_reduce(ss[:, :], sq[:, :, :], AX.X, ALU.add).then_inc(*vec_s.step(f"ss{n}"))
                if n is not None and h == TURN:
                    zi, qn = z[:, n % 2, :], qkn[:, n % 2, :, :]
                    act(f"std{n}")
                    dve.reciprocal(ss[:, :], ss[:, :]).then_inc(*vec_s.step(f"r{n}"))
                    own(f"r{n}")
                    if n >= 2:
                        dve.wait_ge(k_st[n % 2], 32 * (n // 2))
                        pe(f"Tk{n - 2}")
                    for q in range(2):
                        op = dve.tensor_tensor(qn[:, 0:4, q * D:(q + 1) * D], zi[:, q * 256:(q + 1) * 256].rearrange("p (j d) -> p j d", j=4),
                                               ss[:, 4 * q:4 * q + 4].unsqueeze(2).to_broadcast([P, 4, D]), ALU.mult)
                    op.then_inc(*vec_s.step(f"nq{n}"))
                    dve.tensor_tensor(qn[:, 4, :].rearrange("p (n d) -> p n d", n=2), zi[:, 512:640].rearrange("p (n d) -> p n d", n=2),
                                      ss[:, 8:10].unsqueeze(2).to_broadcast([P, 2, D]), ALU.mult).then_inc(*vec_s.step(f"nk{n}"))
                    dve.tensor_scalar(kin[:, n % 2, 1, :], zi[:, 1024:1088], ss[:, 10:11], None, ALU.mult).then_inc(*vec_s.step(f"ni{n}"))
                    own(f"nk{n}")
                    dve.tensor_tensor(qn.rearrange("p b d -> p (b d)"), qn.rearrange("p b d -> p (b d)"), gain[:, 0:10, :].rearrange("p h d -> p (h d)"), ALU.mult).then_inc(*vec_s.step(f"gq{n}"))
                    own(f"ni{n}")
                    dve.tensor_tensor(kin[:, n % 2, 0, :], kin[:, n % 2, 1, :], gain[:, 10, :], ALU.mult)
                    dve.tensor_tensor(kin[:, n % 2, 1, :], kin[:, n % 2, 1, :], gain[:, 10, :], ALU.mult).then_inc(*vec_s.step(f"gi{n}"))
                    dve.tensor_scalar(wi[:, :], zi[:, 1088:1092], 0.125 * 0.5, None, ALU.mult).then_inc(*vec_s.step(f"wi{n}"))
                c = scored(n, h, WEIGH)
                if c is not None:
                    at, m = chunks(keys(n))[c]
                    own(f"wi{n}")
                    for x in range(4):
                        act(f"R{n}_{c}_{x}")
                        if x == 0:
                            op = dve.tensor_scalar(sc[:, n % 2, at:at + m], rl[:, 0, 0:m], wi[:, 0:1], None, ALU.mult)
                        else:
                            own(f"A{n}_{c}_{x - 1}")
                            op = dve.scalar_tensor_tensor(out=sc[:, n % 2, at:at + m], in0=rl[:, x, 0:m], scalar=wi[:, x:x + 1], in1=sc[:, n % 2, at:at + m], op0=ALU.mult, op1=ALU.add)
                        op.then_inc(*vec_s.step(f"A{n}_{c}_{x}"))
                if n is not None and h == NH - 1:
                    own(f"A{n}_{len(chunks(keys(n))) - 1}_3")
                    dve.tensor_tensor(sc[:, n % 2, n * P:(n + 1) * P], sc[:, n % 2, n * P:(n + 1) * P], causal[:, :], ALU.add).then_inc(*vec_s.step(f"M{n}"))
                if 2 <= i < QT:
                    row = sc[:, i % 2, 0:keys(i)]
                    for r in range(4 * h, 4 * h + 4):
                        own(f"mr{i}_{r - 1}" if r else f"M{i}")
                        dve.max(best[:, :], row).then_inc(*vec_s.step(f"mx{i}_{r}"))
                        own(f"mx{i}_{r}")
                        dve.match_replace(row, best[:, :], row, GONE).then_inc(*vec_s.step(f"mr{i}_{r}"))
                if h == NH - 1 and 0 <= i < QT:
                    row = sc[:, i % 2, 0:keys(i)]
                    if i >= 2:
                        own(f"mr{i}_{ROUNDS - 1}")
                        op = dve.tensor_scalar(msk[:, 0:keys(i)], row, -1e38, OUT, ALU.is_gt, ALU.mult)
                    else:
                        own(f"M{i}")
                        op = dve.tensor_scalar(msk[:, 0:keys(i)], row, -1e29, OUT, ALU.is_lt, ALU.mult)
                    op.then_inc(*vec_s.step(f"mk{i}"))
                    own(f"mk{i}")
            outputs(QT - 1)


def sample_constants():
    step = np.arange(TS) % DEC_SEQ
    behind = np.where(np.arange(DEC_SEQ)[None, :] > step[:, None], -1e30, 0.0)
    row, b, t_ = np.arange(TS)[:, None, None, None], np.arange(DEC_BATCH)[None, :, None, None], np.arange(DEC_SEQ)[None, None, None, :]
    spread = (row == b * DEC_SEQ + t_) * np.ones((1, 1, 8, 1))
    return dict(behind=behind.astype(np.float32), spread=spread.reshape(TS, DEC_BATCH, TS).astype(np.float32),
                quarter=(np.arange(P) % 4).astype(np.float32).reshape(P, 1))


def attention_sample(nc, ident, t):
    NH, D, L, R = 8, 64, PAST + DEC_SEQ, PAST // P
    ROUNDS = 256 // 8
    OUT, GONE, LEAST = -1e30, -3e38, -3.4e38
    with ExitStack() as outer:
        def make(ctx, prefix):
            return lambda name, shape, dt=F32: ctx.enter_context(nc.sbuf_tensor(prefix + name, shape, dt))

        keep = make(outer, "as_")
        idx = keep("idx", [P, DEC_BATCH], I32)
        Q = keep("Q", [P, DEC_BATCH, NH, DEC_SEQ])
        kTn = keep("kTn", [P, TS])
        Vn = keep("Vn", [DEC_SEQ, DEC_BATCH, P])
        msk = keep("msk", [TS, L])
        spread = keep("spread", [TS, DEC_BATCH, TS])
        with ExitStack() as ctx:
            sb = make(ctx, "ai_")
            z = sb("z", [TS, N_ATT])
            gain = sb("gain", [TS, 11, D])
            behind = sb("behind", [TS, DEC_SEQ])
            quarter = sb("quarter", [P, 1])
            pages = sb("pages", [P, DEC_BATCH], I32)
            sq = sb("sq", [TS, 11, D])
            ss = sb("ss", [TS, 11])
            qkn = sb("qkn", [TS, 5, P])
            kin = sb("kin", [TS, 2, D])
            qid = sb("qid", [TS, 4, 2, D])
            wi = sb("wi", [TS, 4])
            eps = sb("eps", [TS, 1])
            Qi = sb("Qi", [P, 4, 320])
            kiN = sb("kiN", [P, 4, DEC_SEQ])
            raw = sb("raw", [P, 2, R * D])
            kp = sb("kp", [P, 2, R, P])
            kiT = sb("kiT", [P, 4, PAST])
            rl = sb("rl", [TS, 4, 512])
            sc = sb("sc", [TS, L])
            best = sb("best", [TS, 8])
            pb = [ctx.enter_context(nc.psum_tensor(f"ai_ps{k}", [P, 512], F32)) for k in range(8)]
            sem = lambda name: ctx.enter_context(nc.semaphore("ai_" + name))
            par, const, kv_st, idx_ok = sem("parameters_loaded"), sem("constants"), sem("new_kv_stored"), sem("index_ready")
            z_ld, vn_ld = sem("z_loaded"), sem("vn_loaded")
            raw_ld = [sem(f"kidx_loaded{k}") for k in range(2)]
            chunks = [(c * 512, 512) for c in range(PAST // 512)] + [(PAST, DEC_SEQ)]
            GR = R // 4

            def steps_of(engine, names):
                s = Steps(nc, ctx, "ai_" + engine, names)
                s.ahead = 0
                return s

            pe_s = steps_of("pe", ["Tq", "Tk", "Ti"] + [f"T{p}_{g}" for p in range(4) for g in range(GR)] + [f"S{c}_{h}" for c, _ in enumerate(chunks) for h in range(4)])
            act_s = steps_of("act", ["sq", "std", "Q", "k", "Qi"] + [f"T{p}_{g}" for p in range(4) for g in range(GR)] + [f"R{c}_{h}" for c, _ in enumerate(chunks) for h in range(4)])
            vec_s = steps_of("vec", ["ss", "r", "nq", "nk", "ni", "gq", "gi", "qid", "wi"] + [f"A{c}_{h}" for c, _ in enumerate(chunks) for h in range(4)]
                             + ["M"] + [f"{k}{r}" for r in range(ROUNDS) for k in ("mx", "mr")] + ["mk"])
            pool_s = steps_of("pool", [f"kp{b}" for b in range(DEC_BATCH)])
            block = nc.Block()
            with block:
                @block.sync
                def _(sp):
                    sp.dma_start(z[:, :], t["za"][SEQ:NT, :]).then_inc(z_ld, 16)
                    loads = [(gain[:, h, :], t["q_norm"].partition_broadcast(TS)) for h in range(8)]
                    loads += [(gain[:, 8 + h, :], t["k_norm"].partition_broadcast(TS)) for h in range(2)] + [(gain[:, 10, :], t["kidx_norm"].partition_broadcast(TS))]
                    loads += [(behind[:, :], t["behind"]), (spread[:, :, :], t["spread"]), (quarter[:, :], t["quarter"])]
                    with nc.allow_non_contiguous_dma(reason="page numbers"):
                        loads += [(pages[q:P:4, :], t["page_table"].rearrange("b j -> j b")) for q in range(4)]
                        for dst, src in loads:
                            sp.dma_start(dst, src).then_inc(par, 16)
                    sp.dma_start(Vn[:, :, :], t["za"][SEQ:NT, 640:768].rearrange("(b t) d -> t b d", t=DEC_SEQ)).then_inc(vn_ld, 16)
                    sp.dma_start(t["v_s"], t["za"][SEQ:NT, 640:768]).then_inc(kv_st, 16)
                    sp.wait_ge(*vec_s.at("gi", 0))
                    sp.dma_start(t["k_s"], qkn[:, 4, :]).then_inc(kv_st, 16)
                    sp.dma_start(t["ki_s"], kin[:, 0, :]).then_inc(kv_st, 16)
                    sp.wait_ge(kv_st, 48)
                    sp.wait_ge(vn_ld, 16)

                @block.gpsimd
                def _(pool):
                    pool.memset(eps[:, :], NORM_EPS).then_inc(const, 1)
                    pool.memset(Q[:, :, :, :], 0.0).then_inc(const, 1)
                    pool.memset(Qi[:, :, :], 0.0).then_inc(const, 1)
                    pool.wait_ge(idx_ok, 1)
                    kidx_rows = t["cache_kidx"].rearrange("n (q r) d -> (n q) (r d)", q=4)

                    def gather(b):
                        pool.indirect_dma_start(raw[:, b % 2, :], None, kidx_rows, bass.IndirectOffsetOnAxis(ap=idx[:, b:b + 1], axis=0)).then_inc(raw_ld[b % 2], 16)

                    gather(0)
                    for b in range(DEC_BATCH):
                        if b + 1 < DEC_BATCH:
                            if b:
                                pool.wait_ge(*pool_s.at(f"kp{b - 1}", 0))
                            gather(b + 1)
                        pool.wait_ge(raw_ld[b % 2], 16 * (b // 2 + 1))
                        if b >= 4:
                            pool.wait_ge(*pe_s.at(f"T{b // 2 - 2}_{GR - 1}", 0))
                        pool.tensor_copy(kp[:, (b // 2) % 2, :, (b % 2) * D:(b % 2 + 1) * D], raw[:, b % 2, :].rearrange("p (r d) -> p r d", d=D)).then_inc(*pool_s.step(f"kp{b}"))

                @block.tensor
                def _(pe):
                    vec = lambda name: pe.wait_ge(*vec_s.at(name, 0))
                    act = lambda name: pe.wait_ge(*act_s.at(name, 0))
                    i64 = ident[0:TS, 0:TS]
                    vec("gi")
                    for j in range(4):
                        mm = pe.transpose(pb[0][:, j * TS:(j + 1) * TS], qkn[:, j, :], i64)
                    mm.then_inc(*pe_s.step("Tq"))
                    pe.transpose(pb[1][:, 0:TS], qkn[:, 4, :], i64)
                    pe.transpose(pb[1][:, TS:2 * TS], kin[:, :, :].rearrange("p a d -> p (a d)"), i64).then_inc(*pe_s.step("Tk"))
                    vec("qid")
                    for h in range(4):
                        mm = pe.transpose(pb[2][:, h * TS:(h + 1) * TS], qid[:, h, :, :].rearrange("p a d -> p (a d)"), i64)
                    mm.then_inc(*pe_s.step("Ti"))
                    n = 0
                    for p in range(4):
                        pe.wait_ge(*pool_s.at(f"kp{2 * p + 1}", 0))
                        for g in range(GR):
                            if n >= 2:
                                q = n - 2
                                act(f"T{q // GR}_{q % GR}")
                            for x in range(4):
                                mm = pe.transpose(pb[3 + n % 2][:, x * P:(x + 1) * P], kp[:, p % 2, 4 * g + x, :], ident)
                            mm.then_inc(*pe_s.step(f"T{p}_{g}"))
                            n += 1
                    act(f"T3_{GR - 1}")
                    for c, (at, m) in enumerate(chunks):
                        for h in range(4):
                            if c:
                                act(f"R{c - 1}_{h}")
                            else:
                                act("Qi")
                            bank = [5, 6, 7, 0][h]
                            for p in range(4):
                                rhs = kiN[:, p, :] if at == PAST else kiT[:, p, at:at + m]
                                mm = pe.matmul(pb[bank][0:TS, 0:m], Qi[:, h, p * TS:(p + 1) * TS], rhs, start=p == 0, stop=p == 3)
                            mm.then_inc(*pe_s.step(f"S{c}_{h}"))

                @block.scalar
                def _(act):
                    pe = lambda name: act.wait_ge(*pe_s.at(name, 0))
                    vec = lambda name: act.wait_ge(*vec_s.at(name, 0))
                    act.wait_ge(const, 3)
                    act.wait_ge(z_ld, 16)
                    act.activation(sq[:, 0:10, :].rearrange("p a d -> p (a d)"), z[:, 0:640], ACT.Square)
                    act.activation(sq[:, 10, :], z[:, 1024:1088], ACT.Square).then_inc(*act_s.step("sq"))
                    vec("ss")
                    act.activation(ss[:, :], ss[:, :], ACT.Sqrt, scale=1.0 / D, bias=eps[:, :]).then_inc(*act_s.step("std"))
                    pe("Tq")
                    for n in range(2):
                        r = slice(64 * n, 64 * n + 64)
                        for j in range(4):
                            op = act.activation(Q[r, :, 4 * n + j, :], pb[0][r, j * TS:(j + 1) * TS].rearrange("p (b s) -> p b s", s=DEC_SEQ), ACT.Copy)
                    op.then_inc(*act_s.step("Q"))
                    pe("Tk")
                    act.activation(kTn[:, :], pb[1][:, 0:TS], ACT.Copy)
                    for n in range(2):
                        r = slice(64 * n, 64 * n + 64)
                        op = act.activation(kiN[r, :, :], pb[1][r, TS:2 * TS].rearrange("p (c two s) -> p c two s", two=2, s=DEC_SEQ)[:, :, n, :], ACT.Copy)
                    op.then_inc(*act_s.step("k"))
                    pe("Ti")
                    for n in range(2):
                        r = slice(64 * n, 64 * n + 64)
                        for h in range(4):
                            op = act.activation(Qi[r, h, :].rearrange("p (c x) -> p c x", x=80)[:, :, n * DEC_SEQ:(n + 1) * DEC_SEQ],
                                                pb[2][r, h * TS:(h + 1) * TS].rearrange("p (c two s) -> p c two s", two=2, s=DEC_SEQ)[:, :, n, :], ACT.Copy)
                    op.then_inc(*act_s.step("Qi"))
                    n = 0
                    for p in range(4):
                        for g in range(GR):
                            pe(f"T{p}_{g}")
                            act.activation(kiT[:, p, :].rearrange("k (q r) -> k r q", r=R)[:, 4 * g:4 * g + 4, :], pb[3 + n % 2][:, :].rearrange("k (r q) -> k r q", r=4), ACT.Copy).then_inc(*act_s.step(f"T{p}_{g}"))
                            n += 1
                    for c, (at, m) in enumerate(chunks):
                        for h in range(4):
                            pe(f"S{c}_{h}")
                            if c:
                                vec(f"A{c - 1}_{h}")
                            act.activation(rl[:, h, 0:m], pb[[5, 6, 7, 0][h]][0:TS, 0:m], ACT.Relu).then_inc(*act_s.step(f"R{c}_{h}"))

                @block.vector
                def _(dve):
                    act = lambda name: dve.wait_ge(*act_s.at(name, 0))
                    own = lambda name: dve.wait_ge(*vec_s.at(name, 0))
                    dve.wait_ge(par, 16 * 18)
                    dve.tensor_scalar(idx[:, :], pages[:, :], 4.0, quarter[:, 0:1], ALU.mult, ALU.add).then_inc(idx_ok, 1)
                    dve.wait_ge(const, 3)
                    dve.tensor_scalar(gain[:, 0:8, :], gain[:, 0:8, :], D ** -0.5, None, ALU.mult).then_inc(const, 1)
                    act("sq")
                    dve.tensor_reduce(ss[:, :], sq[:, :, :], AX.X, ALU.add).then_inc(*vec_s.step("ss"))
                    act("std")
                    dve.reciprocal(ss[:, :], ss[:, :]).then_inc(*vec_s.step("r"))
                    own("r")
                    for n in range(2):
                        op = dve.tensor_tensor(qkn[:, 0:4, n * D:(n + 1) * D], z[:, n * 256:(n + 1) * 256].rearrange("p (j d) -> p j d", j=4),
                                               ss[:, 4 * n:4 * n + 4].unsqueeze(2).to_broadcast([TS, 4, D]), ALU.mult)
                    op.then_inc(*vec_s.step("nq"))
                    dve.tensor_tensor(qkn[:, 4, :].rearrange("p (n d) -> p n d", n=2), z[:, 512:640].rearrange("p (n d) -> p n d", n=2),
                                      ss[:, 8:10].unsqueeze(2).to_broadcast([TS, 2, D]), ALU.mult).then_inc(*vec_s.step("nk"))
                    dve.tensor_scalar(kin[:, 1, :], z[:, 1024:1088], ss[:, 10:11], None, ALU.mult).then_inc(*vec_s.step("ni"))
                    own("nk")
                    dve.wait_ge(const, 4)
                    flat = qkn[:, :, :].rearrange("p b d -> p (b d)")
                    dve.tensor_tensor(flat, flat, gain[:, 0:10, :].rearrange("p h d -> p (h d)"), ALU.mult).then_inc(*vec_s.step("gq"))
                    own("ni")
                    dve.tensor_tensor(kin[:, 0, :], kin[:, 1, :], gain[:, 10, :], ALU.mult)
                    dve.tensor_tensor(kin[:, 1, :], kin[:, 1, :], gain[:, 10, :], ALU.mult).then_inc(*vec_s.step("gi"))
                    for n in range(2):
                        op = dve.tensor_copy(qid[:, :, n, :], z[:, 768:1024].rearrange("p (h d) -> p h d", h=4))
                    op.then_inc(*vec_s.step("qid"))
                    dve.tensor_scalar(wi[:, :], z[:, 1088:1092], 0.125 * 0.5, None, ALU.mult).then_inc(*vec_s.step("wi"))
                    own("wi")
                    for c, (at, m) in enumerate(chunks):
                        for h in range(4):
                            act(f"R{c}_{h}")
                            if h == 0:
                                op = dve.tensor_scalar(sc[:, at:at + m], rl[:, 0, 0:m], wi[:, 0:1], None, ALU.mult)
                            else:
                                own(f"A{c}_{h - 1}")
                                op = dve.scalar_tensor_tensor(out=sc[:, at:at + m], in0=rl[:, h, 0:m], scalar=wi[:, h:h + 1], in1=sc[:, at:at + m], op0=ALU.mult, op1=ALU.add)
                            op.then_inc(*vec_s.step(f"A{c}_{h}"))
                    own(f"A{len(chunks) - 1}_3")
                    dve.tensor_tensor(sc[:, PAST:L], sc[:, PAST:L], behind[:, :], ALU.add).then_inc(*vec_s.step("M"))
                    own("M")
                    for r in range(ROUNDS):
                        if r:
                            own(f"mr{r - 1}")
                        dve.max(best[:, :], sc[:, :]).then_inc(*vec_s.step(f"mx{r}"))
                        own(f"mx{r}")
                        dve.match_replace(sc[:, :], best[:, :], sc[:, :], GONE).then_inc(*vec_s.step(f"mr{r}"))
                    own(f"mr{ROUNDS - 1}")
                    dve.tensor_scalar(msk[:, :], sc[:, :], -1e38, OUT, ALU.is_gt, ALU.mult).then_inc(*vec_s.step("mk"))

        with ExitStack() as ctx:
            sb = make(ctx, "aa_")
            FAR = PAST - P
            B = sb("B", [TS, P + DEC_SEQ])
            kraw = sb("kraw", [P, R * P])
            v = sb("v", [P, 2, R * P])
            kT = sb("kT", [P, PAST])
            lg = sb("lg", [TS, L])
            PT = sb("PT", [P, 2, 8, TS])
            mxs = sb("mxs", [TS, 9])
            neg = sb("neg", [TS, 1])
            tot = sb("tot", [TS, 1])
            o_sb = sb("o", [TS, 2, D])
            o_all = sb("o_all", [TS, 512])
            oT_sb = sb("oT", [P, 4, TS])
            pb = [ctx.enter_context(nc.psum_tensor(f"aa_ps{k}", [P, 512], F32)) for k in range(8)]
            sem = lambda name: ctx.enter_context(nc.semaphore("aa_" + name))
            b_ld, all_ld, oT_st = sem("bias_loaded"), sem("outputs_loaded"), sem("oT_stored")
            k_ld, v_ld = sem("k_loaded"), [sem(f"v_loaded{k}") for k in range(2)]
            o_st = [sem(f"o_stored{k}") for k in range(2)]
            GR = R // 4
            chunks = [(c * 512, min(512, FAR - c * 512)) for c in range(-(-FAR // 512))] + [(FAR, P + DEC_SEQ)]
            NC_ = len(chunks)
            PG = [list(range(8 * g, 8 * g + 8)) for g in range(R // 8)] + [[R]]

            def steps_of(engine, names):
                s = Steps(nc, ctx, "aa_" + engine, names)
                s.ahead = 0
                return s

            n_pg = len(PG)
            pv = [("P", 0)] + [x for g in range(n_pg) for x in ([("P", g + 1)] if g + 1 < n_pg else []) + [("V", g)]]
            turns = lambda b, first, by: [f"T{b}_{g}" for g in range(first, GR, by)] if b < DEC_BATCH else []
            pe_s = steps_of("pe", turns(0, 0, 1) + [x for b in range(DEC_BATCH) for x in [f"L{b}_{c}" for c in range(NC_)] + turns(b + 1, 0, 1) + [f"{k}{b}_{g}" for k, g in pv]] + ["oT"])
            act_s = steps_of("act", turns(0, 0, 2) + [x for b in range(DEC_BATCH) for x in [f"E{b}"] + turns(b + 1, 0, 2) + [f"e{b}_{g}" for g in range(n_pg)]] + ["oT"])
            vec_s = steps_of("vec", turns(0, 1, 2) + [x for b in range(DEC_BATCH) for x in [f"L{b}_{c}" for c in range(NC_)] + [f"ng{b}"] + turns(b + 1, 1, 2) + [f"rc{b}", f"o{b}"]])
            block = nc.Block()
            with block:
                @block.sync
                def _(sp):
                    for h in range(NH):
                        sp.dma_start(B[h * DEC_SEQ:(h + 1) * DEC_SEQ, :], bass.AP(t["bias"].tensor, h * P * BIAS_W + P - 1, [[BIAS_W - 1, DEC_SEQ], [1, P + DEC_SEQ]])).then_inc(b_ld, 16)
                    for b in range(DEC_BATCH):
                        sp.wait_ge(*vec_s.at(f"o{b}", 0))
                        for h in range(NH):
                            sp.dma_start(t["oas"][b * DEC_SEQ:(b + 1) * DEC_SEQ, h * D:(h + 1) * D], o_sb[h * DEC_SEQ:(h + 1) * DEC_SEQ, b % 2, :]).then_inc(o_st[b % 2], 16)
                    for k in range(2):
                        sp.wait_ge(o_st[k], 16 * NH * DEC_BATCH // 2)
                    sp.dma_start(o_all[:, :], t["oas"]).then_inc(all_ld, 16)
                    sp.wait_ge(*act_s.at("oT", 0))
                    sp.dma_start(t["oT"][4:8, :, SEQ:NT].rearrange("b p t -> p b t"), oT_sb[:, :, :]).then_inc(oT_st, 16)
                    sp.wait_ge(oT_st, 16)

                @block.gpsimd
                def _(pool):
                    rows = lambda name: t[name].rearrange("n (q r) d -> (n q) (r d)", q=4)
                    for b in range(DEC_BATCH):
                        at = bass.IndirectOffsetOnAxis(ap=idx[:, b:b + 1], axis=0)
                        if b >= 2:
                            pool.wait_ge(*pe_s.at(f"V{b - 2}_{n_pg - 1}", 0))
                        pool.indirect_dma_start(v[:, b % 2, :], None, rows("cache_v"), at).then_inc(v_ld[b % 2], 16)
                        if b:
                            pool.wait_ge(*pe_s.at(f"T{b - 1}_{GR - 1}", 0))
                        pool.indirect_dma_start(kraw[:, :], None, rows("cache_k"), at).then_inc(k_ld, 16)

                @block.tensor
                def _(pe):
                    vec = lambda name: pe.wait_ge(*vec_s.at(name, 0))
                    act = lambda name: pe.wait_ge(*act_s.at(name, 0))
                    turned = lambda b, g: (vec if g % 2 else act)(f"T{b}_{g}")

                    def turn_keys(b):
                        pe.wait_ge(k_ld, 16 * (b + 1))
                        for g in range(GR):
                            if g >= 2:
                                turned(b, g - 2)
                            elif b:
                                turned(b - 1, GR - 2 + g)
                            for x in range(4):
                                r = 4 * g + x
                                mm = pe.transpose(pb[g % 2][:, x * P:(x + 1) * P], kraw[:, r * P:(r + 1) * P], ident)
                            mm.then_inc(*pe_s.step(f"T{b}_{g}"))

                    turn_keys(0)
                    for b in range(DEC_BATCH):
                        turned(b, GR - 2)
                        turned(b, GR - 1)
                        for c, (at, m) in enumerate(chunks):
                            if c >= 2:
                                vec(f"L{b}_{c - 2}")
                            elif b:
                                vec(f"L{b - 1}_{NC_ - 2 + c if NC_ % 2 == 0 else NC_ - 1 - c}")
                            out = pb[2 + c % 2]
                            parts = [(0, m, kT[:, at:at + m])] if c < NC_ - 1 else [(0, P, kT[:, FAR:PAST]), (P, DEC_SEQ, kTn[:, b * DEC_SEQ:(b + 1) * DEC_SEQ])]
                            for lo, n, keys in parts:
                                pe.matmul(out[0:TS, lo:lo + n], Q[:, b, :, :].rearrange("p h s -> p (h s)"), keys, start=True, stop=False, skip_group_check=True)
                                mm = pe.matmul(out[0:TS, lo:lo + n], spread[:, b, :], msk[:, at + lo:at + lo + n], start=False, stop=True, skip_group_check=True)
                            mm.then_inc(*pe_s.step(f"L{b}_{c}"))
                        if b + 1 < DEC_BATCH:
                            turn_keys(b + 1)
                        pe.wait_ge(v_ld[b % 2], 16 * (b // 2 + 1))
                        if b:
                            vec(f"o{b - 1}")
                        for kind, g in pv:
                            bank = (b * n_pg + g) % 2
                            if kind == "P":
                                act(f"E{b}")
                                if g >= 2:
                                    act(f"e{b}_{g - 2}")
                                elif b:
                                    act(f"e{b - 1}_{n_pg - 1}")
                                for x, r in enumerate(PG[g]):
                                    if r < R:
                                        mm = pe.transpose(pb[4 + bank][:, x * TS:(x + 1) * TS], lg[:, r:PAST:R], ident[0:TS, 0:TS])
                                    else:
                                        mm = pe.transpose(pb[4 + bank][0:DEC_SEQ, 0:TS], lg[:, PAST:L], ident[0:TS, 0:TS])
                            else:
                                act(f"e{b}_{g}")
                                for x, r in enumerate(PG[g]):
                                    if r < R:
                                        mm = pe.matmul(pb[6][0:TS, 0:P], PT[:, bank, x, :], v[:, b % 2, r * P:(r + 1) * P], start=r == 0, stop=False)
                                    else:
                                        mm = pe.matmul(pb[6][0:TS, 0:P], PT[0:DEC_SEQ, bank, 0, :], Vn[:, b, :], start=False, stop=True)
                            mm.then_inc(*pe_s.step(f"{kind}{b}_{g}"))
                    pe.wait_ge(all_ld, 16)
                    for j in range(4):
                        mm = pe.transpose(pb[7][:, j * TS:(j + 1) * TS], o_all[:, j * P:(j + 1) * P], ident[0:TS, 0:TS])
                    mm.then_inc(*pe_s.step("oT"))

                def turn(engine, copy, b, g):
                    engine.wait_ge(*pe_s.at(f"T{b}_{g}", 0))
                    if b:
                        engine.wait_ge(*pe_s.at(f"L{b - 1}_{NC_ - 1}", 0))
                    return copy(kT[:, :].rearrange("k (q r) -> k r q", r=R)[:, 4 * g:4 * g + 4, :], pb[g % 2][:, :].rearrange("k (r q) -> k r q", r=4))

                @block.scalar
                def _(act):
                    pe = lambda name: act.wait_ge(*pe_s.at(name, 0))

                    def turn_half(b):
                        for g in range(0, GR, 2):
                            turn(act, lambda o, i: act.activation(o, i, ACT.Copy), b, g).then_inc(*act_s.step(f"T{b}_{g}"))

                    turn_half(0)
                    for b in range(DEC_BATCH):
                        act.wait_ge(*vec_s.at(f"ng{b}", 0))
                        act.activation(lg[:, :], lg[:, :], ACT.Exp, bias=neg[:, :], accum_out=tot[:, :]).then_inc(*act_s.step(f"E{b}"))
                        if b + 1 < DEC_BATCH:
                            turn_half(b + 1)
                        for g, slots in enumerate(PG):
                            bank = (b * n_pg + g) % 2
                            pe(f"P{b}_{g}")
                            if b and g < 2:
                                pe(f"V{b - 1}_{n_pg - 1}")
                            elif g >= 2:
                                pe(f"V{b}_{g - 2}")
                            n = P if slots[0] < R else DEC_SEQ
                            act.activation(PT[0:n, bank, 0:len(slots), :].rearrange("p x r -> p (x r)"), pb[4 + bank][0:n, 0:len(slots) * TS], ACT.Copy).then_inc(*act_s.step(f"e{b}_{g}"))
                    pe("oT")
                    act.activation(oT_sb[:, :, :].rearrange("p b r -> p (b r)"), pb[7][:, 0:4 * TS], ACT.Copy).then_inc(*act_s.step("oT"))

                @block.vector
                def _(dve):
                    pe = lambda name: dve.wait_ge(*pe_s.at(name, 0))
                    own = lambda name: dve.wait_ge(*vec_s.at(name, 0))
                    dve.wait_ge(b_ld, 16 * NH)

                    def turn_half(b):
                        for g in range(1, GR, 2):
                            turn(dve, dve.tensor_copy, b, g).then_inc(*vec_s.step(f"T{b}_{g}"))

                    turn_half(0)
                    for b in range(DEC_BATCH):
                        if b:
                            pe(f"P{b - 1}_{n_pg - 1}")
                        for c, (at, m) in enumerate(chunks):
                            pe(f"L{b}_{c}")
                            if c:
                                own(f"L{b}_{c - 1}")
                            src, out = pb[2 + c % 2][0:TS, 0:m], lg[:, at:at + m]
                            least = mxs[:, c - 1:c] if c else LEAST
                            if c < NC_ - 1:
                                op = dve.tensor_scalar(out, src, 0.0, least, ALU.add, ALU.max, accum_out=mxs[:, c:c + 1])
                            else:
                                op = dve.tensor_tensor_reduce(out, src, B[:, :], 1.0, least, ALU.add, ALU.max, mxs[:, c:c + 1])
                            op.then_inc(*vec_s.step(f"L{b}_{c}"))
                        own(f"L{b}_{NC_ - 1}")
                        if b:
                            dve.wait_ge(*act_s.at(f"E{b - 1}", 0))
                        dve.tensor_scalar(neg[:, :], mxs[:, NC_ - 1:NC_], -1.0, None, ALU.mult).then_inc(*vec_s.step(f"ng{b}"))
                        if b + 1 < DEC_BATCH:
                            turn_half(b + 1)
                        dve.wait_ge(*act_s.at(f"E{b}", 0))
                        dve.reciprocal(tot[:, :], tot[:, :]).then_inc(*vec_s.step(f"rc{b}"))
                        own(f"rc{b}")
                        pe(f"V{b}_{n_pg - 1}")
                        if b >= 2:
                            dve.wait_ge(o_st[b % 2], 16 * NH * (b // 2))
                        for n in range(2):
                            r = slice(32 * n, 32 * n + 32)
                            op = dve.tensor_scalar(o_sb[r, b % 2, :], pb[6][r, n * D:(n + 1) * D], tot[r, :], None, ALU.mult)
                        op.then_inc(*vec_s.step(f"o{b}"))


_SCRATCH = dict(zT=(CMB, P, NT + 1), za=(NT, N_ATT), oT=(KD, P, NT), x1=(NT, D_MODEL), h2T=(KD, P, NT), aT=(FB, P, NT), oas=(TS, 512), bias=(8, P, BIAS_W))
_OUTS = dict(
    y_p=(SEQ, 1024), y_s=(TS, 1024), k_p=(SEQ, 128), v_p=(SEQ, 128), ki_p=(SEQ, 64), wkv_p=(4, 64, 64), shift_p=(1, 896),
    conv_p=(30, 256), ffn_p=(2, D_FF), k_s=(TS, 128), v_s=(TS, 128), ki_s=(TS, 64), wkv_s=(8, 4, 64, 64), shift_s=(8, 896),
    conv_s=(8, 30, 256), ffn_s=(8, 2, D_FF))
_PHASES = ("in", "rw", "ap", "as", "out", "up", "down")


def build(nc, t, phases):
    with ExitStack() as ctx:
        ident_t = ctx.enter_context(nc.sbuf_tensor("ident", [P, P], F32))
        made = ctx.enter_context(nc.semaphore("ident_made"))
        ident = ident_t[:, :]
        make_identity(nc, ident, made)
        if "in" in phases:
            with nc.cleanup_on_exit():
                project_in(nc, ident, t["x_prompt"], t["x_sample"], t["norm_mix"], t["w_in"], t["zT"], t["za"])
        if "rw" in phases:
            with ExitStack() as conv_ctx:
                cv = conv_buffers(nc, conv_ctx)
                rwkv(nc, ident, t, cv)
                conv_finish(nc, t, cv)
        if "ap" in phases or "as" in phases:
            bias_table(nc, t)
        if "ap" in phases:
            attention_prompt(nc, ident, t)
        if "as" in phases:
            attention_sample(nc, ident, t)
        if "out" in phases:
            mix_out(nc, ident, t["w_out"], t["oT"], t["x_prompt"], t["x_sample"], t["norm_ffn"], t["x1"], t["h2T"])
        if "up" in phases:
            ffn_up(nc, t["h2T"], t["ffn_up"], t["ffn_conv_w"], t["ffn_conv_b"], t["state_ffn"], t["aT"], t["ffn_p"], t["ffn_s"])
        if "down" in phases:
            ffn_down(nc, ident, t["aT"], t["x1"], t["ffn_down"], t["ple_norm"], t["ple_gate"], t["ple_proj"], t["p_prompt"],
                     t["p_sample"], t["y_p"], t["y_s"])


def declare_and_build(nc, inputs, phases=_PHASES, given=None):
    given = given or {}
    views = dict(x_prompt=(SEQ, D_MODEL), x_sample=(TS, D_MODEL), p_prompt=(SEQ, D_PLE), p_sample=(TS, D_PLE))
    arrays, t = {}, {}
    for name, a in inputs.items():
        a = np.ascontiguousarray(a)
        if name in views:
            a = a.reshape(views[name])
        elif name in ("cache_k", "cache_v"):
            a = a.reshape(a.shape[1], PAGE, P)
        elif name not in ("rel_bias", "page_table"):
            a = a.reshape(a.shape[1:])
        arrays["in_" + name] = a
        t[name] = nc.dram_tensor("in_" + name, a.shape, mybir.dt.from_np(a.dtype), kind="ExternalInput").ap()
    for name, a in dict(bias_rows=bias_rows(), **sample_constants()).items():
        arrays[name] = a
        t[name] = nc.dram_tensor(name, a.shape, F32, kind="ExternalInput").ap()
    for name, shape in _OUTS.items():
        t[name] = nc.dram_tensor("out_" + name, shape, F32, kind="ExternalOutput").ap()
    for name, shape in _SCRATCH.items():
        kind = "ExternalInput" if name in given else "Internal"
        if name in given:
            arrays[name] = given[name]
        t[name] = nc.dram_tensor(name, shape, F32, kind=kind).ap()
    build(nc, t, phases)
    return arrays


def kernel(**inputs):
    import concourse.bacc as bacc
    from concourse.bass_utils import run_bass_kernel_spmd as run

    nc = bacc.Bacc("TRN2", target_bir_lowering=False, num_devices=1)
    arrays = declare_and_build(nc, inputs)
    got = run(nc, [arrays], core_ids=[0]).results[0]
    shapes = [(1, SEQ, 1024), (8, 8, 1024), (1, 1, SEQ, 2, 64), (1, 1, SEQ, 2, 64), (1, 1, SEQ, 64), (1, 1, 4, 64, 64), (1, 1, 896),
              (1, 1, 30, 256), (1, 1, 2, D_FF), (1, 8, 8, 2, 64), (1, 8, 8, 2, 64), (1, 8, 8, 64), (1, 8, 4, 64, 64), (1, 8, 896),
              (1, 8, 30, 256), (1, 8, 2, D_FF)]
    return tuple(np.asarray(got["out_" + n]).reshape(s) for n, s in zip(_OUTS, shapes))
```
